# Optimizing a Trainium2 kernel written in Bass

```python
import math
import jax, jax.numpy as jnp
from jax import lax
import numpy as np

D_MODEL = 1024
BATCH = 1
SEQ = 512
DEPTH = 2

BLOCK = 128
RET_HEADS = 4
RET_DIM = 128
SB_HEADS = 8
SB_DIM = 64
DIFF_HEADS = 8
DIFF_DIM = 64
REL_BUCKETS = 32
REL_MAX_DIST = 128
D_FF = 2816
CONV_W = 3
ALPHA = (2 * DEPTH) ** 0.25
BETA = (8 * DEPTH) ** -0.25
LN_EPS = 1e-5
ROPE_BASE = 10000.0

RET_W = RET_HEADS * RET_DIM
SB_W = SB_HEADS * SB_DIM
EVEN_IN = 4 * RET_W + 3 * SB_W
EVEN_SPLITS = [RET_W, 2 * RET_W, 3 * RET_W, 4 * RET_W, 4 * RET_W + SB_W, 4 * RET_W + 2 * SB_W]
DIFF_W = DIFF_HEADS * 2 * DIFF_DIM
ODD_IN = 3 * DIFF_W
N_EVEN = (DEPTH + 1) // 2
N_ODD = DEPTH // 2


def layer_norm(x, g, b):
    xf = x.astype(jnp.float32)
    mu = xf.mean(-1, keepdims=True)
    var = jnp.square(xf - mu).mean(-1, keepdims=True)
    return ((xf - mu) * lax.rsqrt(var + LN_EPS) * g.astype(jnp.float32) + b.astype(jnp.float32)).astype(x.dtype)

def rotary(x):
    S, dh = x.shape[1], x.shape[-1]
    inv = ROPE_BASE ** (-jnp.arange(0, dh, 2, dtype=jnp.float32) / dh)
    ang = jnp.arange(S, dtype=jnp.float32)[:, None] * inv[None, :]
    cos = jnp.cos(ang)[None, :, None, :]
    sin = jnp.sin(ang)[None, :, None, :]
    xf = x.astype(jnp.float32)
    x1, x2 = xf[..., : dh // 2], xf[..., dh // 2:]
    return jnp.concatenate([x1 * cos - x2 * sin, x1 * sin + x2 * cos], -1).astype(x.dtype)

def retention(q, k, v):
    bsz, S, H, dh = q.shape
    n = S // BLOCK
    log_g = jnp.log(1.0 - 2.0 ** (-5.0 - jnp.arange(H, dtype=jnp.float32)))
    idx = jnp.arange(BLOCK, dtype=jnp.float32)
    rel = idx[:, None] - idx[None, :]
    decay = jnp.where(rel >= 0, jnp.exp(log_g[:, None, None] * jnp.maximum(rel, 0.0)), 0.0)
    q_dec = jnp.exp(log_g[:, None] * (idx[None, :] + 1.0))
    k_dec = jnp.exp(log_g[:, None] * (BLOCK - 1.0 - idx[None, :]))
    chunk_g = jnp.exp(log_g * BLOCK)

    def chunks(t):
        return t.astype(jnp.float32).reshape(bsz, n, BLOCK, H, dh).transpose(1, 0, 3, 2, 4)

    qc, kc, vc = chunks(q), chunks(k) * (dh ** -0.5), chunks(v)

    def step(state, inp):
        qi, ki, vi = inp
        s = jnp.einsum('bhid,bhjd->bhij', qi, ki) * decay[None]
        intra = jnp.einsum('bhij,bhjd->bhid', s, vi)
        cross = jnp.einsum('bhid,bhde->bhie', qi, state) * q_dec[None, :, :, None]
        new_state = state * chunk_g[None, :, None, None] + jnp.einsum(
            'bhjd,bhje->bhde', ki * k_dec[None, :, :, None], vi)
        return new_state, intra + cross

    state0 = jnp.zeros((bsz, H, dh, dh), jnp.float32)
    _, out = lax.scan(step, state0, (qc, kc, vc))
    return out.transpose(1, 0, 3, 2, 4).reshape(bsz, S, H, dh)

def stick_breaking(q, k, v):
    bsz, S, H, dh = q.shape
    n = S // BLOCK
    qb = q.reshape(bsz, n, BLOCK, H, dh).transpose(1, 0, 3, 2, 4)
    kh = k.transpose(0, 2, 1, 3)
    vh = v.transpose(0, 2, 1, 3)
    kpos = jnp.arange(S)
    scale = dh ** -0.5

    def block(args):
        qi, start = args
        qpos = start + jnp.arange(BLOCK)
        z = jnp.einsum('bhid,bhsd->bhis', qi, kh).astype(jnp.float32) * scale
        past = (kpos[None, :] < qpos[:, None])[None, None]
        log_keep = jnp.where(past, jax.nn.log_sigmoid(-z), 0.0)
        between = lax.cumsum(log_keep, axis=3, reverse=True) - log_keep
        a = jnp.where(past, jnp.exp(jax.nn.log_sigmoid(z) + between), 0.0)
        return jnp.einsum('bhis,bhsd->bhid', a.astype(vh.dtype), vh)

    out = lax.map(block, (qb, jnp.arange(n) * BLOCK))
    return out.transpose(1, 0, 3, 2, 4).reshape(bsz, S, H * dh)

def t5_bucket(rel):
    n = jnp.maximum(rel, 0)
    max_exact = REL_BUCKETS // 2
    nf = jnp.maximum(n, 1).astype(jnp.float32)
    large = max_exact + (jnp.log(nf / max_exact) / math.log(REL_MAX_DIST / max_exact)
                         * (REL_BUCKETS - max_exact)).astype(jnp.int32)
    large = jnp.minimum(large, REL_BUCKETS - 1)
    return jnp.where(n < max_exact, n, large)

def diff_attention(q, k, v, lam, rel_bias):
    _, bsz, H, S, dh = q.shape
    n = S // BLOCK
    qb = q.reshape(2, bsz, H, n, BLOCK, dh).transpose(3, 0, 1, 2, 4, 5)
    kpos = jnp.arange(S)
    scale = dh ** -0.5
    table = rel_bias.astype(jnp.float32)

    def block(args):
        qi, start = args
        qpos = start + jnp.arange(BLOCK)
        rel = qpos[:, None] - kpos[None, :]
        bias = table[t5_bucket(rel)].transpose(2, 0, 1)
        s = jnp.einsum('pbhid,pbhsd->pbhis', qi, k).astype(jnp.float32) * scale + bias[None, None]
        s = jnp.where((rel >= 0)[None, None, None], s, -jnp.inf)
        p = jax.nn.softmax(s, axis=-1)
        w = p[0] - lam * p[1]
        return jnp.einsum('bhis,bhse->bhie', w.astype(v.dtype), v).astype(jnp.float32)

    out = lax.map(block, (qb, jnp.arange(n) * BLOCK))
    return out.transpose(1, 2, 0, 3, 4).reshape(bsz, H, S, 2 * dh)

def even_mixer(x, w_in, w_out):
    bsz, S, _ = x.shape
    h = x @ w_in
    rq, rk, rv, rg, sq, sk, sv = jnp.split(h, EVEN_SPLITS, axis=-1)
    hd = lambda t, nh, dh: t.reshape(bsz, S, nh, dh)
    ret = retention(rotary(hd(rq, RET_HEADS, RET_DIM)), rotary(hd(rk, RET_HEADS, RET_DIM)),
                    hd(rv, RET_HEADS, RET_DIM))
    mu = ret.mean(-1, keepdims=True)
    var = jnp.square(ret - mu).mean(-1, keepdims=True)
    ret = ((ret - mu) * lax.rsqrt(var + LN_EPS)).reshape(bsz, S, RET_W)
    ret = jax.nn.silu(rg.astype(jnp.float32)) * ret
    sb = stick_breaking(hd(sq, SB_HEADS, SB_DIM), hd(sk, SB_HEADS, SB_DIM), hd(sv, SB_HEADS, SB_DIM))
    y = jnp.concatenate([ret.astype(x.dtype), sb.astype(x.dtype)], axis=-1)
    return y @ w_out

def odd_mixer(x, w_in, w_out, lq1, lk1, lq2, lk2, sub_g, rel_bias, layer):
    bsz, S, _ = x.shape
    h = x @ w_in
    q, k, v = jnp.split(h, 3, axis=-1)
    q = q.reshape(bsz, S, DIFF_HEADS, 2, DIFF_DIM).transpose(3, 0, 2, 1, 4)
    k = k.reshape(bsz, S, DIFF_HEADS, 2, DIFF_DIM).transpose(3, 0, 2, 1, 4)
    v = v.reshape(bsz, S, DIFF_HEADS, 2 * DIFF_DIM).transpose(0, 2, 1, 3)
    lam_init = 0.8 - 0.6 * math.exp(-0.3 * layer)
    lam = (jnp.exp(jnp.sum(lq1.astype(jnp.float32) * lk1.astype(jnp.float32)))
           - jnp.exp(jnp.sum(lq2.astype(jnp.float32) * lk2.astype(jnp.float32))) + lam_init)
    o = diff_attention(q, k, v, lam, rel_bias)
    o = o * lax.rsqrt(jnp.square(o).mean(-1, keepdims=True) + LN_EPS) * sub_g.astype(jnp.float32)
    o = (o * (1.0 - lam_init)).transpose(0, 2, 1, 3).reshape(bsz, S, DIFF_W).astype(x.dtype)
    return o @ w_out

def conv_ffn(x, w_up, conv_w, conv_b, w_down):
    S = x.shape[1]
    h = x @ w_up
    hp = jnp.pad(h, ((0, 0), (CONV_W - 1, 0), (0, 0)))
    h = sum(hp[:, j:j + S] * conv_w[j] for j in range(CONV_W)) + conv_b
    u, g = jnp.split(h, 2, axis=-1)
    return (jax.nn.silu(g) * u) @ w_down

def first_inputs(seed: int = 0) -> dict:
    key = jax.random.key(seed)
    ks = jax.random.split(key, 20)
    nrm = lambda k, shape, s: jax.random.normal(k, shape, jnp.float32) * s
    return {
        "x": nrm(ks[0], (BATCH, SEQ, D_MODEL), 1.0),
        "w_in_even": nrm(ks[1], (N_EVEN, D_MODEL, EVEN_IN), D_MODEL ** -0.5),
        "w_out_even": nrm(ks[2], (N_EVEN, RET_W + SB_W, D_MODEL), (RET_W + SB_W) ** -0.5 * BETA),
        "w_in_odd": nrm(ks[3], (N_ODD, D_MODEL, ODD_IN), D_MODEL ** -0.5),
        "w_out_odd": nrm(ks[4], (N_ODD, DIFF_W, D_MODEL), DIFF_W ** -0.5 * BETA),
        "lam_q1": nrm(ks[5], (N_ODD, DIFF_DIM), 0.1),
        "lam_k1": nrm(ks[6], (N_ODD, DIFF_DIM), 0.1),
        "lam_q2": nrm(ks[7], (N_ODD, DIFF_DIM), 0.1),
        "lam_k2": nrm(ks[8], (N_ODD, DIFF_DIM), 0.1),
        "subln_g": 1.0 + nrm(ks[9], (N_ODD, 2 * DIFF_DIM), 0.02),
        "rel_bias": nrm(ks[10], (REL_BUCKETS, DIFF_HEADS), 0.5),
        "w_up": nrm(ks[11], (DEPTH, D_MODEL, 2 * D_FF), D_MODEL ** -0.5),
        "conv_w": nrm(ks[12], (DEPTH, CONV_W, 2 * D_FF), CONV_W ** -0.5),
        "conv_b": nrm(ks[13], (DEPTH, 2 * D_FF), 0.02),
        "w_down": nrm(ks[14], (DEPTH, D_FF, D_MODEL), D_FF ** -0.5 * BETA),
        "ln1_g": 1.0 + nrm(ks[15], (DEPTH, D_MODEL), 0.02),
        "ln1_b": nrm(ks[16], (DEPTH, D_MODEL), 0.02),
        "ln2_g": 1.0 + nrm(ks[17], (DEPTH, D_MODEL), 0.02),
        "ln2_b": nrm(ks[18], (DEPTH, D_MODEL), 0.02),
    }

def first_block(x, w_in_even, w_out_even, w_in_odd, w_out_odd, lam_q1, lam_k1, lam_q2, lam_k2,
              subln_g, rel_bias, w_up, conv_w, conv_b, w_down, ln1_g, ln1_b, ln2_g, ln2_b):
    for l in range(DEPTH):
        i = l // 2
        if l % 2 == 0:
            m = even_mixer(x, w_in_even[i], w_out_even[i])
        else:
            m = odd_mixer(x, w_in_odd[i], w_out_odd[i], lam_q1[i], lam_k1[i], lam_q2[i], lam_k2[i],
                          subln_g[i], rel_bias, l)
        x = layer_norm(ALPHA * x + m, ln1_g[l], ln1_b[l])
        f = conv_ffn(x, w_up[l], conv_w[l], conv_b[l], w_down[l])
        x = layer_norm(ALPHA * x + f, ln2_g[l], ln2_b[l])
    return x


DEPTH_2 = 1

D_MIX = D_MODEL
D_CONV = D_MIX // 2
D_MLSTM = D_MIX - D_CONV
N_HEADS = 4
HEAD_DIM = D_MLSTM // N_HEADS
CONV_WIDTH = 31
QK_CONV_WIDTH = 4
CHUNK = 128
N_GROUPS = 4
EXPERTS_PER_GROUP = 8
N_EXPERTS = N_GROUPS * EXPERTS_PER_GROUP
TOP_K = 2
D_EXPERT = D_MODEL // 2
MOE_BLOCK = 256
EPS = 1e-6
F_BIAS_LO = 3.0
F_BIAS_HI = 6.0
D_IN = 2 * D_CONV + 4 * D_MLSTM + 2 * N_HEADS


def rmsnorm(x, g):
    xf = x.astype(jnp.float32)
    y = xf * lax.rsqrt(jnp.mean(xf * xf, axis=-1, keepdims=True) + EPS)
    return (y * g.astype(jnp.float32)).astype(x.dtype)

def layernorm(x, g, b):
    xf = x.astype(jnp.float32)
    mu = jnp.mean(xf, axis=-1, keepdims=True)
    var = jnp.mean(jnp.square(xf - mu), axis=-1, keepdims=True)
    y = (xf - mu) * lax.rsqrt(var + EPS)
    return (y * g.astype(jnp.float32) + b.astype(jnp.float32)).astype(x.dtype)

def causal_depthwise_conv(x, w, b):
    width, ch = w.shape
    y = lax.conv_general_dilated(
        x, w[:, None, :].astype(x.dtype), window_strides=(1,), padding=[(width - 1, 0)],
        dimension_numbers=("NWC", "WIO", "NWC"), feature_group_count=ch)
    return y + b.astype(x.dtype)

def mlstm_chunkwise(q, k, v, i_pre, f_pre):
    B, H, S, Dh = q.shape
    nc = S // CHUNK
    k = k * (Dh ** -0.5)
    log_f = jax.nn.log_sigmoid(f_pre)

    def to_chunks(a):
        a = a.reshape(a.shape[:2] + (nc, CHUNK) + a.shape[3:])
        return jnp.moveaxis(a, 2, 0)

    qc, kc, vc = to_chunks(q), to_chunks(k), to_chunks(v)
    ic, fc = to_chunks(i_pre), to_chunks(log_f)
    causal = jnp.tril(jnp.ones((CHUNK, CHUNK), dtype=bool))

    def step(carry, inp):
        C, n, m = carry
        qb, kb, vb, ib, fb = inp
        b = jnp.cumsum(fb, axis=-1)
        d = b[..., :, None] - b[..., None, :] + ib[..., None, :]
        d = jnp.where(causal, d, -jnp.inf)
        g = b + m[..., None]
        m_t = jnp.maximum(g, jnp.max(d, axis=-1))
        w_intra = jnp.exp(d - m_t[..., None])
        w_inter = jnp.exp(g - m_t)
        s = jnp.einsum("bhtd,bhsd->bhts", qb, kb) * w_intra
        num = (jnp.einsum("bhts,bhsd->bhtd", s, vb)
               + w_inter[..., None] * jnp.einsum("bhvk,bhtk->bhtv", C, qb))
        den = jnp.sum(s, axis=-1) + w_inter * jnp.einsum("bhk,bhtk->bht", n, qb)
        h = num / jnp.maximum(jnp.abs(den), jnp.exp(-m_t))[..., None]
        b_last = b[..., -1]
        log_w = b_last[..., None] - b + ib
        m_new = jnp.maximum(b_last + m, jnp.max(log_w, axis=-1))
        decay = jnp.exp(b_last + m - m_new)
        w_state = jnp.exp(log_w - m_new[..., None])
        kw = kb * w_state[..., None]
        C_new = decay[..., None, None] * C + jnp.einsum("bhsv,bhsk->bhvk", vb, kw)
        n_new = decay[..., None] * n + jnp.sum(kw, axis=2)
        return (C_new, n_new, m_new), h

    init = (jnp.zeros((B, H, Dh, Dh), jnp.float32),
            jnp.zeros((B, H, Dh), jnp.float32),
            jnp.zeros((B, H), jnp.float32))
    _, hc = lax.scan(step, init, (qc, kc, vc, ic, fc))
    return jnp.moveaxis(hc, 0, 2).reshape(B, H, S, Dh)

def hybrid_mixer(h, w_in, b_in, conv_w, conv_b, conv_ln_g, conv_ln_b,
                 qk_conv_w, qk_conv_b, mlstm_norm_g, w_out):
    B, S, _ = h.shape
    z = jnp.einsum("bsd,de->bse", h, w_in) + b_in
    splits = np.cumsum([D_CONV, D_CONV, D_MLSTM, D_MLSTM, D_MLSTM, D_MLSTM, N_HEADS])
    conv_a, conv_gate, q, k, v, o, i_pre, f_pre = jnp.split(z, [int(i) for i in splits], axis=-1)

    u = conv_a * jax.nn.sigmoid(conv_gate)
    u = causal_depthwise_conv(u, conv_w, conv_b)
    u = jax.nn.silu(layernorm(u, conv_ln_g, conv_ln_b))

    qk = jax.nn.silu(causal_depthwise_conv(jnp.concatenate([q, k], axis=-1), qk_conv_w, qk_conv_b))
    q, k = qk[..., :D_MLSTM], qk[..., D_MLSTM:]

    def heads(a):
        return jnp.transpose(a.reshape(B, S, N_HEADS, HEAD_DIM), (0, 2, 1, 3)).astype(jnp.float32)

    ht = mlstm_chunkwise(heads(q), heads(k), heads(v),
                         jnp.transpose(i_pre, (0, 2, 1)).astype(jnp.float32),
                         jnp.transpose(f_pre, (0, 2, 1)).astype(jnp.float32))
    ht = jnp.transpose(ht, (0, 2, 1, 3))
    hm = jax.nn.sigmoid(o.astype(jnp.float32)).reshape(B, S, N_HEADS, HEAD_DIM) * ht
    mu = jnp.mean(hm, axis=-1, keepdims=True)
    var = jnp.mean(jnp.square(hm - mu), axis=-1, keepdims=True)
    hm = (hm - mu) * lax.rsqrt(var + EPS) * mlstm_norm_g.astype(jnp.float32).reshape(N_HEADS, HEAD_DIM)
    hm = hm.reshape(B, S, D_MLSTM).astype(h.dtype)

    y = jnp.concatenate([u, hm], axis=-1)
    return jnp.einsum("bse,ed->bsd", y, w_out)

def hierarchical_moe(h, rg_w, rg_b, re_w, re_b, w_gate, w_up, w_down):
    B, S, D = h.shape
    T = B * S
    xt = h.reshape(T, D)
    group_logits = (xt @ rg_w + rg_b).astype(jnp.float32)
    group_prob = jax.nn.softmax(group_logits, axis=-1)
    grp = jnp.argmax(group_logits, axis=-1).astype(jnp.int32)
    p_grp = jnp.take_along_axis(group_prob, grp[:, None], axis=-1)
    expert_logits = (xt @ re_w + re_b).astype(jnp.float32).reshape(T, N_GROUPS, EXPERTS_PER_GROUP)
    in_group = expert_logits[jnp.arange(T), grp]
    top_val, top_idx = lax.top_k(in_group, TOP_K)
    gate = p_grp * jax.nn.softmax(top_val, axis=-1)
    expert_id = grp[:, None] * EXPERTS_PER_GROUP + top_idx.astype(jnp.int32)

    n_assign = T * TOP_K
    e_flat = expert_id.reshape(-1)
    tok_flat = jnp.repeat(jnp.arange(T, dtype=jnp.int32), TOP_K)
    g_flat = gate.reshape(-1)
    order = jnp.argsort(e_flat)
    e_sorted, tok_sorted, g_sorted = e_flat[order], tok_flat[order], g_flat[order]
    counts = jnp.zeros((N_EXPERTS,), jnp.int32).at[e_flat].add(1)
    starts = jnp.cumsum(counts) - counts
    padded = (counts + MOE_BLOCK - 1) // MOE_BLOCK * MOE_BLOCK
    padded_ends = jnp.cumsum(padded)
    padded_starts = padded_ends - padded
    dest = padded_starts[e_sorted] + (jnp.arange(n_assign, dtype=jnp.int32) - starts[e_sorted])
    n_blocks = -(-n_assign // MOE_BLOCK) + N_EXPERTS
    n_slots = n_blocks * MOE_BLOCK
    slot_tok = jnp.zeros((n_slots,), jnp.int32).at[dest].set(tok_sorted)
    slot_gate = jnp.zeros((n_slots,), jnp.float32).at[dest].set(g_sorted)
    block_start = jnp.arange(n_blocks, dtype=jnp.int32) * MOE_BLOCK
    block_expert = jnp.minimum(jnp.sum(block_start[:, None] >= padded_ends[None, :], axis=1),
                               N_EXPERTS - 1).astype(jnp.int32)

    xs = xt[slot_tok].reshape(n_blocks, MOE_BLOCK, D)

    def expert_block(args):
        xb, e = args
        a = xb @ w_gate[e]
        u = xb @ w_up[e]
        return (jax.nn.silu(a) * u) @ w_down[e]

    ys = lax.map(expert_block, (xs, block_expert)).reshape(n_slots, D)
    ys = ys * slot_gate[:, None].astype(ys.dtype)
    out = jnp.zeros((T, D), ys.dtype).at[slot_tok].add(ys)
    return out.reshape(B, S, D).astype(h.dtype)

def second_inputs(seed: int = 0) -> dict:
    key = jax.random.key(seed)
    ks = jax.random.split(key, 21)
    f32 = jnp.float32
    L = DEPTH_2

    def nrm(k, shape, scale):
        return jax.random.normal(k, shape, f32) * scale

    b_in = nrm(ks[3], (L, D_IN), 0.02)
    b_in = b_in.at[:, D_IN - N_HEADS:].add(jnp.linspace(F_BIAS_LO, F_BIAS_HI, N_HEADS, dtype=f32))
    return {
        "x": nrm(ks[0], (BATCH, SEQ, D_MODEL), 1.0),
        "norm_mix_g": 1.0 + nrm(ks[1], (L, D_MODEL), 0.02),
        "w_in": nrm(ks[2], (L, D_MODEL, D_IN), D_MODEL ** -0.5),
        "b_in": b_in,
        "conv_w": nrm(ks[4], (L, CONV_WIDTH, D_CONV), CONV_WIDTH ** -0.5),
        "conv_b": nrm(ks[5], (L, D_CONV), 0.02),
        "conv_ln_g": 1.0 + nrm(ks[6], (L, D_CONV), 0.02),
        "conv_ln_b": nrm(ks[7], (L, D_CONV), 0.02),
        "qk_conv_w": nrm(ks[8], (L, QK_CONV_WIDTH, 2 * D_MLSTM), QK_CONV_WIDTH ** -0.5),
        "qk_conv_b": nrm(ks[9], (L, 2 * D_MLSTM), 0.02),
        "mlstm_norm_g": 1.0 + nrm(ks[10], (L, D_MLSTM), 0.02),
        "w_out": nrm(ks[11], (L, D_MIX, D_MODEL), D_MIX ** -0.5),
        "norm_ffn_g": 1.0 + nrm(ks[12], (L, D_MODEL), 0.02),
        "router_group_w": nrm(ks[13], (L, D_MODEL, N_GROUPS), D_MODEL ** -0.5),
        "router_group_b": nrm(ks[14], (L, N_GROUPS), 0.01),
        "router_expert_w": nrm(ks[15], (L, D_MODEL, N_EXPERTS), D_MODEL ** -0.5),
        "router_expert_b": nrm(ks[16], (L, N_EXPERTS), 0.01),
        "expert_w_gate": nrm(ks[17], (L, N_EXPERTS, D_MODEL, D_EXPERT), D_MODEL ** -0.5),
        "expert_w_up": nrm(ks[18], (L, N_EXPERTS, D_MODEL, D_EXPERT), D_MODEL ** -0.5),
        "expert_w_down": nrm(ks[19], (L, N_EXPERTS, D_EXPERT, D_MODEL), D_EXPERT ** -0.5),
        "final_norm_g": 1.0 + nrm(ks[20], (D_MODEL,), 0.02),
    }

def second_block(x, norm_mix_g, w_in, b_in, conv_w, conv_b, conv_ln_g, conv_ln_b,
              qk_conv_w, qk_conv_b, mlstm_norm_g, w_out, norm_ffn_g,
              router_group_w, router_group_b, router_expert_w, router_expert_b,
              expert_w_gate, expert_w_up, expert_w_down, final_norm_g):
    for l in range(DEPTH_2):
        h = rmsnorm(x, norm_mix_g[l])
        x = x + hybrid_mixer(h, w_in[l], b_in[l], conv_w[l], conv_b[l], conv_ln_g[l], conv_ln_b[l],
                             qk_conv_w[l], qk_conv_b[l], mlstm_norm_g[l], w_out[l])
        h = rmsnorm(x, norm_ffn_g[l])
        x = x + hierarchical_moe(h, router_group_w[l], router_group_b[l],
                                 router_expert_w[l], router_expert_b[l],
                                 expert_w_gate[l], expert_w_up[l], expert_w_down[l])
    return rmsnorm(x, final_norm_g)


def setup_inputs(seed=0):
    out = dict(first_inputs(seed))
    for name, value in second_inputs(seed + 1).items():
        if name != "x":
            out[name + "_2"] = value
    return out


def reference(
    x, w_in_even, w_out_even, w_in_odd, w_out_odd, lam_q1, lam_k1, lam_q2, lam_k2, subln_g,
    rel_bias, w_up, conv_w, conv_b, w_down, ln1_g, ln1_b, ln2_g, ln2_b, norm_mix_g_2, w_in_2,
    b_in_2, conv_w_2, conv_b_2, conv_ln_g_2, conv_ln_b_2, qk_conv_w_2, qk_conv_b_2,
    mlstm_norm_g_2, w_out_2, norm_ffn_g_2, router_group_w_2, router_group_b_2,
    router_expert_w_2, router_expert_b_2, expert_w_gate_2, expert_w_up_2, expert_w_down_2,
    final_norm_g_2,
):
    x = first_block(
        x, w_in_even, w_out_even, w_in_odd, w_out_odd, lam_q1, lam_k1, lam_q2, lam_k2, subln_g,
        rel_bias, w_up, conv_w, conv_b, w_down, ln1_g, ln1_b, ln2_g, ln2_b,
    )
    return second_block(
        x, norm_mix_g_2, w_in_2, b_in_2, conv_w_2, conv_b_2, conv_ln_g_2, conv_ln_b_2,
        qk_conv_w_2, qk_conv_b_2, mlstm_norm_g_2, w_out_2, norm_ffn_g_2, router_group_w_2,
        router_group_b_2, router_expert_w_2, router_expert_b_2, expert_w_gate_2, expert_w_up_2,
        expert_w_down_2, final_norm_g_2,
    )


_drawn_inputs = setup_inputs


def setup_inputs(seed=0):
    import zlib

    import numpy as np

    out = dict(_drawn_inputs(seed))
    spreads = {}
    factors = {'lam_q1': 64.0,
     'subln_g': 9.005,
     'conv_ln_g_2': 14.557,
     'conv_ln_b_2': 15.895,
     'qk_conv_b_2': 3.855,
     'mlstm_norm_g_2': 9.439,
     'router_group_b_2': 58.555,
     'router_expert_b_2': 19.605,
     'final_norm_g_2': 7.825,
     'conv_b': 2.911,
     'norm_ffn_g_2': 5.812}
    for name, (base, spread) in spreads.items():
        noise = np.random.default_rng([zlib.crc32(name.encode()), seed]).standard_normal(out[name].shape)
        drawn = base * np.exp(spread * noise) if base else spread * noise
        out[name] = __import__('jax').numpy.asarray(drawn.astype(out[name].dtype))
    for name, factor in factors.items():
        out[name] = (out[name] * factor).astype(out[name].dtype)
    return out
```

```python
from contextlib import ExitStack
import math

import numpy as np

import concourse.bass as bass
from concourse import mybir

ALU = mybir.AluOpType
ACT = mybir.ActivationFunctionType
F32 = mybir.dt.float32
U32 = mybir.dt.uint32
I32 = mybir.dt.int32

P = 128
S = 512
NT = S // P
D = 1024
KC = D // P
DH = 64
FF = 2816
FT = FF // P
UD = FF // 256
ALPHA = 4.0 ** 0.25
LN_EPS = 1e-5
EPS = 1e-6
EVEN_IN, ODD_IN, IN_2 = 3584, 3072, 3080
CW = 31
NE, NG, EPG = 32, 4, 8
DE = 512
EXTRA = 7
NBLK = NE + EXTRA
LAM_INIT = 0.8 - 0.6 * math.exp(-0.3)
NEG = -1e30

RING = 12
SLOT = 2048
OFF = [0, 512, 896, 1152]
CAUSAL = 1280


class Namespace:
    pass


class Plan:

    def __init__(self):
        self.at, self.uses, self.dmas = 0, [0] * RING, [0] * RING

    def place(self, s, dmas, times=1):
        out = (s, self.uses[s], self.dmas[s], dmas)
        self.uses[s] += times
        self.dmas[s] += dmas * times
        return out

    def take(self, n, dmas=1):
        out = [self.place((self.at + i) % RING, dmas) for i in range(n)]
        self.at = (self.at + n) % RING
        return out

    def turn(self, n, dmas, times):
        self.at = n % RING
        return [self.place(s, dmas, times) for s in range(n)]


def shape_constants():
    pos = np.arange(S, dtype=np.float32)
    inv = (10000.0 ** (-np.arange(0, P, 2, dtype=np.float32) / P)).astype(np.float32)
    ang = (pos[:, None] * inv[None, :]).astype(np.float32)
    cos, sin = np.cos(ang), np.sin(ang)
    c = np.concatenate([cos, cos], 1).reshape(NT, P, P).transpose(1, 0, 2)
    s = np.concatenate([-sin, sin], 1).reshape(NT, P, P).transpose(1, 0, 2)
    rope = np.stack([c, s], 1).reshape(P, 2 * NT * P).astype(np.float32)
    j, i = np.arange(P)[:, None], np.arange(S)[None, :]
    decay = []
    for h in range(4):
        g = math.log(1.0 - 2.0 ** (-5.0 - h))
        decay.append(np.where(i >= j, np.exp(g * np.maximum(i - j, 0)), 0.0) * P ** -0.5)
    decay = np.stack(decay, 1).reshape(P, 4 * S).astype(np.float32)
    a, b = np.arange(P)[:, None], np.arange(P)[None, :]
    small = [np.eye(P), -(a >= b).astype(np.float32), -np.ones((P, P)), (a < b).astype(np.float32)]
    small = np.concatenate(small, 1).astype(np.float32)
    n = np.maximum(511 - np.arange(640), 0)
    nf = np.maximum(n, 1).astype(np.float32)
    large = 16 + (np.log(nf / np.float32(16)) / np.float32(math.log(8.0)) * np.float32(16)).astype(np.int32)
    bucket = np.where(n < 16, n, np.minimum(large, 31))
    onehot = (np.arange(32)[:, None] == bucket[None, :]).astype(np.float32)
    sel = (np.arange(4)[:, None] == (np.arange(512)[None, :] // P)).astype(np.float32)
    iota = np.zeros((P, 64), np.float32)
    iota[:, 0:32] = np.arange(32)[None, :]
    iota[:, 32:40] = np.arange(8)[None, :]
    iota[:, 40:44] = np.arange(4)[None, :] * P + np.arange(P)[:, None]
    return {"c_rope": rope, "c_decay": decay, "c_small": small, "c_onehot": onehot, "c_sel": sel,
            "c_iota": iota}




def columns(w, col, n, k0=0, nk=KC):
    v = w.rearrange("(k p) c -> p k c", p=P)
    return v[:, k0:k0 + nk, col:col + n] if isinstance(col, int) else v[:, k0:k0 + nk, bass.ds(col, n)]


def load_slab(k, sp, slab, sources, turn=0):
    slot, uses, _, dmas = slab
    assert dmas == len(sources)
    if uses:
        sp.wait_ge(k.freed[slot], turn + uses)
    chunks = sources[0].shape[1]
    n = sources[0].shape[2]
    to = k.ring[:, slot, 0:chunks * n * dmas].rearrange("p (k q n) -> p k q n", q=dmas, n=n)
    for i, source in enumerate(sources):
        sp.dma_start(to[:, :, i, :], source).then_inc(k.landed[slot], 16)


def slab_ready(k, pe, slab, turn=0):
    slot, _, before, dmas = slab
    pe.wait_ge(k.landed[slot], turn * (16 * dmas) + 16 * (before + dmas))


def wait_for(eng, what):
    if what is not None:
        eng.wait_ge(*what)


def row_piece(w, n):
    return bass.AP(tensor=w.tensor, offset=w.offset, ap=[[0, 128], [1, n]])


def entry(k):
    A = k.A
    k.s_const = k.sem("constants_in")
    turned, out = k.sem("in_turned"), k.sem("in_transposed")
    loaded = [k.sem(f"x_loaded{t}") for t in range(NT)]
    k.xt_in = out

    def sync(sp):
        sp.dma_start(k.small[:], A["c_small"]).then_inc(k.s_const, 16)
        for t in range(NT):
            sp.dma_start(k.X[:, t, :], A["x"][0, t * P:(t + 1) * P, :]).then_inc(loaded[t], 16)

    def tensor(pe):
        pe.wait_ge(k.s_const, 16)
        for t in range(NT):
            pe.wait_ge(loaded[t], 16)
            for half in range(2):
                if t > 0:
                    pe.wait_ge(out, 2 * (t - 1) + half + 1)
                for c in range(4):
                    i = 4 * half + c
                    mm = pe.transpose(k.PS[:, 4 + half, c * P:(c + 1) * P],
                                      k.X[:, t, i * P:(i + 1) * P], k.ident)
                mm.then_inc(turned, 1)

    def scalar(act):
        for t in range(NT):
            for half in range(2):
                act.wait_ge(turned, 2 * t + half + 1)
                act.copy(k.XT[:, 4 * half:4 * half + 4, t * P:(t + 1) * P],
                         k.PS[:, 4 + half, :].rearrange("p (c n) -> p c n", c=4)).then_inc(out, 1)

    return dict(sync=sync, tensor=tensor, scalar=scalar)


def retention_stage(k):
    A, W, PS = k.A, k.W, k.PS
    YT = W[:, 0:4096].rearrange("p (c n) -> p c n", c=KC)
    cos = W[:, 4096:4608].rearrange("p (t n) -> p t n", t=NT)
    sin = W[:, 4608:5120].rearrange("p (t n) -> p t n", t=NT)
    decay = W[:, 5120:7168].rearrange("p (h n) -> p h n", h=4)
    rot = W[:, 7168:8192].rearrange("p (t n) -> p t n", t=NT)
    tmp = W[:, 8192:8448]
    v = W[:, 8448:9472].rearrange("p (b t n) -> p b t n", b=2, t=NT)
    gate = W[:, 9472:10496].rearrange("p (b t n) -> p b t n", b=2, t=NT)
    qT, kT = W[:, 10496:11008], W[:, 11008:11520]
    probs = W[:, 11520:12800]
    on = W[:, 12800:13312].rearrange("p (t n) -> p t n", t=NT)
    stats, mv = k.stat[:, :, 0:6], k.stat[:, :, 6:8]
    sd, rstd = k.stat[:, :, 8], k.stat[:, :, 9]
    ident = k.ident
    tables = k.sem("ret_tables")
    projected, rotated, kept = k.sem("ret_projected"), k.sem("ret_rotated"), k.sem("ret_kept")
    qk_turned, qk_out = k.sem("ret_qk_turned"), k.sem("ret_qk_out")
    scored, masked = k.sem("ret_scored"), k.sem("ret_masked")
    summed, varied, rooted = k.sem("ret_summed"), k.sem("ret_varied"), k.sem("ret_rooted")
    normed, y_turned, y_out = k.sem("ret_normed"), k.sem("ret_y_turned"), k.sem("ret_y_out")
    k.ret_y_out, k.ret_masked, k.ret_summed = y_out, masked, summed
    k.ret_rotated, k.ret_kept, k.ret_normed = rotated, kept, normed
    H = 4
    place = [(2, 0), (3, 0), (0, 0), (3, 384)]

    def sync(sp):
        w = A["w_in_even"][0]
        for h in range(H):
            for half in range(2):
                load_slab(k, sp, k.ret_slabs[h][half],
                          [columns(w, h * P + 512 * part, P, 4 * half, 4) for part in range(4)])
            if h == 0:
                sp.dma_start(W[:, 4096:5120], A["c_rope"]).then_inc(tables, 16)
                sp.dma_start(W[:, 5120:7168], A["c_decay"]).then_inc(tables, 16)

    def tensor(pe):
        def project(h, t):
            if h > 0:
                pe.wait_ge(rotated, 4 * (h - 1) + t + 1)
                pe.wait_ge(kept, 4 * (h - 1) + t + 1)
            for c in range(KC):
                slab = k.ret_slabs[h][c // 4]
                if t == 0 and c % 4 == 0:
                    slab_ready(k, pe, slab)
                w = k.ring[:, slab[0], :].rearrange("p (k n) -> p k n", k=4)[:, c % 4, :]
                mm = pe.matmul(PS[:, 4 + t, :], k.XT[:, c, t * P:(t + 1) * P], w,
                               start=(c == 0), stop=(c == KC - 1))
                if t == NT - 1 and c == 3:
                    mm.then_inc(k.freed[slab[0]], 1)
            mm.then_inc(projected, 1)

        def turn_y(h):
            pe.wait_ge(normed, h + 1)
            for t in range(NT):
                mm = pe.transpose(PS[:, 2, t * P:(t + 1) * P], on[:, t, :], ident)
            mm.then_inc(y_turned, 1)

        pe.wait_ge(k.xt_in, 2 * NT)
        pe.wait_ge(k.taps_in, 1)
        pe.wait_ge(k.cols_in, 1)
        for t in range(NT):
            project(0, t)
        for h in range(H):
            pe.drain().then_inc(k.freed[k.ret_slabs[h][1][0]], 1)
            pe.wait_ge(rotated, 4 * h + 4)
            for part in range(2):
                for t in range(NT):
                    mm = pe.transpose(PS[:, part, t * P:(t + 1) * P],
                                      rot[:, t, part * P:(part + 1) * P], ident)
                mm.then_inc(qk_turned, 1)
            pe.wait_ge(qk_out, 2 * h + 2)
            if h > 0:
                pe.wait_ge(y_out, h)
            for j in range(NT):
                bank, col = place[j]
                n = S - j * P
                mm = pe.matmul(PS[:, bank, col:col + n], kT[:, j * P:(j + 1) * P], qT[:, j * P:S],
                               start=True, stop=True)
                mm.then_inc(scored, 1)
            if h + 1 < H:
                project(h + 1, 0)
                project(h + 1, 1)
            pe.wait_ge(masked, 4 * h + 4)
            pe.wait_ge(kept, 4 * h + 4)
            for i in range(NT):
                for j in range(i + 1):
                    p0 = OFF[j] + (i - j) * P
                    mm = pe.matmul(PS[:, 1, i * P:(i + 1) * P], probs[:, p0:p0 + P],
                                   v[:, h % 2, j, :], start=(j == 0), stop=(j == i))
            mm.then_inc(summed, 1)
            if h + 1 < H:
                project(h + 1, 2)
                project(h + 1, 3)
            turn_y(h)

    def scalar(act):
        def keep(h, t):
            act.wait_ge(rotated, 4 * h + t + 1)
            if h > 1:
                act.wait_ge(summed, h - 1)
                act.wait_ge(normed, h - 1)
            act.activation(gate[:, h % 2, t, :], PS[:, 4 + t, 384:512], ACT.Silu)
            act.copy(v[:, h % 2, t, :], PS[:, 4 + t, 256:384]).then_inc(kept, 1)

        def roots(h):
            act.wait_ge(varied, h + 1)
            act.activation(sd, mv[:, :, 1], ACT.Sqrt, bias=k.eps_ln).then_inc(rooted, 1)

        for t in range(NT):
            keep(0, t)
        for h in range(H):
            for part in range(2):
                act.wait_ge(qk_turned, 2 * h + part + 1)
                if h > 0:
                    act.wait_ge(scored, 4 * h)
                act.copy([qT, kT][part], PS[:, part, :]).then_inc(qk_out, 1)
            if h + 1 < H:
                keep(h + 1, 0)
                keep(h + 1, 1)
            roots(h)
            if h + 1 < H:
                keep(h + 1, 2)
                keep(h + 1, 3)
            act.wait_ge(y_turned, h + 1)
            act.copy(YT[:, h, :], PS[:, 2, :]).then_inc(y_out, 1)

    def vector(dve):
        def rotate(h, t):
            dve.wait_ge(projected, 4 * h + t + 1)
            if h > 0:
                dve.wait_ge(qk_turned, 2 * h)
            two = lambda ap: bass.AP(tensor=ap.tensor, offset=ap.offset,
                                     ap=[list(ap.ap[0]), [0, 2], list(ap.ap[1])])
            qk = PS[:, 4 + t, 0:256].rearrange("p (q n) -> p q n", q=2)
            r = rot[:, t, :].rearrange("p (q n) -> p q n", q=2)
            w = tmp.rearrange("p (q n) -> p q n", q=2)
            dve.drain()
            dve.tensor_tensor(r, qk, two(cos[:, t, :]), ALU.mult)
            dve.tensor_tensor(w[:, :, 0:64], qk[:, :, 64:128], two(sin[:, t, 0:64]), ALU.mult)
            dve.tensor_tensor(w[:, :, 64:128], qk[:, :, 0:64], two(sin[:, t, 64:128]), ALU.mult)
            dve.drain()
            dve.tensor_tensor(r, r, w, ALU.add).then_inc(rotated, 1)

        dve.wait_ge(tables, 32)
        for t in range(NT):
            rotate(0, t)
        for h in range(H):
            if h > 0:
                dve.wait_ge(summed, h)
            dve.wait_ge(scored, 4 * h + 4)
            for j in range(NT):
                bank, col = place[j]
                n = S - j * P
                dve.tensor_tensor(probs[:, OFF[j]:OFF[j] + n], PS[:, bank, col:col + n],
                                  decay[:, h, 0:n], ALU.mult).then_inc(masked, 1)
            if h + 1 < H:
                rotate(h + 1, 0)
                rotate(h + 1, 1)
            dve.wait_ge(summed, h + 1)
            for t in range(NT):
                dve.bn_stats(stats[:, t, :], PS[:, 1, t * P:(t + 1) * P])
            dve.drain()
            for t in range(NT):
                mm = dve.bn_aggr(mv[:, t, :], stats[:, t, :])
            mm.then_inc(varied, 1)
            dve.wait_ge(rooted, h + 1)
            dve.reciprocal(rstd, sd)
            dve.drain()
            if h > 0:
                dve.wait_ge(y_turned, h)
            for t in range(NT):
                dve.tensor_scalar(on[:, t, :], PS[:, 1, t * P:(t + 1) * P], mv[:, t, 0:1],
                                  rstd[:, t:t + 1], ALU.subtract, ALU.mult)
            dve.drain()
            dve.wait_ge(kept, 4 * h + 4)
            dve.tensor_tensor(on, on, gate[:, h % 2, :, :], ALU.mult).then_inc(normed, 1)
            if h + 1 < H:
                rotate(h + 1, 2)
                rotate(h + 1, 3)

    return dict(sync=sync, tensor=tensor, scalar=scalar, vector=vector)

def stick_stage(k):
    A, W, PS = k.A, k.W, k.PS
    YT = W[:, 0:4096].rearrange("p (c n) -> p c n", c=KC)
    q, kk = W[:, 13312:13824], W[:, 13824:14336]
    v = W[:, 14336:14848].rearrange("p (t n) -> p t n", t=NT)
    e = W[:, 14848:16128]
    soft = [W[:, 4096:5376], W[:, 5376:6656]]
    a = [W[:, 6656:7936], W[:, 7936:9216]]
    projected, kept = k.sem("sb_projected"), k.sem("sb_kept")
    v_kept = k.sem("sb_v_kept")
    scored, logged, softened, cut = k.sem("sb_scored"), k.sem("sb_logged"), k.sem("sb_softened"), k.sem("sb_cut")
    summed, exped, masked = k.sem("sb_summed"), k.sem("sb_exped"), k.sem("sb_masked")
    valued, y_out = k.sem("sb_valued"), k.sem("sb_y_out")
    k.sb_y_out = y_out
    place = [(0, 0), (1, 0), (2, 0), (1, 384)]
    COL = [0, 512, 1024, 896]

    def sync(sp):
        w = A["w_in_even"][0]
        for p in range(4):
            for half in range(2):
                load_slab(k, sp, k.sb_slabs[p][half],
                          [columns(w, 2048 + p * P + 512 * part, P, 4 * half, 4) for part in range(3)])

    def tensor(pe):
        def project(p, part):
            n = 3 * p + part
            slabs = k.sb_slabs[p]
            if n >= 2:
                if part == 2:
                    pe.wait_ge(kept, 2 * p + 1)
                elif part == 0:
                    pe.wait_ge(kept, 2 * p)
                else:
                    pe.wait_ge(v_kept, p)
            elif part == 0:
                pe.wait_ge(k.ret_kept, 16)
                pe.wait_ge(k.ret_rotated, 16)
            bank = 6 + (n % 2)
            for c in range(KC):
                slab = slabs[c // 4]
                if part == 0 and c % 4 == 0:
                    slab_ready(k, pe, slab)
                w = k.ring[:, slab[0], 0:4 * 3 * P].rearrange("p (k n) -> p k n", k=4)[:, c % 4, :]
                w = w[:, part * P:(part + 1) * P]
                if part < 2:
                    mm = pe.matmul(PS[:, bank, :], w, k.XT[:, c, :], start=(c == 0), stop=(c == KC - 1))
            if part == 2:
                for t in range(NT):
                    for c in range(KC):
                        slab = slabs[c // 4]
                        w = k.ring[:, slab[0], 0:4 * 3 * P].rearrange("p (k n) -> p k n", k=4)[:, c % 4, :]
                        mm = pe.matmul(PS[:, bank, t * P:(t + 1) * P], k.XT[:, c, t * P:(t + 1) * P],
                                       w[:, 2 * P:3 * P], start=(c == 0), stop=(c == KC - 1))
                        if t == NT - 1 and c == 3:
                            mm.then_inc(k.freed[slabs[0][0]], 1)
            mm.then_inc(projected, 1)
            if part == 2:
                pe.drain().then_inc(k.freed[slabs[1][0]], 1)

        for part in range(3):
            project(0, part)
        for p in range(4):
            pe.wait_ge(kept, 2 * p + 2)
            for hh in range(2):
                if p > 0:
                    pe.wait_ge(y_out, 2 * (p - 1) + hh + 1)
                elif hh == 0:
                    pe.wait_ge(k.ret_masked, 16)
                    pe.wait_ge(k.ret_normed, 4)
                    pe.wait_ge(k.ret_y_out, 4)
                r = slice(64 * hh, 64 * hh + 64)
                for j in range(NT):
                    bank, col = place[j]
                    n = S - j * P
                    mm = pe.matmul(PS[:, 3 * hh + bank, col:col + n], kk[r, j * P:(j + 1) * P],
                                   q[r, j * P:S], start=(j != 3), stop=False, skip_group_check=True)
                mm.then_inc(scored, 1)
            if p < 3:
                for part in range(3):
                    project(p + 1, part)
            for hh in range(2):
                pe.wait_ge(cut, 2 * p + hh + 1)
                for j in range(NT):
                    bank, col = place[j]
                    for j2 in range(j, NT):
                        lo = (j2 - j) * P
                        n = S - j2 * P
                        mm = pe.matmul(PS[:, 3 * hh + bank, col + lo:col + lo + n],
                                       k.negtri if j2 == j else k.negone,
                                       soft[hh][:, COL[j2]:COL[j2] + n],
                                       start=False, stop=(j2 == NT - 1), skip_group_check=True)
                mm.then_inc(summed, 1)
            pe.wait_ge(v_kept, p + 1)
            for hh in range(2):
                pe.wait_ge(masked, 2 * p + hh + 1)
                r = slice(64 * hh, 64 * hh + 64)
                for j in range(NT):
                    mm = pe.matmul(PS[r, 3 * hh, j * P:S], v[:, j, r],
                                   a[hh][:, COL[j]:COL[j] + S - j * P],
                                   start=(j == 0), stop=(j == NT - 1), skip_group_check=True)
                mm.then_inc(valued, 1)

    def scalar(act):
        def keep(p):
            for part in range(2):
                act.wait_ge(projected, 3 * p + part + 1)
                if p > 0:
                    act.wait_ge(scored, 2 * p)
                elif part == 0:
                    act.wait_ge(k.ret_y_out, 4)
                act.mul([q, kk][part], PS[:, 6 + (3 * p + part) % 2, :],
                        [DH ** -0.5, 1.0][part]).then_inc(kept, 1)

        def keep_v(p):
            act.wait_ge(projected, 3 * p + 3)
            if p > 0:
                act.wait_ge(valued, 2 * p)
            act.copy(v, PS[:, 6 + (3 * p + 2) % 2, :].rearrange("p (t n) -> p t n", t=NT))\
               .then_inc(v_kept, 1)

        keep(0)
        keep_v(0)
        for p in range(4):
            for hh in range(2):
                act.wait_ge(scored, 2 * p + hh + 1)
                if 2 * p + hh > 0:
                    act.wait_ge(softened, 2 * p + hh)
                zz = PS[:, 3 * hh:3 * hh + 3, :].rearrange("p b n -> p (b n)")[:, 0:CAUSAL]
                act.activation(e, zz, ACT.Abs)
                act.drain()
                act.activation(e, e, ACT.Exp, scale=-1.0)
                act.drain()
                act.activation(e, e, ACT.Ln, bias=1.0).then_inc(logged, 1)
            if p < 3:
                keep(p + 1)
            for hh in range(2):
                act.wait_ge(summed, 2 * p + hh + 1)
                if p > 0:
                    act.wait_ge(valued, 2 * (p - 1) + hh + 1)
                zz = PS[:, 3 * hh:3 * hh + 3, :].rearrange("p b n -> p (b n)")[:, 0:CAUSAL]
                act.activation(a[hh], zz, ACT.Exp).then_inc(exped, 1)
            if p < 3:
                keep_v(p + 1)

    def gpsimd(pool):
        cols = COL
        for p in range(4):
            for hh in range(2):
                pool.wait_ge(softened, 2 * p + hh + 1)
                for j in range(NT):
                    d = soft[hh][:, cols[j]:cols[j] + P]
                    mm = pool.affine_select(out=d, in_=d, pattern=[[1, P]], compare_op=ALU.is_gt,
                                            fill=0.0, base=0, channel_multiplier=-1)
                mm.then_inc(cut, 1)
            for hh in range(2):
                pool.wait_ge(exped, 2 * p + hh + 1)
                for j in range(NT):
                    d = a[hh][:, cols[j]:cols[j] + P]
                    mm = pool.affine_select(out=d, in_=d, pattern=[[1, P]], compare_op=ALU.is_gt,
                                            fill=0.0, base=0, channel_multiplier=-1)
                mm.then_inc(masked, 1)

    def vector(dve):
        def keep_y(p):
            for hh in range(2):
                r = slice(64 * hh, 64 * hh + 64)
                dve.wait_ge(valued, 2 * p + hh + 1)
                dve.tensor_copy(YT[r, 4 + p, :], PS[r, 3 * hh, :]).then_inc(y_out, 1)

        for p in range(4):
            for hh in range(2):
                dve.wait_ge(logged, 2 * p + hh + 1)
                if p > 0:
                    dve.wait_ge(summed, 2 * (p - 1) + hh + 1)
                zz = PS[:, 3 * hh:3 * hh + 3, :].rearrange("p b n -> p (b n)")[:, 0:CAUSAL]
                dve.scalar_tensor_tensor(soft[hh], zz, 0.0, e, ALU.max, ALU.add).then_inc(softened, 1)
            keep_y(p)

    return dict(sync=sync, tensor=tensor, scalar=scalar, vector=vector, gpsimd=gpsimd)

def mix_out_stage(k, name, w_out, slabs, ready, gains, mode):
    W = k.W
    YT = W[:, 0:4096].rearrange("p (c n) -> p c n", c=KC)
    tail = norm_tail(k, name, gains, mode)

    def sync(sp):
        for i in range(4):
            load_slab(k, sp, slabs[i], [columns(w_out, 0, D, 2 * i, 2)])

    def tensor(pe):
        for s, v in ready:
            pe.wait_ge(s, v)
        for t in range(NT):
            if t >= 2:
                pe.wait_ge(tail.summed, t - 1)
            for c in range(KC):
                slab = slabs[c // 2]
                if t == 0 and c % 2 == 0:
                    slab_ready(k, pe, slab)
                w = k.ring[:, slab[0], :].rearrange("p (k n) -> p k n", k=2)[:, c % 2, :]
                for half in range(2):
                    mm = pe.matmul(k.PS[:, 2 * (t % 2) + half, :], YT[:, c, t * P:(t + 1) * P],
                                   w[:, 512 * half:512 * half + 512], start=(c == 0), stop=(c == KC - 1))
                if t == NT - 1 and c % 2 == 1 and c < KC - 1:
                    mm.then_inc(k.freed[slab[0]], 1)
            mm.then_inc(tail.product, 1)
            if t > 0:
                tail.turn(pe, t - 1)
        pe.drain().then_inc(k.freed[slabs[3][0]], 1)
        tail.turn(pe, NT - 1)

    return dict(sync=sync, tensor=tensor, scalar=tail.scalar, vector=tail.vector, gpsimd=tail.gpsimd)


def norm_tail(k, name, gains, mode):
    W, X, PS = k.W, k.X, k.PS
    r = W[:, 13824:14848]
    nh = 4 if mode == "rms" else 2
    hrow = (W[:, 4096:8192] if mode == "rms" else W[:, 11264:13312]).rearrange("p (b n) -> p b n", b=nh)
    tail = Namespace()
    tail.product = product = k.sem(name + "_product")
    tail.summed = summed = k.sem(name + "_summed")
    varied, rooted = k.sem(name + "_varied"), k.sem(name + "_rooted")
    normed, turned, xt_out = k.sem(name + "_normed"), k.sem(name + "_turned"), k.sem(name + "_xt_out")
    rows_in = k.sem(name + "_rows")
    before = k.rows_used
    k.rows_used = (normed, NT)
    st = k.stat
    pair = (lambda t: 2 * (t % 2)) if name != "ffn0" and name != "ffn1" else (lambda t: 2 * t)
    src = (lambda t: X[:, t, :]) if mode == "ln" else (lambda t: hrow[:, t % nh, :])
    scale = 1.0 if mode == "rms" else ALPHA

    def gpsimd(pool):
        wait_for(pool, before)
        for i, g in enumerate(gains):
            pool.dma_start(k.rows[:, i, :], row_piece(g, D)).then_inc(rows_in, 16)
        pool.wait_ge(rows_in, 16 * len(gains))

    def turn(pe, t):
        pe.wait_ge(normed, t + 1)
        for half in range(2):
            if t > 0:
                pe.wait_ge(xt_out, 2 * (t - 1) + half + 1)
            bank = tail.turn_banks[half]
            for c in range(4):
                i = 4 * half + c
                mm = pe.transpose(PS[:, bank, c * P:(c + 1) * P], src(t)[:, i * P:(i + 1) * P], k.ident)
            mm.then_inc(turned, 1)

    norms = 2 if mode == "ln+rms" else 1

    def scalar(act):
        for t in range(NT):
            for n in range(norms):
                act.wait_ge(varied, norms * t + n + 1)
                act.activation(st[:, t, 14:15], st[:, t, 13:14], ACT.Sqrt,
                               bias=k.eps_ln if mode != "rms" and n == 0 else k.eps_rms)\
                   .then_inc(rooted, 1)
            for half in range(2):
                act.wait_ge(turned, 2 * t + half + 1)
                act.copy(k.XT[:, 4 * half:4 * half + 4, t * P:(t + 1) * P],
                         PS[:, tail.turn_banks[half], :].rearrange("p (c n) -> p c n", c=4))\
                   .then_inc(xt_out, 1)

    def vector(dve):
        dve.wait_ge(rows_in, 16 * len(gains))
        for t in range(NT):
            dve.wait_ge(product, t + 1)
            for half in range(2):
                c = slice(512 * half, 512 * half + 512)
                to = r if mode != "rms" else X[:, t, :]
                mm = dve.scalar_tensor_tensor(to[:, c], X[:, t, c], scale, PS[:, pair(t) + half, :],
                                              ALU.mult, ALU.add)
            mm.then_inc(summed, 1)
            dve.drain()
            if mode != "rms":
                for half in range(2):
                    dve.bn_stats(st[:, t, 6 * half:6 * half + 6], r[:, 512 * half:512 * half + 512])
                dve.drain()
                dve.bn_aggr(st[:, t, 12:14], st[:, t, 0:12]).then_inc(varied, 1)
                dve.wait_ge(rooted, norms * t + 1)
                dve.reciprocal(st[:, t, 15:16], st[:, t, 14:15])
                dve.drain()
                dve.tensor_scalar(r, r, st[:, t, 12:13], st[:, t, 15:16], ALU.subtract, ALU.mult)
                dve.drain()
                dve.tensor_tensor(r, r, k.rows[:, 0, :], ALU.mult)
                dve.drain()
                mm = dve.tensor_tensor(X[:, t, :], r, k.rows[:, 1, :], ALU.add)
                if mode == "ln":
                    mm.then_inc(normed, 1)
                dve.drain()
            if mode != "ln":
                g = k.rows[:, 2 if mode == "ln+rms" else 0, :]
                if t >= nh:
                    dve.wait_ge(turned, 2 * (t - nh + 1))
                h = hrow[:, t % nh, :]
                dve.tensor_tensor_reduce(h, X[:, t, :], X[:, t, :], 1.0 / D, 0.0, ALU.mult, ALU.add,
                                         st[:, t, 13:14]).then_inc(varied, 1)
                dve.wait_ge(rooted, norms * t + norms)
                dve.reciprocal(st[:, t, 15:16], st[:, t, 14:15])
                dve.drain()
                dve.scalar_tensor_tensor(h, X[:, t, :], st[:, t, 15:16], g, ALU.mult, ALU.mult)\
                   .then_inc(normed, 1)
    tail.turn, tail.scalar, tail.vector, tail.gpsimd = turn, scalar, vector, gpsimd
    tail.turn_banks = (4, 5)
    tail.normed, tail.hrow, tail.turned = normed, hrow, turned
    k.xt_ready = (xt_out, 2 * NT)
    k.x_ready = (normed, NT)
    k.tail = tail
    return tail


def ffn_stage(k, layer, slabs_up, slabs_down, gains, mode):
    A, W, PS = k.A, k.W, k.PS
    name = f"ffn{layer}"
    hT = W[:, 0:FT * S].rearrange("p (c n) -> p c n", c=FT)
    conv = W[:, 11264:13312].rearrange("p (b q n) -> p b q n", b=2, q=2)
    silu = W[:, 13312:13824]
    taps = k.taps
    xt_ready = k.xt_ready
    up, seeded, shifted = k.sem(name + "_up"), k.sem(name + "_seeded"), k.sem(name + "_shifted")
    gated, silued = k.sem(name + "_gated"), k.sem(name + "_silued")
    tail = norm_tail(k, name, gains, mode)
    tail.turn_banks = (0, 1)

    def sync(sp):
        w = A["w_up"][layer]
        with sp.Fori(0, 2) as turn:
            for i in range(UD):
                load_slab(k, sp, slabs_up[i],
                          [columns(w, (turn * UD + i) * P + q * FF, P) for q in range(2)], turn)
        w = A["w_down"][layer]
        for i in range(UD):
            load_slab(k, sp, slabs_down[i], [columns(w, 0, D, 2 * i, 2)])

    def tensor(pe):
        wait_for(pe, xt_ready)
        with pe.Fori(0, 2) as turn:
            for i in range(UD):
                slot = slabs_up[i][0]
                slab_ready(k, pe, slabs_up[i], turn)
                w = k.ring[:, slot, :].rearrange("p (k q n) -> p k q n", k=KC, q=2)
                b = (i % 2) * 2
                pe.wait_ge(shifted, turn * UD + max(i - 1, 0) + 1)
                for q in range(2):
                    for c in range(KC):
                        mm = pe.matmul(PS[:, b + q, :], w[:, c, q, :], k.XT[:, c, :],
                                       start=(c == 0), stop=(c == KC - 1))
                    if q == 0:
                        mm.then_inc(up, 1)
                mm.then_inc(k.freed[slot], 1)
        pe.wait_ge(shifted, FT + 1)
        for i in range(UD):
            slot = slabs_down[i][0]
            slab_ready(k, pe, slabs_down[i])
            w = k.ring[:, slot, :].rearrange("p (k n) -> p k n", k=2)
            for t in range(NT):
                for c in range(2):
                    if t == 0:
                        pe.wait_ge(gated, 2 * i + c + 2)
                    for half in range(2):
                        mm = pe.matmul(PS[:, 2 * t + half, :], hT[:, 2 * i + c, t * P:(t + 1) * P],
                                       w[:, c, 512 * half:512 * half + 512],
                                       start=(i == 0 and c == 0), stop=(i == UD - 1 and c == 1))
                if i == UD - 1:
                    mm.then_inc(tail.product, 1)
            if i < UD - 1:
                mm.then_inc(k.freed[slot], 1)
        pe.drain().then_inc(k.freed[slabs_down[UD - 1][0]], 1)
        pe.wait_ge(tail.summed, 1)
        for t in range(NT):
            tail.turn(pe, t)

    def scalar(act):
        act.wait_ge(k.taps_in, 1)
        with act.Fori(0, 2) as turn:
            for i in range(UD):
                b = (i % 2) * 2
                n = turn * UD + i
                for q in range(2):
                    if q == 0:
                        act.wait_ge(up, n + 1)
                    else:
                        act.wait_ge(k.freed[slabs_up[i][0]], slabs_up[i][1] + turn + 1)
                    act.wait_ge(gated, turn * UD + max(i - 1, 0) + 1)
                    act.activation(conv[:, i % 2, q, :], PS[:, b + q, :], ACT.Identity,
                                   bias=tap_at(k, layer, 3, q, turn, i), scale=tap_at(k, layer, 2, q, turn, i))\
                       .then_inc(seeded, 1)
                act.wait_ge(shifted, n + 2)
                act.wait_ge(gated, n + 1)
                act.activation(silu, conv[:, i % 2, 1, :], ACT.Silu).then_inc(silued, 1)
        tail.scalar(act)

    def vector(dve):
        dve.sem_inc(shifted, 1)
        dve.sem_inc(gated, 1)
        dve.wait_ge(k.taps_in, 1)
        with dve.Fori(0, 2) as turn:
            for i in range(UD):
                b = (i % 2) * 2
                n = turn * UD + i
                for q in range(2):
                    dve.wait_ge(seeded, n * 2 + q + 1)
                    y = conv[:, i % 2, q, :]
                    dve.scalar_tensor_tensor(y[:, 1:S], PS[:, b + q, 0:S - 1], tap_at(k, layer, 1, q, turn, i),
                                             y[:, 1:S], ALU.mult, ALU.add)
                    dve.drain()
                    mm = dve.scalar_tensor_tensor(y[:, 2:S], PS[:, b + q, 0:S - 2], tap_at(k, layer, 0, q, turn, i),
                                                  y[:, 2:S], ALU.mult, ALU.add)
                mm.then_inc(shifted, 1)
                dve.drain()
                dve.wait_ge(silued, n + 1)
                dve.tensor_tensor(hT_at(k, turn, i), conv[:, i % 2, 0, :], silu, ALU.mult).then_inc(gated, 1)
        tail.vector(dve)

    return dict(sync=sync, tensor=tensor, scalar=scalar, vector=vector, gpsimd=tail.gpsimd)


def hT_at(k, turn, i):
    return k.W[:, 0:FT * S].rearrange("p (u n) -> p u n", u=2)[:, turn, i * S:(i + 1) * S]


def tap_at(k, layer, tap, q, turn, i):
    t = k.taps[:, layer, tap, :].rearrange("p (q n) -> p q n", q=2)[:, q, :]
    return t[:, turn * UD + i:turn * UD + i + 1] if isinstance(turn, int) else t[:, bass.ds(turn * UD + i, 1)]


def bias_stage(k):
    A, W, PS = k.A, k.W, k.PS
    onehot = W[0:32, 13824:14464]
    table = W[0:32, 14464:14472]
    lam = k.lam
    vec_in, table_in, looked, masked = (k.sem("lam_vectors"), k.sem("bias_table"), k.sem("bias_looked"),
                                        k.sem("bias_masked"))
    dots, exps, k.lam_ready = k.sem("lam_dots"), k.sem("lam_exps"), k.sem("lam_ready")
    k.bias_out = k.sem("bias_rows_out")
    k.bias_rows = k.dram("bias_rows", (8, 640))
    k.bias_skew = k.dram("bias_skewed", (8, P * 641))
    skewed = k.sem("bias_skewed")
    vec = k.lam_vec[:].rearrange("p (v n) -> p v n", v=4)

    def gpsimd(pool):
        for i, n in enumerate(["lam_q1", "lam_k1", "lam_q2", "lam_k2"]):
            pool.dma_start(vec[:, i, :], row_piece(A[n], DH)).then_inc(vec_in, 16)
        pool.dma_start(onehot, A["c_onehot"]).then_inc(table_in, 16)
        pool.dma_start(table, A["rel_bias"]).then_inc(table_in, 16)

    def tensor(pe):
        pe.wait_ge(table_in, 32)
        for half in range(2):
            mm = pe.matmul(PS[0:8, half, 0:320], table, onehot[:, 320 * half:320 * half + 320],
                           start=True, stop=True)
        mm.then_inc(looked, 1)

    def scalar(act):
        act.wait_ge(dots, 1)
        act.activation(lam[:, 2:4], lam[:, 0:2], ACT.Exp).then_inc(exps, 1)

    def vector(dve):
        dve.wait_ge(vec_in, 64)
        for i in range(2):
            mm = dve.tensor_tensor_reduce(vec[:, 2 * i, :], vec[:, 2 * i, :], vec[:, 2 * i + 1, :], 1.0, 0.0,
                                          ALU.mult, ALU.add, lam[:, i:i + 1])
        mm.then_inc(dots, 1)
        dve.wait_ge(looked, 1)
        for half in range(2):
            dve.tensor_copy(k.bias_line[:, 320 * half:320 * half + 320], PS[0:8, half, 0:320])
        dve.drain()
        dve.memset(k.bias_line[:, 512:640], NEG).then_inc(masked, 1)
        dve.wait_ge(exps, 1)
        dve.tensor_tensor(lam[:, 4:5], lam[:, 3:4], lam[:, 2:3], ALU.subtract)
        dve.drain()
        dve.tensor_scalar(lam[:, 5:6], lam[:, 4:5], -LAM_INIT, None, ALU.add).then_inc(k.lam_ready, 1)

    def sync(sp):
        sp.wait_ge(masked, 1)
        sp.dma_start(k.bias_rows, k.bias_line).then_inc(k.bias_out, 16)
        sp.wait_ge(k.bias_out, 16)
        for h in range(8):
            to = bass.AP(tensor=k.bias_skew.tensor, offset=h * P * 641, ap=[[641, P], [1, 640]])
            src = bass.AP(tensor=k.bias_rows.tensor, offset=h * 640, ap=[[0, P], [1, 640]])
            sp.dma_start(to, src).then_inc(skewed, 16)
        sp.wait_ge(skewed, 128)

    return dict(gpsimd=gpsimd, tensor=tensor, scalar=scalar, vector=vector, late_sync=sync)


def diff_stage(k):
    A, W, PS = k.A, k.W, k.PS
    YT = W[:, 0:4096].rearrange("p (c n) -> p c n", c=KC)
    bias = W[:, 4096:8192].rearrange("p (h n) -> p h n", h=8)
    q = [W[:, 8192 + 1536 * b:8704 + 1536 * b] for b in range(2)]
    kk = [W[:, 8704 + 1536 * b:9216 + 1536 * b] for b in range(2)]
    v = [W[:, 9216 + 1536 * b:9728 + 1536 * b].rearrange("p (t n) -> p t n", t=NT) for b in range(2)]
    s = W[:, 11264:13312].rearrange("p (b r n) -> p b r n", b=2, r=2)
    w = W[:, 13312:14336].rearrange("p (b n) -> p b n", b=2)
    wT = W[:, 14336:15360].rearrange("p (b n) -> p b n", b=2)
    on = W[:, 15360:15872].rearrange("p (t n) -> p t n", t=NT)
    gain = W[:, 15872:16000]
    junk = W[:, 16000:16128]
    col = k.cols
    bias_in, gain_in, gain_set = k.sem("bias_tiles"), k.sem("subln_in"), k.sem("subln_scaled")
    projected, kept = k.sem("df_projected"), k.sem("df_kept")
    scored, biased, negated, exped = k.sem("df_scored"), k.sem("df_biased"), k.sem("df_negated"), k.sem("df_exped")
    mixed, w_turned, w_out = k.sem("df_mixed"), k.sem("df_w_turned"), k.sem("df_w_out")
    valued, squared, rooted = k.sem("df_valued"), k.sem("df_squared"), k.sem("df_rooted")
    normed, y_turned, y_out = k.sem("df_normed"), k.sem("df_y_turned"), k.sem("df_y_out")
    k.df_y_out = y_out
    xt_ready, x_ready = k.xt_ready, k.x_ready
    HD = 8

    def sync(sp):
        for h in range(HD):
            src = bass.AP(tensor=k.bias_skew.tensor, offset=h * P * 641 + 127, ap=[[640, P], [1, 512]])
            sp.dma_start(bias[:, h, :], src).then_inc(bias_in, 16)
        wi = A["w_in_odd"][0]
        for h in range(HD):
            for half in range(2):
                load_slab(k, sp, k.odd_slabs[h][half],
                          [columns(wi, h * P + D * part, P, 4 * half, 4) for part in range(3)])

    def gpsimd(pool):
        wait_for(pool, x_ready)
        pool.dma_start(gain, row_piece(A["subln_g"], P)).then_inc(gain_in, 16)

    def tensor(pe):
        def project(h, part):
            n = 3 * h + part
            if n >= 2:
                pe.wait_ge(kept, n - 1)
            bank = 6 + n % 2
            slabs = k.odd_slabs[h]
            for half in range(2):
                if part == 0:
                    slab_ready(k, pe, slabs[half])
            view = [k.ring[:, sl[0], 0:1536].rearrange("p (k q n) -> p k q n", k=4, q=3) for sl in slabs]
            if part < 2:
                for c in range(KC):
                    mm = pe.matmul(PS[:, bank, :], view[c // 4][:, c % 4, part, :], k.XT[:, c, :],
                                   start=(c == 0), stop=(c == KC - 1))
            else:
                for t in range(NT):
                    for c in range(KC):
                        mm = pe.matmul(PS[:, bank, t * P:(t + 1) * P], k.XT[:, c, t * P:(t + 1) * P],
                                       view[c // 4][:, c % 4, 2, :], start=(c == 0), stop=(c == KC - 1))
                        if t == NT - 1 and c == 3:
                            mm.then_inc(k.freed[slabs[0][0]], 1)
            mm.then_inc(projected, 1)
            if part == 2:
                pe.drain().then_inc(k.freed[slabs[1][0]], 1)

        def score(h, i):
            n = 4 * h + i
            b = n % 2
            if n >= 2:
                pe.wait_ge(biased, n - 1)
            for r in range(2):
                rows = slice(64 * r, 64 * r + 64)
                mm = pe.matmul(PS[:, 2 * b + r, 0:(i + 1) * P], q[h % 2][rows, i * P:(i + 1) * P],
                               kk[h % 2][rows, 0:(i + 1) * P], start=True, stop=True)
            mm.then_inc(scored, 1)

        def turn_w(h, i):
            n = 4 * h + i
            pe.wait_ge(mixed, n + 1)
            if n > 0:
                pe.wait_ge(w_out, n)
            pe.wait_ge(y_out, h)
            for j in range(i + 1):
                mm = pe.transpose(PS[:, 4, j * P:(j + 1) * P], w[:, n % 2, j * P:(j + 1) * P], k.ident)
            mm.then_inc(w_turned, 1)

        def value(h, i):
            n = 4 * h + i
            pe.wait_ge(w_out, n + 1)
            pe.wait_ge(kept, 3 * h + 3)
            if i == 0 and h > 0:
                pe.wait_ge(normed, h)
            for j in range(i + 1):
                mm = pe.matmul(PS[:, 5, i * P:(i + 1) * P], wT[:, n % 2, j * P:(j + 1) * P],
                               v[h % 2][:, j, :], start=(j == 0), stop=(j == i))
            mm.then_inc(valued, 1)

        def turn_y(h):
            pe.wait_ge(normed, h + 1)
            pe.wait_ge(w_out, 4 * h + 4)
            for t in range(NT):
                mm = pe.transpose(PS[:, 4, t * P:(t + 1) * P], on[:, t, :], k.ident)
            mm.then_inc(y_turned, 1)

        wait_for(pe, xt_ready)
        for part in range(3):
            project(0, part)
        for h in range(HD):
            pe.wait_ge(kept, 3 * h + 2)
            more = [lambda part=part: project(h + 1, part) for part in range(3)] if h + 1 < HD else \
                [lambda: None] * 3
            score(h, 0)
            score(h, 1)
            if h > 0:
                turn_y(h - 1)
            more[0]()
            turn_w(h, 0)
            score(h, 2)
            value(h, 0)
            turn_w(h, 1)
            score(h, 3)
            more[1]()
            value(h, 1)
            turn_w(h, 2)
            more[2]()
            value(h, 2)
            turn_w(h, 3)
            value(h, 3)
        turn_y(HD - 1)

    def scalar(act):
        def keep(h, part):
            act.wait_ge(projected, 3 * h + part + 1)
            src = PS[:, 6 + (3 * h + part) % 2, :]
            if part == 0:
                act.mul(q[h % 2], src, DH ** -0.5).then_inc(kept, 1)
            elif part == 1:
                act.copy(kk[h % 2], src).then_inc(kept, 1)
            else:
                act.copy(v[h % 2], src.rearrange("p (t n) -> p t n", t=NT)).then_inc(kept, 1)

        def rows(h, i):
            n = 4 * h + i
            L = (i + 1) * P
            act.wait_ge(negated, n + 1)
            if n >= 2:
                act.wait_ge(mixed, n - 1)
            for r in range(2):
                mm = act.activation(s[:, n % 2, r, 0:L], s[:, n % 2, r, 0:L], ACT.Exp,
                                    bias=col[:, n % 2, 2 + r:3 + r], accum_out=col[:, n % 2, 4 + r:5 + r])
            mm.then_inc(exped, 1)

        def leave_w(h, i):
            n = 4 * h + i
            act.wait_ge(w_turned, n + 1)
            if n >= 2:
                act.wait_ge(valued, n - 1)
            act.copy(wT[:, n % 2, 0:(i + 1) * P], PS[:, 4, 0:(i + 1) * P]).then_inc(w_out, 1)

        def leave_y(h):
            act.wait_ge(y_turned, h + 1)
            act.copy(YT[:, h, :], PS[:, 4, :]).then_inc(y_out, 1)

        for part in range(3):
            keep(0, part)
        for h in range(HD):
            more = [lambda part=part: keep(h + 1, part) for part in range(3)] if h + 1 < HD else \
                [lambda: None] * 3
            if h > 0:
                act.wait_ge(squared, h)
                act.activation(k.stat[:, :, 9], k.stat[:, :, 8], ACT.Sqrt, bias=k.eps_ln).then_inc(rooted, 1)
            rows(h, 0)
            rows(h, 1)
            if h > 0:
                leave_y(h - 1)
            leave_w(h, 0)
            more[0]()
            rows(h, 2)
            leave_w(h, 1)
            rows(h, 3)
            more[1]()
            leave_w(h, 2)
            leave_w(h, 3)
            more[2]()
        act.wait_ge(squared, HD)
        act.activation(k.stat[:, :, 9], k.stat[:, :, 8], ACT.Sqrt, bias=k.eps_ln).then_inc(rooted, 1)
        leave_y(HD - 1)

    def vector(dve):
        def add_bias(h, i):
            n = 4 * h + i
            L = (i + 1) * P
            b = n % 2
            dve.wait_ge(scored, n + 1)
            for r in range(2):
                dve.tensor_tensor_reduce(s[:, b, r, 0:L], PS[:, 2 * b + r, 0:L], bias[:, h, 512 - L:512],
                                         1.0, -3e38, ALU.add, ALU.max, col[:, b, r:r + 1])
            dve.drain().then_inc(biased, 1)
            dve.tensor_scalar(col[:, b, 2:4], col[:, b, 0:2], -1.0, None, ALU.mult).then_inc(negated, 1)

        def mix(h, i):
            n = 4 * h + i
            L = (i + 1) * P
            b = n % 2
            dve.wait_ge(exped, n + 1)
            dve.reciprocal(col[:, b, 6:8], col[:, b, 4:6])
            dve.drain()
            if n >= 2:
                dve.wait_ge(w_turned, n - 1)
            dve.tensor_scalar(col[:, b, 8:9], col[:, b, 7:8], k.lam[:, 5:6], None, ALU.mult)
            dve.tensor_scalar(w[:, b, 0:L], s[:, b, 0, 0:L], col[:, b, 6:7], None, ALU.mult)
            dve.drain()
            dve.scalar_tensor_tensor(w[:, b, 0:L], s[:, b, 1, 0:L], col[:, b, 8:9], w[:, b, 0:L],
                                     ALU.mult, ALU.add).then_inc(mixed, 1)

        def squares(h):
            dve.wait_ge(valued, 4 * h + 4)
            for t in range(NT):
                dve.tensor_copy(on[:, t, :], PS[:, 5, t * P:(t + 1) * P])
            dve.drain()
            for t in range(NT):
                mm = dve.tensor_tensor_reduce(junk, on[:, t, :], on[:, t, :], 1.0 / P, 0.0,
                                              ALU.mult, ALU.add, k.stat[:, t, 8:9])
                dve.drain()
            dve.drain().then_inc(squared, 1)

        def norm(h):
            dve.wait_ge(rooted, h + 1)
            dve.reciprocal(k.stat[:, :, 10], k.stat[:, :, 9])
            dve.drain()
            for t in range(NT):
                mm = dve.scalar_tensor_tensor(on[:, t, :], on[:, t, :], k.stat[:, t, 10:11], gain,
                                              ALU.mult, ALU.mult)
            mm.then_inc(normed, 1)

        dve.wait_ge(bias_in, 16 * HD)
        dve.wait_ge(gain_in, 16)
        dve.tensor_scalar(gain, gain, 1.0 - LAM_INIT, None, ALU.mult)
        for h in range(HD):
            add_bias(h, 0)
            add_bias(h, 1)
            if h > 0:
                norm(h - 1)
            mix(h, 0)
            add_bias(h, 2)
            mix(h, 1)
            add_bias(h, 3)
            mix(h, 2)
            mix(h, 3)
            if h > 0:
                dve.wait_ge(y_turned, h)
            squares(h)
        norm(HD - 1)

    return dict(sync=sync, gpsimd=gpsimd, tensor=tensor, scalar=scalar, vector=vector)


def column_stage(k):
    A, W, PS = k.A, k.W, k.PS
    rows = W[:, 12288:12544].rearrange("p (a n) -> p a n", a=2)
    rows_in, turned = k.sem("col_rows"), k.sem("cols_turned")
    k.cols_in = k.sem("cols_in")

    def gpsimd(pool):
        for at, half, src in [(0, 0, A["conv_w_2"][0].rearrange("t (n p) -> (t n) p", p=P)),
                              (4 * CW, 0, A["conv_b_2"][0].rearrange("(n p) -> n p", p=P)),
                              (0, 1, A["qk_conv_w_2"][0].rearrange("t (n p) -> (t n) p", p=P)),
                              (32, 1, A["qk_conv_b_2"][0].rearrange("(n p) -> n p", p=P)),
                              (40, 1, A["b_in_2"][0, 0:2048].rearrange("(n p) -> n p", p=P))]:
            pool.dma_start(rows[at:at + src.shape[0], half, :], src).then_inc(rows_in, 16)

    def tensor(pe):
        pe.wait_ge(rows_in, 80)
        pe.transpose(PS[:, 6, 0:128], rows[:, 0, :], k.ident)
        pe.transpose(PS[:, 6, 128:184], rows[0:56, 1, :], k.ident[0:56, 0:56]).then_inc(turned, 1)

    def scalar(act):
        act.wait_ge(turned, 1)
        act.copy(k.chan[:], PS[:, 6, 0:184]).then_inc(k.cols_in, 1)

    return dict(gpsimd=gpsimd, tensor=tensor, scalar=scalar)


def hybrid_stage(k):
    A, W, PS = k.A, k.W, k.PS
    YT = W[:, 0:4096].rearrange("p (c n) -> p c n", c=KC)
    PAD = CW - 1
    u = W[:, 4096:6272].rearrange("p (c n) -> p c n", c=4)
    acc = W[:, 6272:8320].rearrange("p (c n) -> p c n", c=4)
    pre = W[:, 8320:9352].rearrange("p (q n) -> p q n", q=2)
    qk = W[:, 9352:10376].rearrange("p (q n) -> p q n", q=2)
    v = W[:, 10376:11432].rearrange("p (b t n) -> p b t n", b=2, t=NT)
    og = W[:, 11432:12456].rearrange("p (b t n) -> p b t n", b=2, t=NT)
    wt = W[:, 12456:13736]
    on = W[:, 13736:14248].rearrange("p (t n) -> p t n", t=NT)
    fl, t1, t2 = W[0:4, 12456:12968], W[0:4, 12968:13480], W[0:4, 13736:14248]
    negM = W[0:4, 14248:14760]
    sel = W[0:4, 14760:15272]
    arow = W[0:4, 15272:15784]
    acol = W[:, 15784:15800].rearrange("p (t h) -> p t h", t=NT)
    emcol = W[:, 15800:15816].rearrange("p (t h) -> p t h", t=NT)
    gw = W[:, 15816:15880].rearrange("p (k n) -> p k n", k=KC)
    gb = W[0:4, 15880:15882]
    sig = [W[:, 10376:10888], W[:, 11432:11944]]
    unorm = [W[:, 8320:8832], W[:, 8832:9344]]
    wide = k.chan[:, 0:124].rearrange("p (t n) -> p t n", n=4)
    wide_b = k.chan[:, 124:128]
    qk_w = k.chan[:, 128:160].rearrange("p (t n) -> p t n", n=8)
    qk_b, b_in = k.chan[:, 160:168], k.chan[:, 168:184]
    place = [(0, 0), (1, 0), (2, 0), (1, 384)]
    COL = [0, 512, 1024, 896]
    st = k.stat
    names = ("gate_w_in rows_in padded pair_done sig_done u_done g_done g_kept g_kept2 g_exp g_abs g_row g_em "
             "g_turned g_cols projected kept vo_raw og_done seeded convd qk_ready scored bcast exped cut "
             "weighted valued varied rooted normed y_turned y_out acc_done c_turned c_varied c_rooted "
             "c_normed c_silu c_back c_out").split()
    s = Namespace()
    (s.gate_w_in, s.rows_in, s.padded, s.pair_done, s.sig_done, s.u_done, s.g_done, s.g_kept, s.g_kept2,
     s.g_exp, s.g_abs, s.g_row, s.g_em, s.g_turned, s.g_cols, s.projected, s.kept, s.vo_raw, s.og_done,
     s.seeded, s.convd, s.qk_ready, s.scored, s.bcast, s.exped, s.cut, s.weighted, s.valued, s.varied,
     s.rooted, s.normed, s.y_turned, s.y_out, s.acc_done, s.c_turned, s.c_varied, s.c_rooted, s.c_normed,
     s.c_silu, s.c_back, s.c_out) = (k.sem("hy_" + n) for n in names)
    k.hy_y_out, k.hy_c_out = s.y_out, s.c_out
    xt_ready, x_ready = k.xt_ready, k.x_ready
    before = k.rows_used
    k.rows_used = (s.c_normed, 4)
    k.rows_used2 = (s.normed, 4)
    HL = 4

    def sync(sp):
        w = A["w_in_2"][0]
        for c in range(4):
            load_slab(k, sp, k.cv_slabs[c], [columns(w, c * P + 512 * q, P) for q in range(2)])
            if c == 0:
                sp.dma_start(gw, columns(w, 3072, 8)).then_inc(s.gate_w_in, 16)
                for i in range(2):
                    sp.dma_start(gb[:, i:i + 1], A["b_in_2"][0, 3072 + 4 * i:3076 + 4 * i]
                                 .rearrange("(p o) -> p o", o=1)).then_inc(s.gate_w_in, 16)
                sp.dma_start(sel, A["c_sel"]).then_inc(s.gate_w_in, 16)
        for h in range(HL):
            for half in range(2):
                load_slab(k, sp, k.ml_slabs[h][half],
                          [columns(w, 1024 + h * P + 512 * part, P, 4 * half, 4) for part in range(4)])

    def gpsimd(pool):
        wait_for(pool, before)
        pool.dma_start(k.rows[:, 0, :], row_piece(A["b_in_2"][0, 2048:3072], D)).then_inc(s.rows_in, 16)
        pool.dma_start(k.rows[:, 1, 0:512], row_piece(A["conv_ln_g_2"][0], 512)).then_inc(s.rows_in, 16)
        pool.dma_start(k.rows[:, 1, 512:1024], row_piece(A["conv_ln_b_2"][0], 512)).then_inc(s.rows_in, 16)
        pool.dma_start(k.rows[:, 2, 0:512], row_piece(A["mlstm_norm_g_2"][0], 512)).then_inc(s.rows_in, 16)
        for h in range(HL):
            pool.wait_ge(s.exped, h + 1)
            for j in range(NT):
                d = wt[:, COL[j]:COL[j] + P]
                mm = pool.affine_select(out=d, in_=d, pattern=[[1, P]], compare_op=ALU.is_ge,
                                        fill=0.0, base=0, channel_multiplier=-1)
            mm.then_inc(s.cut, 1)

    def tensor(pe):
        wait_for(pe, xt_ready)
        pe.wait_ge(s.gate_w_in, 64)
        for i in range(2):
            for c in range(KC):
                mm = pe.matmul(PS[0:4, 2 + i, :], gw[:, c, 4 * i:4 * i + 4], k.XT[:, c, :],
                               start=(c == 0), stop=(c == KC - 1))
        mm.then_inc(s.g_done, 1)
        for c in range(4):
            slab_ready(k, pe, k.cv_slabs[c])
            slot = k.cv_slabs[c][0]
            w = k.ring[:, slot, :].rearrange("p (k q n) -> p k q n", k=KC, q=2)
            if c > 1:
                pe.wait_ge(s.u_done, c - 1)
            for q in range(2):
                for kc in range(KC):
                    mm = pe.matmul(PS[:, 4 + 2 * (c % 2) + q, :], w[:, kc, q, :], k.XT[:, kc, :],
                                   start=(kc == 0), stop=(kc == KC - 1))
            mm.then_inc(s.pair_done, 1)
            pe.drain().then_inc(k.freed[slot], 1)

        def views(h):
            return [k.ring[:, sl[0], :].rearrange("p (k n) -> p k n", k=4) for sl in k.ml_slabs[h]]

        def project_qk(h):
            w = views(h)
            for part in range(2):
                slab_ready(k, pe, k.ml_slabs[h][part])
            if h == 0:
                pe.wait_ge(s.u_done, 4)
            for part in range(2):
                if h > 0:
                    pe.wait_ge(s.kept, 2 * (h - 1) + part + 1)
                for c in range(KC):
                    mm = pe.matmul(PS[:, 6 + part, :], w[c // 4][:, c % 4, part * P:(part + 1) * P],
                                   k.XT[:, c, :], start=(c == 0), stop=(c == KC - 1))
                mm.then_inc(s.projected, 1)

        def project_vo(h):
            w = views(h)
            for t in range(NT):
                if h > 0:
                    pe.wait_ge(s.vo_raw, 2 * (h - 1) + t // 2 + 1)
                for c in range(KC):
                    mm = pe.matmul(PS[:, 4 + t // 2, 256 * (t % 2):256 * (t % 2) + 256],
                                   k.XT[:, c, t * P:(t + 1) * P], w[c // 4][:, c % 4, 256:512],
                                   start=(c == 0), stop=(c == KC - 1))
                    if t == NT - 1 and c == 3:
                        mm.then_inc(k.freed[k.ml_slabs[h][0][0]], 1)
            mm.then_inc(s.projected, 1)
            pe.drain().then_inc(k.freed[k.ml_slabs[h][1][0]], 1)

        project_qk(0)
        project_vo(0)
        pe.wait_ge(s.g_row, 1)
        for i, row in enumerate([arow, t1]):
            for t in range(NT):
                at = 16 * i + 4 * t
                mm = pe.transpose(PS[:, 2, at:at + 4], row[:, t * P:(t + 1) * P], k.ident[0:4, 0:4])
        mm.then_inc(s.g_turned, 1)
        pe.wait_ge(s.g_cols, 1)

        for h in range(HL):
            pe.wait_ge(s.qk_ready, 2 * h + 2)
            if h > 0:
                pe.wait_ge(s.y_out, h)
                pe.wait_ge(s.normed, h)
            pe.matmul(PS[:, 3, :], sel[:, h * P:(h + 1) * P], negM, start=True, stop=True).then_inc(s.bcast, 1)
            for j in range(NT):
                bank, col = place[j]
                n = S - j * P
                mm = pe.matmul(PS[:, bank, col:col + n], qk[:, 1, j * P:(j + 1) * P], qk[:, 0, j * P:S],
                               start=True, stop=True)
            mm.then_inc(s.scored, 1)
            if h + 1 < HL:
                project_qk(h + 1)
            pe.wait_ge(s.weighted, h + 1)
            for i in range(NT):
                for j in range(i + 1):
                    at = COL[j] + (i - j) * P
                    mm = pe.matmul(PS[:, 3 - 3 * (i // 2), 256 * (i % 2):256 * (i % 2) + 129], wt[:, at:at + P],
                                   v[:, h % 2, j, 0:129], start=(j == 0), stop=(j == i))
            mm.then_inc(s.valued, 1)
            if h + 1 < HL:
                project_vo(h + 1)
            pe.wait_ge(s.normed, h + 1)
            for t in range(NT):
                mm = pe.transpose(PS[:, 1, t * P:(t + 1) * P], on[:, t, :], k.ident)
            mm.then_inc(s.y_turned, 1)
        for t in range(NT):
            pe.wait_ge(s.acc_done, 4)
            if t > 1:
                pe.wait_ge(s.c_normed, t - 1)
            for c in range(4):
                mm = pe.transpose(PS[:, 6 + t % 2, c * P:(c + 1) * P], acc[:, c, t * P:(t + 1) * P], k.ident)
            mm.then_inc(s.c_turned, 1)
        for t in range(NT):
            pe.wait_ge(s.c_silu, t + 1)
            if t > 1:
                pe.wait_ge(s.c_out, t - 1)
            if t == 0:
                pe.wait_ge(s.vo_raw, 8)
            for c in range(4):
                mm = pe.transpose(PS[:, 4 + t % 2, c * P:(c + 1) * P], unorm[t % 2][:, c * P:(c + 1) * P], k.ident)
            mm.then_inc(s.c_back, 1)

    def scalar(act):
        def keep(h):
            for part in range(2):
                act.wait_ge(s.projected, 3 * h + part + 1)
                if h > 0:
                    act.wait_ge(s.convd, 2 * (h - 1) + part + 1)
                else:
                    act.wait_ge(s.padded, 1)
                act.activation(pre[:, part, 3:515], PS[:, 6 + part, :], ACT.Identity,
                               bias=b_in[:, 8 + 4 * part + h:9 + 4 * part + h]).then_inc(s.kept, 1)

        def silu_qk(h):
            for part in range(2):
                act.wait_ge(s.convd, 2 * h + part + 1)
                act.activation(qk[:, part, :], qk[:, part, :], ACT.Silu).then_inc(s.qk_ready, 1)

        act.wait_ge(s.g_done, 1)
        act.wait_ge(s.gate_w_in, 64)
        act.activation(arow, PS[0:4, 2, :], ACT.Identity, bias=gb[:, 0:1]).then_inc(s.g_kept, 1)
        act.activation(fl, PS[0:4, 3, :], ACT.Identity, bias=gb[:, 1:2]).then_inc(s.g_kept2, 1)
        act.drain()
        act.activation(t1, fl, ACT.Abs)
        act.drain()
        act.activation(t1, t1, ACT.Exp, scale=-1.0)
        act.drain()
        act.activation(t1, t1, ACT.Ln, bias=1.0).then_inc(s.g_abs, 1)
        for c in range(4):
            act.wait_ge(s.pair_done, c + 1)
            if c > 1:
                act.wait_ge(s.u_done, c - 1)
            act.activation(sig[c % 2], PS[:, 5 + 2 * (c % 2), :], ACT.Sigmoid,
                           bias=b_in[:, 4 + c:5 + c]).then_inc(s.sig_done, 1)
        keep(0)
        act.wait_ge(s.g_em, 1)
        act.activation(t1, t2, ACT.Exp, scale=-1.0).then_inc(s.g_row, 1)
        act.wait_ge(s.g_turned, 1)
        act.copy(W[:, 15784:15816], PS[:, 2, 0:32]).then_inc(s.g_cols, 1)
        act.wait_ge(s.vo_raw, 2)
        act.activation(og[:, 0, :, :], og[:, 0, :, :], ACT.Sigmoid).then_inc(s.og_done, 1)
        silu_qk(0)
        for h in range(HL):
            act.wait_ge(s.bcast, h + 1)
            if h > 0:
                act.wait_ge(s.valued, h)
            for j in range(NT):
                n = S - j * P
                mm = act.activation(wt[:, COL[j]:COL[j] + n], PS[:, 3, j * P:S], ACT.Exp,
                                    bias=acol[:, j, h:h + 1])
            mm.then_inc(s.exped, 1)
            act.wait_ge(s.varied, h + 1)
            act.activation(st[:, :, 14], st[:, :, 7], ACT.Sqrt, bias=k.eps_rms).then_inc(s.rooted, 1)
            if h + 1 < HL:
                keep(h + 1)
                act.wait_ge(s.vo_raw, 2 * h + 4)
                act.activation(og[:, (h + 1) % 2, :, :], og[:, (h + 1) % 2, :, :], ACT.Sigmoid).then_inc(s.og_done, 1)
                silu_qk(h + 1)
            act.wait_ge(s.y_turned, h + 1)
            act.copy(YT[:, 4 + h, :], PS[:, 1, :]).then_inc(s.y_out, 1)

        def root(t):
            act.wait_ge(s.c_varied, t + 1)
            act.activation(st[:, t, 14:15], st[:, t, 7:8], ACT.Sqrt, bias=k.eps_rms).then_inc(s.c_rooted, 1)

        root(0)
        root(1)
        for t in range(NT):
            act.wait_ge(s.c_normed, t + 1)
            act.activation(unorm[t % 2], unorm[t % 2], ACT.Silu).then_inc(s.c_silu, 1)
            act.wait_ge(s.c_back, t + 1)
            act.copy(YT[:, 0:4, t * P:(t + 1) * P],
                     PS[:, 4 + t % 2, :].rearrange("p (c n) -> p c n", c=4)).then_inc(s.c_out, 1)
            if t + 2 < NT:
                root(t + 2)

    def vector(dve):
        def make_u(c):
            dve.wait_ge(s.sig_done, c + 1)
            dve.scalar_tensor_tensor(u[:, c, PAD:PAD + S], PS[:, 4 + 2 * (c % 2), :], b_in[:, c:c + 1],
                                     sig[c % 2], ALU.add, ALU.mult).then_inc(s.u_done, 1)

        def convolve(c):
            dve.drain()
            dve.tensor_scalar(acc[:, c, :], u[:, c, PAD:PAD + S], wide[:, PAD, c:c + 1], wide_b[:, c:c + 1],
                              ALU.mult, ALU.add)
            for tap in range(PAD):
                dve.drain()
                mm = dve.scalar_tensor_tensor(acc[:, c, :], u[:, c, tap:tap + S], wide[:, tap, c:c + 1],
                                              acc[:, c, :], ALU.mult, ALU.add)
            mm.then_inc(s.acc_done, 1)

        def bc(ap):
            return bass.AP(tensor=ap.tensor, offset=ap.offset, ap=[list(ap.ap[0]), [0, 2], list(ap.ap[1])])

        def convolve_qk(h):
            for part in range(2):
                dve.wait_ge(s.kept, 2 * h + part + 1)
                if h > 0:
                    dve.wait_ge(s.scored, h)
                ch = 4 * part + h
                dve.tensor_scalar(qk[:, part, :], pre[:, part, 3:515], qk_w[:, 3, ch:ch + 1],
                                  qk_b[:, ch:ch + 1], ALU.mult, ALU.add)
                for tap in range(3):
                    dve.drain()
                    mm = dve.scalar_tensor_tensor(qk[:, part, :], pre[:, part, tap:tap + S],
                                                  qk_w[:, tap, ch:ch + 1], qk[:, part, :], ALU.mult, ALU.add)
                mm.then_inc(s.convd, 1)

        def keep_vo(h):
            dve.wait_ge(s.projected, 3 * h + 3)
            for half in range(2):
                src = PS[:, 4 + half, :].rearrange("p (t n) -> p t n", t=2)
                dve.tensor_tensor(v[:, h % 2, 2 * half:2 * half + 2, 0:P], src[:, :, 0:P],
                                  bc(k.rows[:, 0, h * P:(h + 1) * P]), ALU.add)
                dve.tensor_tensor(og[:, h % 2, 2 * half:2 * half + 2, :], src[:, :, P:2 * P],
                                  bc(k.rows[:, 0, 512 + h * P:512 + (h + 1) * P]), ALU.add)\
                   .then_inc(s.vo_raw, 1)

        dve.wait_ge(s.rows_in, 64)
        dve.memset(u[:, :, 0:PAD], 0.0)
        dve.memset(pre[:, :, 0:3], 0.0).then_inc(s.padded, 1)
        make_u(0)
        dve.wait_ge(s.g_abs, 1)
        dve.scalar_tensor_tensor(fl, fl, 0.0, t1, ALU.min, ALU.subtract)
        dve.drain()
        dve.tensor_tensor_scan(t2, fl, fl, 0.0, ALU.add, ALU.bypass)
        dve.drain()
        dve.tensor_tensor(arow, arow, t2, ALU.subtract)
        dve.drain()
        dve.tensor_tensor_scan(fl, arow, arow, 0.0, ALU.max, ALU.max)
        dve.drain()
        dve.tensor_scalar(negM, fl, -1.0, None, ALU.mult)
        dve.tensor_tensor(t2, t2, fl, ALU.add)
        dve.drain().then_inc(s.g_em, 1)
        convolve(0)
        make_u(1)
        make_u(2)
        convolve(1)
        make_u(3)
        dve.drain()
        dve.memset(v[:, :, :, P:P + 1], 1.0)
        convolve_qk(0)
        keep_vo(0)
        for h in range(HL):
            dve.wait_ge(s.scored, h + 1)
            dve.wait_ge(s.cut, h + 1)
            zz = PS[:, 0:3, :].rearrange("p b n -> p (b n)")[:, 0:CAUSAL]
            dve.scalar_tensor_tensor(wt, zz, P ** -0.5, wt, ALU.mult, ALU.mult).then_inc(s.weighted, 1)
            if h < 2:
                convolve(2 + h)
            dve.wait_ge(s.valued, h + 1)
            if h > 0:
                dve.wait_ge(s.y_turned, h)
            dve.wait_ge(s.og_done, h + 1)
            for t in range(NT):
                o = PS[:, 3 - 3 * (t // 2), 256 * (t % 2):256 * (t % 2) + 129]
                dve.tensor_copy(st[:, t, 8:9], o[:, P:P + 1])
            dve.drain()
            dve.scalar_tensor_tensor(st[:, :, 8], st[:, :, 8], -1.0, st[:, :, 8], ALU.mult, ALU.max)
            dve.drain()
            dve.tensor_tensor(st[:, :, 8], st[:, :, 8], emcol[:, :, h], ALU.max)
            dve.drain()
            dve.reciprocal(st[:, :, 9], st[:, :, 8])
            dve.drain()
            for t in range(NT):
                o = PS[:, 3 - 3 * (t // 2), 256 * (t % 2):256 * (t % 2) + 128]
                dve.scalar_tensor_tensor(on[:, t, :], o, st[:, t, 9:10], og[:, h % 2, t, :], ALU.mult, ALU.mult)
            dve.drain()
            for t in range(NT):
                dve.bn_stats(st[:, t, 0:6], on[:, t, :])
            dve.drain()
            for t in range(NT):
                mm = dve.bn_aggr(st[:, t, 6:8], st[:, t, 0:6])
            mm.then_inc(s.varied, 1)
            dve.wait_ge(s.rooted, h + 1)
            dve.reciprocal(st[:, :, 15], st[:, :, 14])
            dve.drain()
            for t in range(NT):
                dve.tensor_scalar(on[:, t, :], on[:, t, :], st[:, t, 6:7], st[:, t, 15:16], ALU.subtract, ALU.mult)
            dve.drain()
            for t in range(NT):
                mm = dve.tensor_tensor(on[:, t, :], on[:, t, :], k.rows[:, 2, h * P:(h + 1) * P], ALU.mult)
            mm.then_inc(s.normed, 1)
            if h + 1 < HL:
                convolve_qk(h + 1)
                keep_vo(h + 1)
        for t in range(NT):
            bank = PS[:, 6 + t % 2, :]
            dve.wait_ge(s.c_turned, t + 1)
            dve.bn_stats(st[:, t, 0:6], bank)
            dve.drain()
            dve.bn_aggr(st[:, t, 6:8], st[:, t, 0:6]).then_inc(s.c_varied, 1)
            dve.wait_ge(s.c_rooted, t + 1)
            dve.reciprocal(st[:, t, 15:16], st[:, t, 14:15])
            dve.drain()
            if t > 1:
                dve.wait_ge(s.c_back, t - 1)
            dve.tensor_scalar(unorm[t % 2], bank, st[:, t, 6:7], st[:, t, 15:16], ALU.subtract, ALU.mult)
            dve.drain()
            dve.tensor_tensor(unorm[t % 2], unorm[t % 2], k.rows[:, 1, 0:512], ALU.mult)
            dve.drain()
            dve.tensor_tensor(unorm[t % 2], unorm[t % 2], k.rows[:, 1, 512:1024], ALU.add).then_inc(s.c_normed, 1)

    return dict(sync=sync, gpsimd=gpsimd, tensor=tensor, scalar=scalar, vector=vector)


NB = 42


def along(ap, n):
    return bass.AP(tensor=ap.tensor, offset=ap.offset, ap=[list(x) for x in ap.ap] + [[0, n]])


def across(ap, n):
    return bass.AP(tensor=ap.tensor, offset=ap.offset, ap=[list(ap.ap[0]), [0, n]] + [list(x) for x in ap.ap[1:]])


YB = 40


def clear_stage(k):
    k.y_rows = k.dram("expert_rows", (YB * P, D))
    zeroed, out = k.sem("rows_zeroed"), k.sem("expert_rows_zeroed")
    zero = k.rows[:, 2, :]

    def vector(dve):
        dve.memset(zero, 0.0).then_inc(zeroed, 1)

    def gpsimd(pool):
        pool.wait_ge(zeroed, 1)
        for n in range(8, YB, 8):
            to = k.y_rows[n * P:(n + 8) * P, :].rearrange("(n p) c -> p n c", p=P)
            pool.dma_start(to, across(zero, 8)).then_inc(out, 16)
        pool.wait_ge(out, 16 * (YB // 8 - 1))

    return dict(vector=vector, gpsimd=gpsimd)


def moe_stages(k):
    A, W, PS, X = k.A, k.W, k.PS, k.X
    st = k.stat
    h = W[:, 4096:8192].rearrange("p (t n) -> p t n", t=NT)
    base = [8704]

    def room(n):
        base[0] += n
        return W[:, base[0] - n:base[0]]

    def tiled(n):
        return room(NT * n).rearrange("p (t n) -> p t n", t=NT)

    rw = room(8 * 36).rearrange("p (k n) -> p k n", k=KC)
    rb = room(36)
    iota = room(64)
    e_iota, g_iota, tokf = iota[:, 0:32], iota[:, 32:40], iota[:, 40:44]
    L, work, one1, one2, both, neg, dest = (tiled(n) for n in (36, 32, 32, 32, 32, 32, 32))
    gexp = tiled(4)
    gid = room(32)
    cnt, nblk, ends, first = (room(32) for _ in range(4))
    gmax, gsum, gidx, m1, e1, m2, e2, ex, g1, g2, pg, tmp4 = (room(4) for _ in range(12))
    destf = room(8)
    dest_i = room(8).bitcast(I32)
    tok_i = room(4).bitcast(I32)
    bid = room(NB)
    cmpb = room(NB * 32)
    bef = room(NB + 2)
    be_i = room(NB + 2).bitcast(I32)
    idx = room(NB).bitcast(I32)
    idxcol = room(2).bitcast(I32)
    zeros = room(NB).bitcast(I32)
    assert base[0] <= 16128
    xg = [W[:, 1024 * b:1024 * b + 1024] for b in range(2)]
    xT = [W[:, 2048 + 1024 * b:3072 + 1024 * b].rearrange("p (c n) -> p c n", c=KC) for b in range(2)]
    silu = W[:, 4096:4608]
    mid = [W[:, 4608 + 512 * b:5120 + 512 * b] for b in range(2)]
    midT = [W[:, 5632 + 512 * b:6144 + 512 * b].rearrange("p (c n) -> p c n", c=4) for b in range(2)]
    ys = [W[:, 6656 + 1024 * b:7680 + 1024 * b] for b in range(2)]
    h_rows = k.dram("h_rows", (S, D))
    slot_tok = k.dram("slot_tokens", (NB * P, 1), I32)
    y_rows = k.y_rows
    names = ("h_saved table_in logits ranked gexp ex ready placed zeroed zero_out scattered idx_in col_set "
             "x_in0 x_in1 x_turned x_out silued mid mid_turned mid_out y_done y_kept y_saved y_free "
             "found combined rooted final out_saved0 out_saved1 gain_in found1").split()
    s = Namespace()
    (s.h_saved, s.table_in, s.logits, s.ranked, s.gexp, s.ex, s.ready, s.placed, s.zeroed, s.zero_out,
     s.scattered, s.idx_in, s.col_set, s.x_in0, s.x_in1, s.x_turned, s.x_out, s.silued, s.mid,
     s.mid_turned, s.mid_out, s.y_done, s.y_kept, s.y_saved, s.y_free, s.found, s.combined, s.rooted,
     s.final, s.out_saved0, s.out_saved1, s.gain_in, s.found1) = (k.sem("moe_" + n) for n in names)
    x_in = [s.x_in0, s.x_in1]
    found, out_saved = [s.found, s.found1], [s.out_saved0, s.out_saved1]
    normed, product_1 = k.tail.normed, k.tail.product
    xt_ready, rows_before = k.xt_ready, k.rows_used
    slabs = k.moe_slabs
    AX = mybir.AxisListType

    def done(eng, slot, turn):
        eng.wait_ge(k.freed[slot], turn + slabs[slot][1] + 1)

    def pairs(eng):
        eng.wait_ge(s.placed, 1)
        return eng.value_load(be_i[0:1, NB:NB + 1], min_val=4, max_val=20)

    def route_sync(sp):
        sp.wait_ge(product_1, 1)
        sp.dma_start(rw[:, :, 0:4], columns(A["router_group_w_2"][0], 0, 4)).then_inc(s.table_in, 16)
        sp.dma_start(rw[:, :, 4:36], columns(A["router_expert_w_2"][0], 0, 32)).then_inc(s.table_in, 16)
        sp.dma_start(rb[:, 0:4], row_piece(A["router_group_b_2"][0], 4)).then_inc(s.table_in, 16)
        sp.dma_start(rb[:, 4:36], row_piece(A["router_expert_b_2"][0], 32)).then_inc(s.table_in, 16)
        sp.dma_start(iota, A["c_iota"]).then_inc(s.table_in, 16)
        for t in range(NT):
            sp.wait_ge(normed, t + 1)
            sp.dma_start(h_rows[t * P:(t + 1) * P, :], h[:, t, :]).then_inc(s.h_saved, 16)
        sp.wait_ge(s.zeroed, 1)
        sp.dma_start(slot_tok.rearrange("(p n) o -> p (n o)", p=P), zeros).then_inc(s.zero_out, 16)

    def route_tensor(pe):
        pe.wait_ge(*xt_ready)
        pe.wait_ge(s.table_in, 80)
        for t in range(NT):
            for c in range(KC):
                mm = pe.matmul(PS[:, 6, 36 * t:36 * t + 36], k.XT[:, c, t * P:(t + 1) * P], rw[:, c, :],
                               start=(c == 0), stop=(c == KC - 1))
        mm.then_inc(s.logits, 1)
        pe.wait_ge(s.ready, 1)
        for t in range(NT):
            mm = pe.matmul(PS[:, 7, 32 * t:32 * t + 32], k.before, both[:, t, :], start=True, stop=(t == 0))
            for t2 in range(t):
                mm = pe.matmul(PS[:, 7, 32 * t:32 * t + 32], k.negone, neg[:, t2, :],
                               start=False, stop=(t2 == t - 1))
        for t in range(NT):
            mm = pe.matmul(PS[:, 7, 128:160], k.negone, neg[:, t, :], start=(t == 0), stop=(t == NT - 1))
        mm.then_inc(s.ranked, 1)

    def route_scalar(act):
        act.wait_ge(s.gexp, 1)
        act.activation(gexp, gexp, ACT.Exp).then_inc(s.gexp, 1)
        act.wait_ge(s.ex, 1)
        act.activation(ex, ex, ACT.Exp).then_inc(s.ex, 1)

    def route_vector(dve):
        dve.drain()
        dve.memset(zeros, 0).then_inc(s.zeroed, 1)
        dve.wait_ge(s.table_in, 80)
        dve.wait_ge(s.logits, 1)
        dve.tensor_tensor(L, PS[:, 6, 0:144].rearrange("p (t n) -> p t n", t=NT), across(rb, NT), ALU.add)
        dve.tensor_copy(tok_i, tokf)
        dve.tensor_scalar(gid, e_iota, 8.0, None, ALU.is_ge)
        dve.drain()
        for edge in (16.0, 24.0):
            dve.scalar_tensor_tensor(gid, e_iota, edge, gid, ALU.is_ge, ALU.add)
            dve.drain()
        G, E = L[:, :, 0:4], L[:, :, 4:36]
        dve.tensor_reduce(gmax, G, AX.X, ALU.max)
        dve.drain()
        dve.tensor_tensor(gexp, G, along(gmax, 4), ALU.subtract).then_inc(s.gexp, 1)
        w4 = work[:, :, 0:4]
        dve.tensor_tensor(w4, G, along(gmax, 4), ALU.is_equal)
        dve.drain()
        dve.scalar_tensor_tensor(w4, w4, -1000.0, across(g_iota[:, 0:4], NT), ALU.mult, ALU.add)
        dve.drain()
        dve.tensor_reduce(gidx, w4, AX.X, ALU.min)
        dve.drain()
        dve.tensor_scalar(gidx, gidx, 1000.0, None, ALU.add)
        dve.drain()
        dve.tensor_tensor(work, across(gid, NT), along(gidx, 32), ALU.not_equal)
        dve.drain()
        dve.scalar_tensor_tensor(E, work, NEG, E, ALU.mult, ALU.add)
        for m, e, one in ((m1, e1, one1), (m2, e2, one2)):
            dve.drain()
            dve.tensor_reduce(m, E, AX.X, ALU.max)
            dve.drain()
            dve.tensor_tensor(work, E, along(m, 32), ALU.is_equal)
            dve.drain()
            dve.scalar_tensor_tensor(work, work, -1000.0, across(e_iota, NT), ALU.mult, ALU.add)
            dve.drain()
            dve.tensor_reduce(e, work, AX.X, ALU.min)
            dve.drain()
            dve.tensor_scalar(e, e, 1000.0, None, ALU.add)
            dve.drain()
            dve.tensor_tensor(one, across(e_iota, NT), along(e, 32), ALU.is_equal)
            dve.drain()
            dve.scalar_tensor_tensor(E, one, 2 * NEG, E, ALU.mult, ALU.add)
        dve.tensor_tensor(both, one1, one2, ALU.add)
        dve.drain()
        dve.tensor_scalar(neg, both, -1.0, None, ALU.mult).then_inc(s.ready, 1)
        dve.tensor_tensor(ex, m2, m1, ALU.subtract).then_inc(s.ex, 1)
        dve.wait_ge(s.gexp, 2)
        dve.tensor_reduce(gsum, gexp, AX.X, ALU.add)
        dve.wait_ge(s.ex, 2)
        dve.tensor_scalar(tmp4, ex, 1.0, None, ALU.add)
        dve.drain()
        dve.tensor_tensor(tmp4, tmp4, gsum, ALU.mult)
        dve.drain()
        dve.reciprocal(g1, tmp4)
        dve.drain()
        dve.tensor_tensor(g2, g1, ex, ALU.mult)
        dve.wait_ge(s.ranked, 1)
        dve.tensor_copy(cnt, PS[:, 7, 128:160])
        dve.drain()
        dve.tensor_scalar(nblk, cnt, 0.5, None, ALU.is_gt)
        for m in range(1, 4):
            dve.drain()
            dve.scalar_tensor_tensor(nblk, cnt, 128.0 * m + 0.5, nblk, ALU.is_gt, ALU.add)
        dve.drain()
        dve.tensor_tensor_scan(ends, nblk, nblk, 0.0, ALU.add, ALU.bypass)
        dve.drain()
        dve.tensor_tensor(first, ends, nblk, ALU.subtract)
        dve.drain()
        dve.tensor_scalar(first, first, 128.0, None, ALU.mult)
        dve.drain()
        dve.tensor_tensor(dest, PS[:, 7, 0:128].rearrange("p (t n) -> p t n", t=NT), across(first, NT), ALU.add)
        for j, one in ((0, one1), (1, one2)):
            dve.drain()
            dve.tensor_tensor(work, dest, one, ALU.mult)
            dve.drain()
            dve.tensor_reduce(destf[:, 4 * j:4 * j + 4], work, AX.X, ALU.add)
        dve.drain()
        dve.tensor_copy(dest_i, destf).then_inc(s.ready, 1)
        for b in range(NB):
            dve.tensor_scalar(cmpb[:, 32 * b:32 * b + 32], ends, float(b), None, ALU.is_le)
        dve.tensor_scalar(bid[:, 0:20], e_iota[:, 0:20], 2.0, None, ALU.mult)
        dve.drain()
        dve.tensor_reduce(bef[:, 0:NB], cmpb.rearrange("p (b e) -> p b e", e=32), AX.X, ALU.add)
        dve.tensor_scalar(bid[:, 0:20], bid[:, 0:20], ends[:, 31:32], None, ALU.is_lt)
        dve.drain()
        dve.tensor_scalar(bef[:, 0:NB], bef[:, 0:NB], float(NE - 1), None, ALU.min)
        dve.tensor_reduce(bef[:, NB:NB + 1], bid[:, 0:20], AX.X, ALU.add)
        dve.drain()
        dve.tensor_copy(be_i[:, 0:NB + 1], bef[:, 0:NB + 1]).then_inc(s.placed, 1)

    def route_gpsimd(pool):
        pool.dma_start(k.rows[:, 1, :], row_piece(A["final_norm_g_2"], D)).then_inc(s.gain_in, 16)
        pool.wait_ge(s.ready, 2)
        pool.wait_ge(s.zero_out, 16)
        for j in range(2):
            for t in range(NT):
                pool.indirect_dma_start(slot_tok, bass.IndirectOffsetOnAxis(
                    ap=dest_i[:, 4 * j + t:4 * j + t + 1].bitcast(U32), axis=0),
                    tok_i[:, t:t + 1], None).then_inc(s.scattered, 16)
        pool.wait_ge(s.scattered, 128)
        with k.nc.allow_non_contiguous_dma(reason="slot numbers onto partitions"):
            pool.dma_start(idx, slot_tok.rearrange("(n p) o -> p (n o)", p=P)).then_inc(s.idx_in, 16)
        pool.wait_ge(s.idx_in, 16)
        pool.wait_ge(s.h_saved, 64)

    def experts_sync(sp):
        n = pairs(sp)
        wg = A["expert_w_gate_2"][0].rearrange("e (k p) n -> e p k n", p=P)
        wu = A["expert_w_up_2"][0].rearrange("e (k p) n -> e p k n", p=P)
        wd = A["expert_w_down_2"][0].rearrange("e (k p) n -> e p k n", p=P)
        with sp.Fori(0, n) as i:
            for b in range(2):
                e = sp.value_load(be_i[0:1, bass.ds(2 * i + b, 1)], min_val=0, max_val=NE - 1)
                for m, (w, nk) in enumerate(((wg, 4), (wg, 4), (wu, 4), (wu, 4), (wd, 2), (wd, 2))):
                    half = m % 2
                    src = w[bass.ds(e, 1), :, nk * half:nk * half + nk, :].rearrange("e p k n -> (e p) k n")
                    load_slab(k, sp, slabs[6 * b + m], [src], i)

    def experts_gpsimd(pool):
        pool.sem_inc(s.y_free, 1)

        def gather(b, n):
            pool.tensor_copy(idxcol[:, b:b + 1], idx[:, bass.ds(n, 1)] if not isinstance(n, int)
                             else idx[:, n:n + 1])
            pool.drain()
            pool.indirect_dma_start(xg[b], None, h_rows, bass.IndirectOffsetOnAxis(
                ap=idxcol[:, b:b + 1].bitcast(U32), axis=0)).then_inc(x_in[b], 16)

        for b in range(2):
            gather(b, b)
        n = pairs(pool)
        with pool.Fori(0, n) as i:
            for b in range(2):
                pool.wait_ge(s.x_turned, 4 * i + 2 * b + 2)
                pool.wait_ge(x_in[b], 16 * i + 16)
                gather(b, 2 * i + 2 + b)
            for b in range(2):
                pool.wait_ge(s.y_kept, 2 * i + b + 2)
                pool.dma_start(y_rows[bass.ds((2 * i + b) * P, P), :], ys[b]).then_inc(s.y_saved, 16)
            for b in range(2):
                pool.wait_ge(x_in[b], 16 * i + 32)
            pool.wait_ge(s.y_saved, 32 * i + 32)
            pool.sem_inc(s.y_free, 1)

    def experts_tensor(pe):
        n = pairs(pe)
        with pe.Fori(0, n) as i:
            def turn_x(b):
                pe.wait_ge(x_in[b], 16 * i + 16)
                for half in range(2):
                    pe.wait_ge(s.x_out, 4 * i + (2 * b + half if b else 1))
                    if b == 0:
                        pe.wait_ge(s.mid_out, 2 * i + 1)
                    for c in range(4):
                        at = (4 * half + c) * P
                        mm = pe.transpose(PS[:, 6 + half, c * P:(c + 1) * P], xg[b][:, at:at + P], k.ident)
                    mm.then_inc(s.x_turned, 1)

            def product(b, m):
                for half in range(2):
                    slab = slabs[6 * b + 2 * m + half]
                    slab_ready(k, pe, slab, i)
                    pe.wait_ge(s.x_out, 4 * i + 2 * b + half + 2)
                    w = k.ring[:, slab[0], :].rearrange("p (k n) -> p k n", k=4)
                    for c in range(4):
                        mm = pe.matmul(PS[:, 2 * b + m, :], xT[b][:, 4 * half + c, :], w[:, c, :],
                                       start=(half == 0 and c == 0), stop=(half == 1 and c == 3))
                    mm.then_inc(k.freed[slab[0]], 1)

            def turn_mid(b):
                pe.wait_ge(s.mid, 2 * i + b + 2)
                for c in range(4):
                    mm = pe.transpose(PS[:, 6 + b, c * P:(c + 1) * P], mid[b][:, c * P:(c + 1) * P], k.ident)
                mm.then_inc(s.mid_turned, 1)

            def down(b):
                pe.wait_ge(s.mid_out, 2 * i + b + 2)
                if b == 0:
                    pe.wait_ge(s.y_kept, 2 * i + 1)
                for half in range(2):
                    slab = slabs[6 * b + 4 + half]
                    slab_ready(k, pe, slab, i)
                    w = k.ring[:, slab[0], :].rearrange("p (k n) -> p k n", k=2)
                    for c in range(2):
                        for side in range(2):
                            bank = (4 if b == 0 else 2) + side
                            mm = pe.matmul(PS[:, bank, :], midT[b][:, 2 * half + c, :],
                                           w[:, c, 512 * side:512 * side + 512],
                                           start=(half == 0 and c == 0), stop=(half == 1 and c == 1))
                    mm.then_inc(k.freed[slab[0]], 1)

            turn_x(0)
            product(0, 0)
            product(0, 1)
            turn_x(1)
            pe.wait_ge(s.y_kept, 2 * i + 1)
            product(1, 0)
            turn_mid(0)
            product(1, 1)
            down(0)
            turn_mid(1)
            down(1)

    def experts_scalar(act):
        act.sem_inc(s.x_out, 1)
        act.sem_inc(s.mid_out, 1)
        n = pairs(act)
        with act.Fori(0, n) as i:
            def leave_x(b):
                for half in range(2):
                    act.wait_ge(s.x_turned, 4 * i + 2 * b + half + 1)
                    act.copy(xT[b][:, 4 * half:4 * half + 4, :],
                             PS[:, 6 + half, :].rearrange("p (c n) -> p c n", c=4)).then_inc(s.x_out, 1)

            def gate(b):
                done(act, 6 * b + 1, i)
                act.wait_ge(s.mid, 2 * i + b + 1)
                act.activation(silu, PS[:, 2 * b, :], ACT.Silu).then_inc(s.silued, 1)

            def leave_mid(b):
                act.wait_ge(s.mid_turned, 2 * i + b + 1)
                act.copy(midT[b], PS[:, 6 + b, :].rearrange("p (c n) -> p c n", c=4)).then_inc(s.mid_out, 1)

            leave_x(0)
            gate(0)
            leave_x(1)
            gate(1)
            leave_mid(0)
            leave_mid(1)

    def experts_vector(dve):
        dve.sem_inc(s.mid, 1)
        dve.sem_inc(s.y_kept, 1)
        n = pairs(dve)
        with dve.Fori(0, n) as i:
            def multiply(b):
                dve.wait_ge(s.silued, 2 * i + b + 1)
                done(dve, 6 * b + 3, i)
                dve.tensor_tensor(mid[b], PS[:, 2 * b + 1, :], silu, ALU.mult).then_inc(s.mid, 1)

            def keep(b):
                done(dve, 6 * b + 5, i)
                dve.wait_ge(s.y_free, i + 1)
                for side in range(2):
                    mm = dve.tensor_copy(ys[b][:, 512 * side:512 * side + 512],
                                         PS[:, (4 if b == 0 else 2) + side, :])
                mm.then_inc(s.y_kept, 1)

            multiply(0)
            multiply(1)
            keep(0)
            keep(1)

    y1 = [W[:, 2048 * b:2048 * b + 1024] for b in range(2)]
    y2 = [W[:, 2048 * b + 1024:2048 * b + 2048] for b in range(2)]
    o = [W[:, 4096 + 1024 * b:5120 + 1024 * b] for b in range(2)]

    def end_gpsimd(pool):
        for t in range(NT):
            if t > 1:
                pool.wait_ge(s.combined, t - 1)
            for j, y in ((0, y1), (1, y2)):
                pool.indirect_dma_start(y[t % 2], None, y_rows, bass.IndirectOffsetOnAxis(
                    ap=dest_i[:, 4 * j + t:4 * j + t + 1].bitcast(U32), axis=0)).then_inc(found[t % 2], 16)

    def end_vector(dve):
        dve.wait_ge(s.gain_in, 16)
        for t in range(NT):
            dve.wait_ge(found[t % 2], 32 * (t // 2 + 1))
            dve.scalar_tensor_tensor(X[:, t, :], y1[t % 2], g1[:, t:t + 1], X[:, t, :], ALU.mult, ALU.add)
            dve.drain()
            dve.scalar_tensor_tensor(X[:, t, :], y2[t % 2], g2[:, t:t + 1], X[:, t, :], ALU.mult, ALU.add)\
               .then_inc(s.combined, 1)
            dve.drain()
            if t > 1:
                dve.wait_ge(out_saved[t % 2], 16)
            dve.tensor_tensor_reduce(o[t % 2], X[:, t, :], X[:, t, :], 1.0 / D, 0.0, ALU.mult, ALU.add,
                                     st[:, t, 13:14]).then_inc(s.final, 1)
            dve.wait_ge(s.rooted, t + 1)
            dve.reciprocal(st[:, t, 15:16], st[:, t, 14:15])
            dve.drain()
            dve.scalar_tensor_tensor(o[t % 2], X[:, t, :], st[:, t, 15:16], k.rows[:, 1, :],
                                     ALU.mult, ALU.mult).then_inc(s.final, 1)

    def end_scalar(act):
        for t in range(NT):
            act.wait_ge(s.final, 2 * t + 1)
            act.activation(st[:, t, 14:15], st[:, t, 13:14], ACT.Sqrt, bias=k.eps_rms).then_inc(s.rooted, 1)

    def end_sync(sp):
        for t in range(NT):
            sp.wait_ge(s.final, 2 * t + 2)
            sp.dma_start(k.out[0, t * P:(t + 1) * P, :], o[t % 2]).then_inc(out_saved[t % 2], 16)
        for b in range(2):
            sp.wait_ge(out_saved[b], 32)

    yield dict(sync=route_sync, gpsimd=route_gpsimd, tensor=route_tensor, scalar=route_scalar, vector=route_vector)
    yield dict(sync=experts_sync, gpsimd=experts_gpsimd, tensor=experts_tensor, scalar=experts_scalar,
               vector=experts_vector)
    yield dict(sync=end_sync, gpsimd=end_gpsimd, scalar=end_scalar, vector=end_vector)


def taps_stage(k):
    A, W, PS = k.A, k.W, k.PS
    n = 2 * FT
    rows = W[0:n, 11264:12288].rearrange("p (l t n) -> p l t n", l=2, t=4)
    rows_in, turned = k.sem("tap_rows"), k.sem("taps_turned")
    k.taps_in = k.sem("taps_in")

    def gpsimd(pool):
        for layer in range(2):
            for tap in range(4):
                src = A["conv_b"][layer] if tap == 3 else A["conv_w"][layer, tap]
                pool.dma_start(rows[:, layer, tap, :], src.rearrange("(n p) -> n p", p=P))\
                    .then_inc(rows_in, 16)
        pool.wait_ge(rows_in, 128)

    def tensor(pe):
        pe.wait_ge(rows_in, 128)
        for layer in range(2):
            for tap in range(4):
                at = (4 * layer + tap) * n
                mm = pe.transpose(PS[:, 7, at:at + n], rows[:, layer, tap, :], k.ident[0:n, 0:n])
        mm.then_inc(turned, 1)

    def scalar(act):
        act.wait_ge(turned, 1)
        act.copy(k.taps[:].rearrange("p l t n -> p (l t n)"), PS[:, 7, 0:8 * n]).then_inc(k.taps_in, 1)

    return dict(gpsimd=gpsimd, tensor=tensor, scalar=scalar)


def program(nc, A, out, stop=99):
    plan = Plan()
    k = Namespace()
    k.nc, k.A, k.out = nc, A, out
    k.ret_slabs = [plan.take(2, 4) for _ in range(4)]
    k.sb_slabs = [plan.take(2, 3) for _ in range(4)]
    k.even_out_slabs = plan.take(4)
    k.up0 = plan.turn(UD, 2, 2)
    k.down0 = plan.take(UD)
    k.odd_slabs = [plan.take(2, 3) for _ in range(8)]
    k.odd_out_slabs = plan.take(4)
    k.up1 = plan.turn(UD, 2, 2)
    k.down1 = plan.take(UD)
    k.cv_slabs = plan.take(4, 2)
    k.ml_slabs = [plan.take(2, 4) for _ in range(4)]
    k.out2_slabs = plan.take(4)
    k.moe_slabs = plan.turn(RING, 1, 0)
    with ExitStack() as ctx:
        def sb(name, shape, dt=F32):
            return ctx.enter_context(nc.sbuf_tensor(name, shape, dt))

        k.sem = lambda name: ctx.enter_context(nc.semaphore(name))
        k.X = sb("X", [P, NT, D])
        k.XT = sb("XT", [P, KC, S])
        k.ring = sb("ring", [P, RING, SLOT])
        k.rows = sb("rows", [P, 3, D])
        k.small = sb("small", [P, 4 * P])
        k.taps = sb("taps", [P, 2, 4, 2 * FT])
        k.stat = sb("stat", [P, NT, 16])
        k.W = sb("W", [P, 16128])
        k.PS = ctx.enter_context(nc.psum_tensor("PS", [P, 8, 512], F32))
        k.eps_col = sb("eps_col", [P, 2])
        k.eps_ln, k.eps_rms = k.eps_col[:, 0:1], k.eps_col[:, 1:2]
        k.ident, k.negtri, k.negone, k.before = (
            k.small[:, i * P:(i + 1) * P] for i in range(4))
        k.chan = sb("chan", [P, 184])
        k.lam = sb("lam", [P, 8])
        k.cols = sb("cols", [P, 2, 9])
        k.lam_vec = k.W[:, 12544:12800]
        k.bias_line = k.W[0:8, 14472:15112]
        k.landed = [k.sem(f"slab_landed{s}") for s in range(RING)]
        k.freed = [k.sem(f"slab_freed{s}") for s in range(RING)]
        k.rows_used = None
        k.dram = lambda name, shape, dt=F32: nc.dram_tensor(name, shape, dt).ap()

        def start_vector(dve):
            dve.memset(k.eps_col[:, 0:1], LN_EPS).then_inc(k.s_eps, 1)
            dve.memset(k.eps_col[:, 1:2], EPS).then_inc(k.s_eps, 1)

        def start_scalar(act):
            act.wait_ge(k.s_eps, 2)

        def even_block():
            bias = bias_stage(k)
            k.s_eps = k.sem("eps_set")
            yield dict(vector=start_vector, scalar=start_scalar)
            yield entry(k)
            yield taps_stage(k)
            yield column_stage(k)
            yield bias
            yield retention_stage(k)
            yield dict(sync=bias["late_sync"])
            yield stick_stage(k)
            yield clear_stage(k)
            yield mix_out_stage(k, "even", A["w_out_even"][0], k.even_out_slabs,
                                [(k.ret_y_out, 4), (k.sb_y_out, 8)], [A["ln1_g"][0], A["ln1_b"][0]], "ln")
            yield ffn_stage(k, 0, k.up0, k.down0, [A["ln2_g"][0], A["ln2_b"][0]], "ln")

        def odd_block():
            yield diff_stage(k)
            yield mix_out_stage(k, "odd", A["w_out_odd"][0], k.odd_out_slabs, [(k.df_y_out, 8)],
                                [A["ln1_g"][1], A["ln1_b"][1]], "ln")
            if stop != "1":
                yield ffn_stage(k, 1, k.up1, k.down1,
                                [A["ln2_g"][1], A["ln2_b"][1], A["norm_mix_g_2"][0]], "ln+rms")

        def second_block():
            if stop == "1":
                return
            yield hybrid_stage(k)
            yield mix_out_stage(k, "out2", A["w_out_2"][0], k.out2_slabs, [(k.hy_y_out, 4), (k.hy_c_out, 4)],
                                [A["norm_ffn_g_2"][0]], "rms")
            if stop != "2":
                yield from moe_stages(k)

        for phase in (even_block, odd_block, second_block):
            held = []
            k.xt_ready = k.x_ready = k.rows_used = None

            def phase_sem(name):
                held.append(nc.alloc_semaphore(name=name))
                return held[-1]

            k.sem = phase_sem
            stages = list(phase())
            with nc.Block() as block:
                @block.sync
                def _(sp):
                    for stage in stages:
                        if "sync" in stage:
                            stage["sync"](sp)

                @block.gpsimd
                def _(pool):
                    for stage in stages:
                        if "gpsimd" in stage:
                            stage["gpsimd"](pool)

                @block.scalar
                def _(act):
                    for stage in stages:
                        if "scalar" in stage:
                            stage["scalar"](act)

                @block.tensor
                def _(pe):
                    for stage in stages:
                        if "tensor" in stage:
                            stage["tensor"](pe)

                @block.vector
                def _(dve):
                    for stage in stages:
                        if "vector" in stage:
                            stage["vector"](dve)
            nc.clear_and_free_semaphores(held)
            nc.all_engine_barrier()



def kernel(**inputs):
    import concourse.bacc as bacc
    from concourse.bass_utils import run_bass_kernel_spmd

    nc = bacc.Bacc("TRN2", target_bir_lowering=False, num_devices=1)
    arrays, aps = {}, {}
    for name, a in {**{n: np.ascontiguousarray(v) for n, v in inputs.items()}, **shape_constants()}.items():
        arrays[f"in_{name}"] = a
        aps[name] = nc.dram_tensor(f"in_{name}", a.shape, mybir.dt.from_np(a.dtype), kind="ExternalInput").ap()
    out = nc.dram_tensor("out", (1, S, D), F32, kind="ExternalOutput").ap()
    program(nc, aps, out)
    return run_bass_kernel_spmd(nc, [arrays], core_ids=[0]).results[0]["out"]
```

```python
from contextlib import ExitStack
import math

import numpy as np

import concourse.bass as bass
from concourse import mybir

ALU = mybir.AluOpType
ACT = mybir.ActivationFunctionType
F32 = mybir.dt.float32
F32R = mybir.dt.float32r
U32 = mybir.dt.uint32
I32 = mybir.dt.int32

P = 128
S = 512
NT = S // P
D = 1024
KC = D // P
DH = 64
FF = 2816
FT = FF // P
UD = FF // 256
ALPHA = 4.0 ** 0.25
LN_EPS = 1e-5
EPS = 1e-6
CW = 31
NE = 32
DE = 512
LAM_INIT = 0.8 - 0.6 * math.exp(-0.3)
NEG = -1e30

RING = 12
RAW, SPLIT = 4, 3
AHEAD = 3
SLOT = 2048
OFF = [0, 512, 896, 1152]
CAUSAL = 1280


class Namespace:
    pass


class Plan:

    def __init__(self):
        self.at, self.uses, self.dmas = 0, [0] * RING, [0] * RING

    def place(self, s, dmas, times=1):
        out = (s, self.uses[s], self.dmas[s], dmas, 1)
        self.uses[s] += times
        self.dmas[s] += dmas * times
        return out

    def take(self, n, dmas=1):
        out = [self.place((self.at + i) % RING, dmas) for i in range(n)]
        self.at = (self.at + n) % RING
        return out

    def take_raw(self, n, dmas=1):
        out = [self.place((self.at + i) % RAW, dmas) for i in range(n)]
        self.at = (self.at + n) % RAW
        return out

    def turns(self, n, dmas, times):
        per = [len(range(s, n, RAW)) for s in range(RAW)]
        out = [(i % RAW, self.uses[i % RAW] + i // RAW, self.dmas[i % RAW] + dmas * (i // RAW), dmas,
                per[i % RAW]) for i in range(n)]
        for s in range(RAW):
            self.uses[s] += per[s] * times
            self.dmas[s] += per[s] * times * dmas
        self.at = RAW
        return out


def shape_constants():
    pos = np.arange(S, dtype=np.float32)
    inv = (10000.0 ** (-np.arange(0, P, 2, dtype=np.float32) / P)).astype(np.float32)
    ang = (pos[:, None] * inv[None, :]).astype(np.float32)
    cos, sin = np.cos(ang), np.sin(ang)
    c = np.concatenate([cos, cos], 1).reshape(NT, P, P).transpose(1, 0, 2)
    s = np.concatenate([-sin, sin], 1).reshape(NT, P, P).transpose(1, 0, 2)
    rope = np.stack([c, s], 1).reshape(P, 2 * NT * P).astype(np.float32)
    j, i = np.arange(P)[:, None], np.arange(S)[None, :]
    decay = []
    for h in range(4):
        g = math.log(1.0 - 2.0 ** (-5.0 - h))
        decay.append(np.where(i >= j, np.exp(g * np.maximum(i - j, 0)), 0.0) * P ** -0.5)
    decay = np.stack(decay, 1).reshape(P, 4 * S).astype(np.float32)
    a, b = np.arange(P)[:, None], np.arange(P)[None, :]
    small = [np.eye(P), -(a >= b).astype(np.float32), -np.ones((P, P)), (a < b).astype(np.float32)]
    small = np.concatenate(small, 1).astype(np.float32)
    n = np.maximum(511 - np.arange(640), 0)
    nf = np.maximum(n, 1).astype(np.float32)
    large = 16 + (np.log(nf / np.float32(16)) / np.float32(math.log(8.0)) * np.float32(16)).astype(np.int32)
    bucket = np.where(n < 16, n, np.minimum(large, 31))
    onehot = (np.arange(32)[:, None] == bucket[None, :]).astype(np.float32)
    sel = (np.arange(4)[:, None] == (np.arange(512)[None, :] // P)).astype(np.float32)
    iota = np.zeros((P, 64), np.float32)
    iota[:, 0:32] = np.arange(32)[None, :]
    iota[:, 32:40] = np.arange(8)[None, :]
    iota[:, 40:44] = np.arange(4)[None, :] * P + np.arange(P)[:, None]
    return {"c_rope": rope, "c_decay": decay, "c_small": small, "c_onehot": onehot, "c_sel": sel,
            "c_iota": iota}




def columns(w, col, n, k0=0, nk=KC):
    v = w.rearrange("(k p) c -> p k c", p=P)
    return v[:, k0:k0 + nk, col:col + n] if isinstance(col, int) else v[:, k0:k0 + nk, bass.ds(col, n)]


def load_slab(k, sp, slab, sources, turn=0):
    slot, uses, _, dmas, per = slab
    assert dmas == len(sources)
    if uses:
        sp.wait_ge(k.freed[slot], turn * per + uses)
    chunks = sources[0].shape[1]
    n = sources[0].shape[2]
    to = k.ring[:, slot, 0:chunks * n * dmas].rearrange("p (k q n) -> p k q n", q=dmas, n=n)
    for i, source in enumerate(sources):
        sp.dma_start(to[:, :, i, :], source).then_inc(k.landed[slot], 16)


def slab_ready(k, pe, slab, turn=0):
    slot, _, before, dmas, per = slab
    pe.wait_ge(k.landed[slot], turn * (16 * dmas * per) + 16 * (before + dmas))



def split_high(k, act, raw, hi, sem):
    act.copy(hi, raw).then_inc(sem, 1)


def split_low(dve, raw, hi, lo):
    return dve.tensor_tensor(lo, raw, hi.bitcast(F32), ALU.subtract)


def last_holder(i, g, cycle, per):
    return g - cycle if i >= cycle else g - i - 1 - (per - 1 - i) % cycle


def wait_for(eng, what):
    if what is not None:
        eng.wait_ge(*what)


def row_piece(w, n):
    return bass.AP(tensor=w.tensor, offset=w.offset, ap=[[0, 128], [1, n]])


def entry(k):
    A = k.A
    k.s_const = k.sem("constants_in")
    turned, out = k.sem("in_turned"), k.sem("in_transposed")
    loaded = [k.sem(f"x_loaded{t}") for t in range(NT)]
    k.xt_in = out

    def sync(sp):
        sp.dma_start(k.small[:], A["c_small"]).then_inc(k.s_const, 16)
        for t in range(NT):
            sp.dma_start(k.X[:, t, :], A["x"][0, t * P:(t + 1) * P, :]).then_inc(loaded[t], 16)

    def tensor(pe):
        pe.wait_ge(k.s_const, 16)
        for t in range(NT):
            pe.wait_ge(loaded[t], 16)
            for half in range(2):
                if t > 0:
                    pe.wait_ge(out, 2 * (t - 1) + half + 1)
                for c in range(4):
                    i = 4 * half + c
                    mm = pe.transpose(k.PS[:, 4 + half, c * P:(c + 1) * P],
                                      k.X[:, t, i * P:(i + 1) * P], k.ident)
                mm.then_inc(turned, 1)

    def scalar(act):
        for t in range(NT):
            for half in range(2):
                act.wait_ge(turned, 2 * t + half + 1)
                act.copy(k.XT[:, 4 * half:4 * half + 4, t * P:(t + 1) * P],
                         k.PS[:, 4 + half, :].rearrange("p (c n) -> p c n", c=4)).then_inc(out, 1)

    return dict(sync=sync, tensor=tensor, scalar=scalar)


def retention_stage(k):
    A, W, PS = k.A, k.W, k.PS
    YT = W[:, 0:4096].rearrange("p (c n) -> p c n", c=KC)
    cos = W[:, 4096:4608].rearrange("p (t n) -> p t n", t=NT)
    sin = W[:, 4608:5120].rearrange("p (t n) -> p t n", t=NT)
    decay = W[:, 5120:7168].rearrange("p (h n) -> p h n", h=4)
    rot = W[:, 7168:8192].rearrange("p (t n) -> p t n", t=NT)
    tmp = W[:, 8192:8448]
    v = W[:, 8448:9472].rearrange("p (b t n) -> p b t n", b=2, t=NT)
    gate = W[:, 9472:10496].rearrange("p (b t n) -> p b t n", b=2, t=NT)
    qT, kT = W[:, 10496:11008], W[:, 11008:11520]
    probs = W[:, 11520:12800]
    on = W[:, 12800:13312].rearrange("p (t n) -> p t n", t=NT)
    stats, mv = k.stat[:, :, 0:6], k.stat[:, :, 6:8]
    sd, rstd = k.stat[:, :, 8], k.stat[:, :, 9]
    ident = k.ident
    tables = k.sem("ret_tables")
    projected, rotated, kept = k.sem("ret_projected"), k.sem("ret_rotated"), k.sem("ret_kept")
    qk_turned, qk_out = k.sem("ret_qk_turned"), k.sem("ret_qk_out")
    scored, masked = k.sem("ret_scored"), k.sem("ret_masked")
    summed, varied, rooted = k.sem("ret_summed"), k.sem("ret_varied"), k.sem("ret_rooted")
    normed, y_turned, y_out = k.sem("ret_normed"), k.sem("ret_y_turned"), k.sem("ret_y_out")
    k.ret_y_out, k.ret_masked, k.ret_summed = y_out, masked, summed
    k.ret_rotated, k.ret_kept, k.ret_normed = rotated, kept, normed
    H = 4
    place = [(2, 0), (3, 0), (0, 0), (3, 384)]

    def sync(sp):
        w = A["w_in_even"][0]
        for h in range(H):
            for half in range(2):
                load_slab(k, sp, k.ret_slabs[h][half],
                          [columns(w, h * P + 512 * part, P, 4 * half, 4) for part in range(4)])
            if h == 0:
                sp.dma_start(W[:, 4096:5120], A["c_rope"]).then_inc(tables, 16)
                sp.dma_start(W[:, 5120:7168], A["c_decay"]).then_inc(tables, 16)

    def tensor(pe):
        def project(h, t):
            if h > 0:
                pe.wait_ge(rotated, 4 * (h - 1) + t + 1)
                pe.wait_ge(kept, 4 * (h - 1) + t + 1)
            for c in range(KC):
                slab = k.ret_slabs[h][c // 4]
                if t == 0 and c % 4 == 0:
                    slab_ready(k, pe, slab)
                w = k.ring[:, slab[0], :].rearrange("p (k n) -> p k n", k=4)[:, c % 4, :]
                mm = pe.matmul(PS[:, 4 + t, :], k.XT[:, c, t * P:(t + 1) * P], w,
                               start=(c == 0), stop=(c == KC - 1))
                if t == NT - 1 and c == 3:
                    mm.then_inc(k.freed[slab[0]], 1)
            mm.then_inc(projected, 1)

        def turn_y(h):
            pe.wait_ge(normed, h + 1)
            for t in range(NT):
                mm = pe.transpose(PS[:, 2, t * P:(t + 1) * P], on[:, t, :], ident)
            mm.then_inc(y_turned, 1)

        pe.wait_ge(k.xt_in, 2 * NT)
        for t in range(NT):
            project(0, t)
        for h in range(H):
            pe.drain().then_inc(k.freed[k.ret_slabs[h][1][0]], 1)
            pe.wait_ge(rotated, 4 * h + 4)
            for part in range(2):
                for t in range(NT):
                    mm = pe.transpose(PS[:, part, t * P:(t + 1) * P],
                                      rot[:, t, part * P:(part + 1) * P], ident)
                mm.then_inc(qk_turned, 1)
            pe.wait_ge(qk_out, 2 * h + 2)
            if h > 0:
                pe.wait_ge(y_out, h)
            for j in range(NT):
                bank, col = place[j]
                n = S - j * P
                mm = pe.matmul(PS[:, bank, col:col + n], kT[:, j * P:(j + 1) * P], qT[:, j * P:S],
                               start=True, stop=True)
                mm.then_inc(scored, 1)
            if h + 1 < H:
                project(h + 1, 0)
                project(h + 1, 1)
            pe.wait_ge(masked, 4 * h + 4)
            pe.wait_ge(kept, 4 * h + 4)
            for i in range(NT):
                for j in range(i + 1):
                    p0 = OFF[j] + (i - j) * P
                    mm = pe.matmul(PS[:, 1, i * P:(i + 1) * P], probs[:, p0:p0 + P],
                                   v[:, h % 2, j, :], start=(j == 0), stop=(j == i))
            mm.then_inc(summed, 1)
            if h + 1 < H:
                project(h + 1, 2)
                project(h + 1, 3)
            turn_y(h)

    def scalar(act):
        def keep(h, t):
            act.wait_ge(rotated, 4 * h + t + 1)
            if h > 1:
                act.wait_ge(summed, h - 1)
                act.wait_ge(normed, h - 1)
            act.activation(gate[:, h % 2, t, :], PS[:, 4 + t, 384:512], ACT.Silu)
            act.copy(v[:, h % 2, t, :], PS[:, 4 + t, 256:384]).then_inc(kept, 1)

        def roots(h):
            act.wait_ge(varied, h + 1)
            act.activation(sd, mv[:, :, 1], ACT.Sqrt, bias=k.eps_ln).then_inc(rooted, 1)

        for t in range(NT):
            keep(0, t)
        for h in range(H):
            for part in range(2):
                act.wait_ge(qk_turned, 2 * h + part + 1)
                if h > 0:
                    act.wait_ge(scored, 4 * h)
                act.copy([qT, kT][part], PS[:, part, :]).then_inc(qk_out, 1)
            if h + 1 < H:
                keep(h + 1, 0)
                keep(h + 1, 1)
            roots(h)
            if h + 1 < H:
                keep(h + 1, 2)
                keep(h + 1, 3)
            act.wait_ge(y_turned, h + 1)
            act.copy(YT[:, h, :], PS[:, 2, :]).then_inc(y_out, 1)

    def vector(dve):
        def rotate(h, t):
            dve.wait_ge(projected, 4 * h + t + 1)
            if h > 0:
                dve.wait_ge(qk_turned, 2 * h)
            two = lambda ap: bass.AP(tensor=ap.tensor, offset=ap.offset,
                                     ap=[list(ap.ap[0]), [0, 2], list(ap.ap[1])])
            qk = PS[:, 4 + t, 0:256].rearrange("p (q n) -> p q n", q=2)
            r = rot[:, t, :].rearrange("p (q n) -> p q n", q=2)
            w = tmp.rearrange("p (q n) -> p q n", q=2)
            dve.drain()
            dve.tensor_tensor(r, qk, two(cos[:, t, :]), ALU.mult)
            dve.tensor_tensor(w[:, :, 0:64], qk[:, :, 64:128], two(sin[:, t, 0:64]), ALU.mult)
            dve.tensor_tensor(w[:, :, 64:128], qk[:, :, 0:64], two(sin[:, t, 64:128]), ALU.mult)
            dve.drain()
            dve.tensor_tensor(r, r, w, ALU.add).then_inc(rotated, 1)

        dve.wait_ge(tables, 32)
        for t in range(NT):
            rotate(0, t)
        for h in range(H):
            if h > 0:
                dve.wait_ge(summed, h)
            dve.wait_ge(scored, 4 * h + 4)
            for j in range(NT):
                bank, col = place[j]
                n = S - j * P
                dve.tensor_tensor(probs[:, OFF[j]:OFF[j] + n], PS[:, bank, col:col + n],
                                  decay[:, h, 0:n], ALU.mult).then_inc(masked, 1)
            if h + 1 < H:
                rotate(h + 1, 0)
                rotate(h + 1, 1)
            dve.wait_ge(summed, h + 1)
            for t in range(NT):
                dve.bn_stats(stats[:, t, :], PS[:, 1, t * P:(t + 1) * P])
            dve.drain()
            for t in range(NT):
                mm = dve.bn_aggr(mv[:, t, :], stats[:, t, :])
            mm.then_inc(varied, 1)
            dve.wait_ge(rooted, h + 1)
            dve.reciprocal(rstd, sd)
            dve.drain()
            if h > 0:
                dve.wait_ge(y_turned, h)
            for t in range(NT):
                dve.tensor_scalar(on[:, t, :], PS[:, 1, t * P:(t + 1) * P], mv[:, t, 0:1],
                                  rstd[:, t:t + 1], ALU.subtract, ALU.mult)
            dve.drain()
            dve.wait_ge(kept, 4 * h + 4)
            dve.tensor_tensor(on, on, gate[:, h % 2, :, :], ALU.mult).then_inc(normed, 1)
            if h + 1 < H:
                rotate(h + 1, 2)
                rotate(h + 1, 3)

    return dict(sync=sync, tensor=tensor, scalar=scalar, vector=vector)

def stick_stage(k):
    A, W, PS = k.A, k.W, k.PS
    YT = W[:, 0:4096].rearrange("p (c n) -> p c n", c=KC)
    q, kk = W[:, 13312:13824], W[:, 13824:14336]
    v = W[:, 14336:14848].rearrange("p (t n) -> p t n", t=NT)
    e = W[:, 14848:16128]
    soft = [W[:, 4096:5376], W[:, 5376:6656]]
    a = [W[:, 6656:7936], W[:, 7936:9216]]
    projected, kept = k.sem("sb_projected"), k.sem("sb_kept")
    v_kept = k.sem("sb_v_kept")
    scored, logged, softened, cut = k.sem("sb_scored"), k.sem("sb_logged"), k.sem("sb_softened"), k.sem("sb_cut")
    summed, exped, masked = k.sem("sb_summed"), k.sem("sb_exped"), k.sem("sb_masked")
    valued, y_out = k.sem("sb_valued"), k.sem("sb_y_out")
    k.sb_y_out = y_out
    place = [(0, 0), (1, 0), (2, 0), (1, 384)]
    COL = [0, 512, 1024, 896]

    def sync(sp):
        w = A["w_in_even"][0]
        for p in range(4):
            for half in range(2):
                load_slab(k, sp, k.sb_slabs[p][half],
                          [columns(w, 2048 + p * P + 512 * part, P, 4 * half, 4) for part in range(3)])

    def tensor(pe):
        def project(p, part):
            n = 3 * p + part
            slabs = k.sb_slabs[p]
            if n >= 2:
                if part == 2:
                    pe.wait_ge(kept, 2 * p + 1)
                elif part == 0:
                    pe.wait_ge(kept, 2 * p)
                else:
                    pe.wait_ge(v_kept, p)
            elif part == 0:
                pe.wait_ge(k.ret_kept, 16)
                pe.wait_ge(k.ret_rotated, 16)
            bank = 6 + (n % 2)
            for c in range(KC):
                slab = slabs[c // 4]
                if part == 0 and c % 4 == 0:
                    slab_ready(k, pe, slab)
                w = k.ring[:, slab[0], 0:4 * 3 * P].rearrange("p (k n) -> p k n", k=4)[:, c % 4, :]
                w = w[:, part * P:(part + 1) * P]
                if part < 2:
                    mm = pe.matmul(PS[:, bank, :], w, k.XT[:, c, :], start=(c == 0), stop=(c == KC - 1))
            if part == 2:
                for t in range(NT):
                    for c in range(KC):
                        slab = slabs[c // 4]
                        w = k.ring[:, slab[0], 0:4 * 3 * P].rearrange("p (k n) -> p k n", k=4)[:, c % 4, :]
                        mm = pe.matmul(PS[:, bank, t * P:(t + 1) * P], k.XT[:, c, t * P:(t + 1) * P],
                                       w[:, 2 * P:3 * P], start=(c == 0), stop=(c == KC - 1))
                        if t == NT - 1 and c == 3:
                            mm.then_inc(k.freed[slabs[0][0]], 1)
            mm.then_inc(projected, 1)
            if part == 2:
                pe.drain().then_inc(k.freed[slabs[1][0]], 1)

        pe.wait_ge(k.cols_in, 1)
        pe.wait_ge(k.taps_in, 1)
        for part in range(3):
            project(0, part)
        pe.wait_ge(k.bias_masked, 1)
        for p in range(4):
            pe.wait_ge(kept, 2 * p + 2)
            for hh in range(2):
                if p > 0:
                    pe.wait_ge(y_out, 2 * (p - 1) + hh + 1)
                elif hh == 0:
                    pe.wait_ge(k.ret_masked, 16)
                    pe.wait_ge(k.ret_normed, 4)
                    pe.wait_ge(k.ret_y_out, 4)
                r = slice(64 * hh, 64 * hh + 64)
                for j in range(NT):
                    bank, col = place[j]
                    n = S - j * P
                    mm = pe.matmul(PS[:, 3 * hh + bank, col:col + n], kk[r, j * P:(j + 1) * P],
                                   q[r, j * P:S], start=(j != 3), stop=False, skip_group_check=True)
                mm.then_inc(scored, 1)
            if p < 3:
                for part in range(3):
                    project(p + 1, part)
            for hh in range(2):
                pe.wait_ge(cut, 2 * p + hh + 1)
                for j in range(NT):
                    bank, col = place[j]
                    for j2 in range(j, NT):
                        lo = (j2 - j) * P
                        n = S - j2 * P
                        mm = pe.matmul(PS[:, 3 * hh + bank, col + lo:col + lo + n],
                                       k.negtri if j2 == j else k.negone,
                                       soft[hh][:, COL[j2]:COL[j2] + n],
                                       start=False, stop=(j2 == NT - 1), skip_group_check=True)
                mm.then_inc(summed, 1)
            pe.wait_ge(v_kept, p + 1)
            for hh in range(2):
                pe.wait_ge(masked, 2 * p + hh + 1)
                r = slice(64 * hh, 64 * hh + 64)
                for j in range(NT):
                    mm = pe.matmul(PS[r, 3 * hh, j * P:S], v[:, j, r],
                                   a[hh][:, COL[j]:COL[j] + S - j * P],
                                   start=(j == 0), stop=(j == NT - 1), skip_group_check=True)
                mm.then_inc(valued, 1)

    def scalar(act):
        def keep(p):
            for part in range(2):
                act.wait_ge(projected, 3 * p + part + 1)
                if p > 0:
                    act.wait_ge(scored, 2 * p)
                elif part == 0:
                    act.wait_ge(k.ret_y_out, 4)
                act.mul([q, kk][part], PS[:, 6 + (3 * p + part) % 2, :],
                        [DH ** -0.5, 1.0][part]).then_inc(kept, 1)

        def keep_v(p):
            act.wait_ge(projected, 3 * p + 3)
            if p > 0:
                act.wait_ge(valued, 2 * p)
            act.copy(v, PS[:, 6 + (3 * p + 2) % 2, :].rearrange("p (t n) -> p t n", t=NT))\
               .then_inc(v_kept, 1)

        keep(0)
        keep_v(0)
        for p in range(4):
            for hh in range(2):
                act.wait_ge(scored, 2 * p + hh + 1)
                if 2 * p + hh > 0:
                    act.wait_ge(softened, 2 * p + hh)
                zz = PS[:, 3 * hh:3 * hh + 3, :].rearrange("p b n -> p (b n)")[:, 0:CAUSAL]
                act.activation(e, zz, ACT.Abs)
                act.drain()
                act.activation(e, e, ACT.Exp, scale=-1.0)
                act.drain()
                act.activation(e, e, ACT.Ln, bias=1.0).then_inc(logged, 1)
            if p < 3:
                keep(p + 1)
            for hh in range(2):
                act.wait_ge(summed, 2 * p + hh + 1)
                if p > 0:
                    act.wait_ge(valued, 2 * (p - 1) + hh + 1)
                zz = PS[:, 3 * hh:3 * hh + 3, :].rearrange("p b n -> p (b n)")[:, 0:CAUSAL]
                act.activation(a[hh], zz, ACT.Exp).then_inc(exped, 1)
            if p < 3:
                keep_v(p + 1)

    def gpsimd(pool):
        cols = COL
        for p in range(4):
            for hh in range(2):
                pool.wait_ge(softened, 2 * p + hh + 1)
                for j in range(NT):
                    d = soft[hh][:, cols[j]:cols[j] + P]
                    mm = pool.affine_select(out=d, in_=d, pattern=[[1, P]], compare_op=ALU.is_gt,
                                            fill=0.0, base=0, channel_multiplier=-1)
                mm.then_inc(cut, 1)
            for hh in range(2):
                pool.wait_ge(exped, 2 * p + hh + 1)
                for j in range(NT):
                    d = a[hh][:, cols[j]:cols[j] + P]
                    mm = pool.affine_select(out=d, in_=d, pattern=[[1, P]], compare_op=ALU.is_gt,
                                            fill=0.0, base=0, channel_multiplier=-1)
                mm.then_inc(masked, 1)

    def vector(dve):
        def keep_y(p):
            for hh in range(2):
                r = slice(64 * hh, 64 * hh + 64)
                dve.wait_ge(valued, 2 * p + hh + 1)
                dve.tensor_copy(YT[r, 4 + p, :], PS[r, 3 * hh, :]).then_inc(y_out, 1)

        for p in range(4):
            for hh in range(2):
                dve.wait_ge(logged, 2 * p + hh + 1)
                if p > 0:
                    dve.wait_ge(summed, 2 * (p - 1) + hh + 1)
                zz = PS[:, 3 * hh:3 * hh + 3, :].rearrange("p b n -> p (b n)")[:, 0:CAUSAL]
                dve.scalar_tensor_tensor(soft[hh], zz, 0.0, e, ALU.max, ALU.add).then_inc(softened, 1)
            keep_y(p)

    return dict(sync=sync, tensor=tensor, scalar=scalar, vector=vector, gpsimd=gpsimd)

def mix_out_stage(k, name, w_out, slabs, ready, gains, mode, beside=None):
    W = k.W
    YT = W[:, 0:4096].rearrange("p (c n) -> p c n", c=KC)
    tail = norm_tail(k, name, gains, mode)

    def sync(sp):
        for i in range(4):
            load_slab(k, sp, slabs[i], [columns(w_out, 0, D, 2 * i, 2)])

    def tensor(pe):
        for s, v in ready:
            pe.wait_ge(s, v)
        for t in range(NT):
            if beside:
                beside(pe, t)
            if t >= 2:
                pe.wait_ge(tail.summed, t - 1)
            for c in range(KC):
                slab = slabs[c // 2]
                if t == 0 and c % 2 == 0:
                    slab_ready(k, pe, slab)
                w = k.ring[:, slab[0], :].rearrange("p (k n) -> p k n", k=2)[:, c % 2, :]
                for half in range(2):
                    mm = pe.matmul(k.PS[:, 2 * (t % 2) + half, :], YT[:, c, t * P:(t + 1) * P],
                                   w[:, 512 * half:512 * half + 512], start=(c == 0), stop=(c == KC - 1))
                if t == NT - 1 and c % 2 == 1 and c < KC - 1:
                    mm.then_inc(k.freed[slab[0]], 1)
            mm.then_inc(tail.product, 1)
            if t > 0:
                tail.turn(pe, t - 1)
        pe.drain().then_inc(k.freed[slabs[3][0]], 1)
        if mode == "rms":
            tail.turn(pe, NT - 1)

    return dict(sync=sync, tensor=tensor, scalar=tail.scalar, vector=tail.vector, gpsimd=tail.gpsimd)


def x_half(k, high):
    return k.XS[:, high, :].rearrange("p (c n) -> p c n", c=KC)


def norm_tail(k, name, gains, mode):
    W, X, PS = k.W, k.X, k.PS
    r = W[:, 13824:14848]
    nh = 4 if mode == "rms" else 2
    hrow = (W[:, 4096:8192] if mode == "rms" else W[:, 11264:13312]).rearrange("p (b n) -> p b n", b=nh)
    tail = Namespace()
    tail.product = product = k.sem(name + "_product")
    tail.summed = summed = k.sem(name + "_summed")
    varied, rooted = k.sem(name + "_varied"), k.sem(name + "_rooted")
    normed, turned, xt_out = k.sem(name + "_normed"), k.sem(name + "_turned"), k.sem(name + "_xt_out")
    rows_in = k.sem(name + "_rows")
    before = k.rows_used
    k.rows_used = (normed, NT)
    split = name in ("even", "odd", "ffn1")
    xt_high = k.sem(name + "_xt_high")
    tail.early = None
    st = k.stat
    pair = (lambda t: 2 * (t % 2)) if name != "ffn0" and name != "ffn1" else (lambda t: 2 * t)
    src = (lambda t: X[:, t, :]) if mode == "ln" else (lambda t: hrow[:, t % nh, :])
    scale = 1.0 if mode == "rms" else ALPHA

    def gpsimd(pool):
        wait_for(pool, before)
        for i, g in enumerate(gains):
            pool.dma_start(k.rows[:, i, :], row_piece(g, D)).then_inc(rows_in, 16)
        pool.wait_ge(rows_in, 16 * len(gains))

    def turn(pe, t):
        pe.wait_ge(normed, t + 1)
        for half in range(2):
            if t > 0:
                pe.wait_ge(xt_out, 2 * (t - 1) + half + 1)
            bank = tail.turn_banks[half]
            for c in range(4):
                i = 4 * half + c
                mm = pe.transpose(PS[:, bank, c * P:(c + 1) * P], src(t)[:, i * P:(i + 1) * P], k.ident)
            mm.then_inc(turned, 1)

    norms = 2 if mode == "ln+rms" else 1

    def scalar(act):
        for t in range(NT):
            if t == NT - 1 and tail.early:
                tail.early.scalar(act)
            for n in range(norms):
                act.wait_ge(varied, norms * t + n + 1)
                if mode != "rms" and n == 0:
                    act.activation(st[:, t, 14:15], st[:, t, 13:14], ACT.Sqrt, bias=k.eps_ln).then_inc(rooted, 1)
                else:
                    act.activation(hrow[:, t % nh, :], X[:, t, :], ACT.Square, accum_out=st[:, t, 13:14])
                    act.drain()
                    act.activation(st[:, t, 14:15], st[:, t, 13:14], ACT.Sqrt, bias=k.eps_rms,
                                   scale=1.0 / D).then_inc(rooted, 1)
            for half in range(2):
                act.wait_ge(turned, 2 * t + half + 1)
                to = x_half(k, 1) if split else k.XT
                act.copy(to[:, 4 * half:4 * half + 4, t * P:(t + 1) * P],
                         PS[:, tail.turn_banks[half], :].rearrange("p (c n) -> p c n", c=4))\
                   .then_inc(xt_high if split else xt_out, 1)

    def low(dve, t):
        for half in range(2):
            dve.wait_ge(xt_high, 2 * t + half + 1)
            split_low(dve, PS[:, tail.turn_banks[half], :].rearrange("p (c n) -> p c n", c=4),
                      x_half(k, 1)[:, 4 * half:4 * half + 4, t * P:(t + 1) * P],
                      x_half(k, 0)[:, 4 * half:4 * half + 4, t * P:(t + 1) * P]).then_inc(xt_out, 1)

    def vector(dve):
        dve.wait_ge(rows_in, 16 * len(gains))
        for t in range(NT):
            if t == NT - 1 and tail.early:
                tail.early.vector(dve)
            dve.wait_ge(product, t + 1)
            for half in range(2):
                c = slice(512 * half, 512 * half + 512)
                to = r if mode != "rms" else X[:, t, :]
                mm = dve.scalar_tensor_tensor(to[:, c], X[:, t, c], scale, PS[:, pair(t) + half, :],
                                              ALU.mult, ALU.add)
            mm.then_inc(summed, 1)
            dve.drain()
            if mode != "rms":
                for half in range(2):
                    dve.bn_stats(st[:, t, 6 * half:6 * half + 6], r[:, 512 * half:512 * half + 512])
                dve.drain()
                dve.bn_aggr(st[:, t, 12:14], st[:, t, 0:12]).then_inc(varied, 1)
                dve.drain()
                dve.scalar_tensor_tensor(r, r, st[:, t, 12:13], k.rows[:, 0, :], ALU.subtract, ALU.mult)
                dve.wait_ge(rooted, norms * t + 1)
                dve.reciprocal(st[:, t, 15:16], st[:, t, 14:15])
                dve.drain()
                mm = dve.scalar_tensor_tensor(X[:, t, :], r, st[:, t, 15:16], k.rows[:, 1, :],
                                              ALU.mult, ALU.add)
                if mode == "ln":
                    mm.then_inc(normed, 1)
                    dve.drain()
                if split and t > 0 and mode == "ln":
                    low(dve, t - 1)
            if mode != "ln":
                g = k.rows[:, 2 if mode == "ln+rms" else 0, :]
                if t >= nh:
                    dve.wait_ge(turned, 2 * (t - nh + 1))
                h = hrow[:, t % nh, :]
                dve.drain().then_inc(varied, 1)
                if split and t > 0:
                    low(dve, t - 1)
                dve.wait_ge(rooted, norms * t + norms)
                dve.reciprocal(st[:, t, 15:16], st[:, t, 14:15])
                dve.drain()
                dve.scalar_tensor_tensor(h, X[:, t, :], st[:, t, 15:16], g, ALU.mult, ALU.mult)\
                   .then_inc(normed, 1)
        if split:
            low(dve, NT - 1)
    tail.turn, tail.scalar, tail.vector, tail.gpsimd = turn, scalar, vector, gpsimd
    tail.turn_banks = (4, 5)
    tail.normed, tail.hrow, tail.turned = normed, hrow, turned
    k.xt_ready = (xt_out, 2 * NT)
    k.x_ready = (normed, NT)
    k.tail = tail
    return tail


def ffn_stage(k, layer, slabs, gains, mode):
    A, W, PS = k.A, k.W, k.PS
    name = f"ffn{layer}"
    conv = W[:, 11264:13312].rearrange("p (b q n) -> p b q n", b=2, q=2)
    silu = W[:, 13312:13824]
    taps = k.taps
    xt_ready = k.xt_ready
    up, seeded, shifted = k.sem(name + "_up"), k.sem(name + "_seeded"), k.sem(name + "_shifted")
    gated, silued = k.sem(name + "_gated"), k.sem(name + "_silued")
    w_high, split_used = k.sem(name + "_w_high"), k.sem(name + "_split_used")
    h_high, h_low = k.sem(name + "_h_high"), k.sem(name + "_h_low")
    mixer_tail = k.tail
    tail = norm_tail(k, name, gains, mode)
    tail.turn_banks = (0, 1)

    def pair_of(i):
        return (6, 0, 2)[i % 3]

    def high_w(act, i, turn):
        i, turn = (i, turn) if i < UD else (i - UD, turn + 1)
        slab_ready(k, act, slabs[i], turn)
        act.wait_ge(split_used, last_holder(i, turn * UD + i, SPLIT, UD) + 1 + AHEAD)
        split_high(k, act, k.ring[:, slabs[i][0], :], k.split[:, i % SPLIT, 1, :], w_high)

    def low_w(dve, i, turn):
        i, turn = (i, turn) if i < UD else (i - UD, turn + 1)
        dve.wait_ge(w_high, turn * UD + i + 1)
        split_low(dve, k.ring[:, slabs[i][0], :], k.split[:, i % SPLIT, 1, :],
                  k.split[:, i % SPLIT, 0, :]).then_inc(k.freed[slabs[i][0]], 1)

    def split_ready(pe, i, turn):
        slot, uses, _, _, per = slabs[i]
        pe.wait_ge(k.freed[slot], turn * per + uses + 1)

    def h_half(p, high):
        return k.H0[:, high, :] if p == 0 else k.XS[:, high, (p - 1) % 4 * 1024:(p - 1) % 4 * 1024 + 1024]

    def high_h(act, p):
        if p > 0:
            act.wait_ge(split_used, AHEAD + 2 * UD + max(p - 4 + 1, 0))
        act.wait_ge(gated, 2 * p + 3)
        split_high(k, act, W[:, 1024 * p:1024 * p + 1024], h_half(p, 1), h_high)

    def low_h(dve, p, n):
        dve.wait_ge(h_high, n)
        split_low(dve, W[:, 1024 * p:1024 * p + 1024], h_half(p, 1), h_half(p, 0)).then_inc(h_low, 1)

    def early_scalar(act):
        act.sem_inc(split_used, AHEAD)
        high_w(act, 0, 0)
        act.wait_ge(mixer_tail.product, NT)
        high_w(act, 1, 0)

    def early_vector(dve):
        low_w(dve, 0, 0)
        low_w(dve, 1, 0)

    mixer_tail.early = early = Namespace()
    early.scalar, early.vector = early_scalar, early_vector

    def sync(sp):
        w = A["w_up"][layer]
        with sp.Fori(0, 2) as turn:
            for i in range(UD):
                load_slab(k, sp, slabs[i],
                          [columns(w, (turn * UD + i) * P + q * FF, P) for q in range(2)], turn)
        w = A["w_down"][layer]
        for i in range(UD):
            load_slab(k, sp, slabs[i], [columns(w, 0, D, 2 * i + c, 1) for c in range(2)], 2)

    def up_product(pe, i, rows):
        b = pair_of(i)
        wh, wl = (k.split[:, i % SPLIT, h, :].rearrange("p (k q n) -> p k q n", k=KC, q=2) for h in (1, 0))
        for q in range(2):
            for c in range(KC):
                for m, (w, high) in enumerate(((wh, 1), (wh, 0), (wl, 1))):
                    mm = pe.matmul(PS[:, b + q, rows], w[:, c, q, :], x_half(k, high)[:, c, rows],
                                   start=(c == 0 and m == 0), stop=(c == KC - 1 and m == 2))
            if rows.stop == S:
                mm.then_inc(up if q == 0 else split_used, 1)

    def tensor(pe):
        for turn in range(2):
            for i in range(UD):
                if turn > 0 or i > 1:
                    split_ready(pe, i, turn)
                    pe.wait_ge(shifted, last_holder(i, turn * UD + i, 3, UD) + 1 + AHEAD)
                    up_product(pe, i, slice(0, S))
                elif i == 0:
                    for rows in (slice(0, S // 2), slice(S // 2, S)):
                        pe.wait_ge(xt_ready[0], xt_ready[1] * rows.stop // S)
                        for first in range(2):
                            if rows.start == 0:
                                split_ready(pe, first, 0)
                                if first == 1:
                                    pe.wait_ge(mixer_tail.summed, NT - 1)
                            up_product(pe, first, rows)
                        if rows.start == 0:
                            mixer_tail.turn(pe, NT - 1)

        def down(i, t):
            wh, wl = (k.split[:, i % SPLIT, h, :].rearrange("p (k n) -> p k n", k=2) for h in (1, 0))
            for c in range(2):
                at = c * S + t * P
                for m, (high, w) in enumerate(((1, wh), (1, wl), (0, wh))):
                    for half in range(2):
                        mm = pe.matmul(PS[:, 2 * t + half, :], h_half(i, high)[:, at:at + P],
                                       w[:, c, 512 * half:512 * half + 512],
                                       start=(i == 0 and c == 0 and m == 0),
                                       stop=(i == UD - 1 and c == 1 and m == 2))
            return mm

        for i in range(UD - SPLIT):
            split_ready(pe, i, 2)
            pe.wait_ge(h_low, i + 2)
            for t in (2, 1, 3, 0) if i == 0 else range(NT):
                if i == 0 and t != 2:
                    pe.wait_ge(shifted, FT - {1: 2, 3: 1, 0: 0}[t] + AHEAD)
                mm = down(i, t)
            mm.then_inc(split_used, 1)
        for t in range(NT):
            for i in range(UD - SPLIT, UD):
                if t == 0:
                    split_ready(pe, i, 2)
                    pe.wait_ge(h_low, i + 2)
                mm = down(i, t)
            mm.then_inc(tail.product, 1)
        pe.wait_ge(tail.summed, 1)
        for t in range(NT):
            tail.turn(pe, t)

    def scalar(act):
        act.wait_ge(k.taps_in, 1)
        with act.Fori(0, 2) as turn:
            for i in range(UD):
                b = pair_of(i)
                n = turn * UD + i
                high_w(act, i + 2, turn)
                if i == UD // 2:
                    high_h(act, 0)
                for q in range(2):
                    if q == 0:
                        act.wait_ge(up, n + 1)
                    else:
                        act.wait_ge(split_used, n + 1 + AHEAD)
                    act.wait_ge(gated, turn * UD + max(i - 1, 0) + 1)
                    act.activation(conv[:, i % 2, q, :], PS[:, b + q, :], ACT.Identity,
                                   bias=tap_at(k, layer, 3, q, turn, i), scale=tap_at(k, layer, 2, q, turn, i))\
                       .then_inc(seeded, 1)
                act.wait_ge(shifted, n + 1 + AHEAD)
                act.wait_ge(gated, n + 1)
                act.activation(silu, conv[:, i % 2, 1, :], ACT.Silu).then_inc(silued, 1)
        high_h(act, 1)
        for i in range(UD - 2):
            high_w(act, i + 2, 2)
            high_h(act, i + 2)
        tail.scalar(act)

    def vector(dve):
        dve.sem_inc(shifted, AHEAD)
        dve.sem_inc(gated, 1)
        dve.wait_ge(k.taps_in, 1)
        with dve.Fori(0, 2) as turn:
            for i in range(UD):
                b = pair_of(i)
                n = turn * UD + i
                low_w(dve, i + 2, turn)
                if i == UD // 2:
                    low_h(dve, 0, turn + 1)
                for q in range(2):
                    dve.wait_ge(seeded, n * 2 + q + 1)
                    y = conv[:, i % 2, q, :]
                    dve.scalar_tensor_tensor(y[:, 1:S], PS[:, b + q, 0:S - 1], tap_at(k, layer, 1, q, turn, i),
                                             y[:, 1:S], ALU.mult, ALU.add)
                    dve.drain()
                    mm = dve.scalar_tensor_tensor(y[:, 2:S], PS[:, b + q, 0:S - 2], tap_at(k, layer, 0, q, turn, i),
                                                  y[:, 2:S], ALU.mult, ALU.add)
                mm.then_inc(shifted, 1)
                dve.drain()
                dve.wait_ge(silued, n + 1)
                dve.tensor_tensor(hT_at(k, turn, i), conv[:, i % 2, 0, :], silu, ALU.mult).then_inc(gated, 1)
        low_h(dve, 1, 3)
        for i in range(UD - 2):
            low_w(dve, i + 2, 2)
            low_h(dve, i + 2, i + 4)
        tail.vector(dve)

    return dict(sync=sync, tensor=tensor, scalar=scalar, vector=vector, gpsimd=tail.gpsimd)


def hT_at(k, turn, i):
    return k.W[:, 0:FT * S].rearrange("p (u n) -> p u n", u=2)[:, turn, i * S:(i + 1) * S]


def tap_at(k, layer, tap, q, turn, i):
    t = k.taps[:, layer, tap, :].rearrange("p (q n) -> p q n", q=2)[:, q, :]
    return t[:, turn * UD + i:turn * UD + i + 1] if isinstance(turn, int) else t[:, bass.ds(turn * UD + i, 1)]


def bias_stage(k):
    A, W, PS = k.A, k.W, k.PS
    onehot = k.rows[0:32, 2, 0:640]
    table = k.rows[0:32, 2, 640:648]
    lam = k.lam
    vec_in, table_in, looked, masked = (k.sem("lam_vectors"), k.sem("bias_table"), k.sem("bias_looked"),
                                        k.sem("bias_masked"))
    dots, exps, k.lam_ready = k.sem("lam_dots"), k.sem("lam_exps"), k.sem("lam_ready")
    k.bias_out = k.sem("bias_rows_out")
    k.bias_masked = masked
    k.rows_used = (k.bias_out, 16)
    k.bias_rows = k.dram("bias_rows", (8, 640))
    k.bias_skew = k.dram("bias_skewed", (8, P * 641))
    skewed = k.sem("bias_skewed")
    vec = k.lam_vec[:].rearrange("p (v n) -> p v n", v=4)

    def gpsimd(pool):
        for i, n in enumerate(["lam_q1", "lam_k1", "lam_q2", "lam_k2"]):
            pool.dma_start(vec[:, i, :], row_piece(A[n], DH)).then_inc(vec_in, 16)
        pool.dma_start(onehot, A["c_onehot"]).then_inc(table_in, 16)
        pool.dma_start(table, A["rel_bias"]).then_inc(table_in, 16)

    def tensor(pe):
        pe.wait_ge(table_in, 32)
        for half in range(2):
            mm = pe.matmul(PS[0:8, 4 + half, 0:320], table, onehot[:, 320 * half:320 * half + 320],
                           start=True, stop=True)
        mm.then_inc(looked, 1)

    def scalar(act):
        act.wait_ge(dots, 1)
        act.activation(lam[:, 2:4], lam[:, 0:2], ACT.Exp).then_inc(exps, 1)

    def vector(dve):
        dve.wait_ge(vec_in, 64)
        for i in range(2):
            mm = dve.tensor_tensor_reduce(vec[:, 2 * i, :], vec[:, 2 * i, :], vec[:, 2 * i + 1, :], 1.0, 0.0,
                                          ALU.mult, ALU.add, lam[:, i:i + 1])
        mm.then_inc(dots, 1)
        dve.wait_ge(looked, 1)
        for half in range(2):
            dve.tensor_copy(k.bias_line[:, 320 * half:320 * half + 320], PS[0:8, 4 + half, 0:320])
        dve.drain()
        dve.memset(k.bias_line[:, 512:640], NEG).then_inc(masked, 1)
        dve.wait_ge(exps, 1)
        dve.tensor_tensor(lam[:, 4:5], lam[:, 3:4], lam[:, 2:3], ALU.subtract)
        dve.drain()
        dve.tensor_scalar(lam[:, 5:6], lam[:, 4:5], -LAM_INIT, None, ALU.add).then_inc(k.lam_ready, 1)

    def sync(sp):
        sp.wait_ge(masked, 1)
        sp.dma_start(k.bias_rows, k.bias_line).then_inc(k.bias_out, 16)
        sp.wait_ge(k.bias_out, 16)
        for h in range(8):
            to = bass.AP(tensor=k.bias_skew.tensor, offset=h * P * 641, ap=[[641, P], [1, 640]])
            src = bass.AP(tensor=k.bias_rows.tensor, offset=h * 640, ap=[[0, P], [1, 640]])
            sp.dma_start(to, src).then_inc(skewed, 16)
        sp.wait_ge(skewed, 128)

    return dict(gpsimd=gpsimd, tensor=tensor, scalar=scalar, vector=vector, late_sync=sync)


def load_odd_slab(k, sp, h, half):
    load_slab(k, sp, k.odd_slabs[h][half],
              [columns(k.A["w_in_odd"][0], h * P + D * part, P, 4 * half, 4) for part in range(3)])


def odd_ahead(k):
    def sync(sp):
        for h in range(2):
            for half in range(2):
                load_odd_slab(k, sp, h, half)

    return dict(sync=sync)


def hybrid_ahead(k):
    def sync(sp):
        for c in range(4):
            load_slab(k, sp, k.cv_slabs[c], [columns(k.A["w_in_2"][0], c * P + 512 * q, P) for q in range(2)])

    return dict(sync=sync)


def diff_stage(k):
    A, W, PS = k.A, k.W, k.PS
    YT = W[:, 0:4096].rearrange("p (c n) -> p c n", c=KC)
    bias = W[:, 4096:8192].rearrange("p (h n) -> p h n", h=8)
    q = [W[:, 8192 + 1536 * b:8704 + 1536 * b] for b in range(2)]
    kk = [W[:, 8704 + 1536 * b:9216 + 1536 * b] for b in range(2)]
    v = [W[:, 9216 + 1536 * b:9728 + 1536 * b].rearrange("p (t n) -> p t n", t=NT) for b in range(2)]
    s = W[:, 11264:13312].rearrange("p (b r n) -> p b r n", b=2, r=2)
    w = W[:, 13312:14336].rearrange("p (b n) -> p b n", b=2)
    wT = W[:, 14336:15360].rearrange("p (b n) -> p b n", b=2)
    on = W[:, 15360:15872].rearrange("p (t n) -> p t n", t=NT)
    gain = W[:, 15872:16000]
    junk = W[:, 16000:16128]
    col = k.cols
    bias_in, gain_in, gain_set = k.sem("bias_tiles"), k.sem("subln_in"), k.sem("subln_scaled")
    projected, kept = k.sem("df_projected"), k.sem("df_kept")
    scored, biased, negated, exped = k.sem("df_scored"), k.sem("df_biased"), k.sem("df_negated"), k.sem("df_exped")
    mixed, w_turned, w_out = k.sem("df_mixed"), k.sem("df_w_turned"), k.sem("df_w_out")
    valued, squared, rooted = k.sem("df_valued"), k.sem("df_squared"), k.sem("df_rooted")
    normed, y_turned, y_out = k.sem("df_normed"), k.sem("df_y_turned"), k.sem("df_y_out")
    k.df_y_out = y_out
    xt_ready, x_ready = k.xt_ready, k.x_ready
    HD = 8

    def sync(sp):
        for h in range(HD):
            src = bass.AP(tensor=k.bias_skew.tensor, offset=h * P * 641 + 127, ap=[[640, P], [1, 512]])
            sp.dma_start(bias[:, h, :], src).then_inc(bias_in, 16)
        for h in range(2, HD):
            for half in range(2):
                load_odd_slab(k, sp, h, half)

    def gpsimd(pool):
        wait_for(pool, x_ready)
        pool.dma_start(gain, row_piece(A["subln_g"], P)).then_inc(gain_in, 16)

    def tensor(pe):
        def project(h, part):
            n = 3 * h + part
            if n >= 2:
                pe.wait_ge(kept, n - 1)
            bank = 6 + n % 2
            slabs = k.odd_slabs[h]
            for half in range(2):
                if part == 0:
                    slab_ready(k, pe, slabs[half])
            view = [k.ring[:, sl[0], 0:1536].rearrange("p (k q n) -> p k q n", k=4, q=3) for sl in slabs]
            if part < 2:
                for c in range(KC):
                    mm = pe.matmul(PS[:, bank, :], view[c // 4][:, c % 4, part, :], k.XT[:, c, :],
                                   start=(c == 0), stop=(c == KC - 1))
            else:
                for t in range(NT):
                    for c in range(KC):
                        mm = pe.matmul(PS[:, bank, t * P:(t + 1) * P], k.XT[:, c, t * P:(t + 1) * P],
                                       view[c // 4][:, c % 4, 2, :], start=(c == 0), stop=(c == KC - 1))
                        if t == NT - 1 and c == 3:
                            mm.then_inc(k.freed[slabs[0][0]], 1)
            mm.then_inc(projected, 1)
            if part == 2:
                pe.drain().then_inc(k.freed[slabs[1][0]], 1)

        def score(h, i):
            n = 4 * h + i
            b = n % 2
            if n >= 2:
                pe.wait_ge(biased, n - 1)
            for r in range(2):
                rows = slice(64 * r, 64 * r + 64)
                mm = pe.matmul(PS[:, 2 * b + r, 0:(i + 1) * P], q[h % 2][rows, i * P:(i + 1) * P],
                               kk[h % 2][rows, 0:(i + 1) * P], start=True, stop=True)
            mm.then_inc(scored, 1)

        def turn_w(h, i):
            n = 4 * h + i
            pe.wait_ge(mixed, n + 1)
            if n > 0:
                pe.wait_ge(w_out, n)
            if i == 2:
                pe.wait_ge(y_out, h)
            for j in range(i + 1):
                mm = pe.transpose(PS[:, 4, j * P:(j + 1) * P], w[:, n % 2, j * P:(j + 1) * P], k.ident)
            mm.then_inc(w_turned, 1)

        def value(h, i):
            n = 4 * h + i
            pe.wait_ge(w_out, n + 1)
            pe.wait_ge(kept, 3 * h + 3)
            if i == 0 and h > 0:
                pe.wait_ge(squared, h)
            for j in range(i + 1):
                mm = pe.matmul(PS[:, 5, i * P:(i + 1) * P], wT[:, n % 2, j * P:(j + 1) * P],
                               v[h % 2][:, j, :], start=(j == 0), stop=(j == i))
            mm.then_inc(valued, 1)

        def turn_y(h):
            pe.wait_ge(normed, h + 1)
            pe.wait_ge(w_out, min(4 * h + 6, 4 * HD))
            for t in range(NT):
                mm = pe.transpose(PS[:, 4, t * P:(t + 1) * P], on[:, t, :], k.ident)
            mm.then_inc(y_turned, 1)

        wait_for(pe, xt_ready)
        for part in range(3):
            project(0, part)
        for h in range(HD):
            pe.wait_ge(kept, 3 * h + 2)
            more = [lambda part=part: project(h + 1, part) for part in range(3)] if h + 1 < HD else \
                [lambda: None] * 3
            score(h, 0)
            score(h, 1)
            if h > 0:
                turn_w(h - 1, 3)
                value(h - 1, 3)
            more[0]()
            turn_w(h, 0)
            score(h, 2)
            value(h, 0)
            turn_w(h, 1)
            score(h, 3)
            more[1]()
            if h > 0:
                turn_y(h - 1)
            value(h, 1)
            turn_w(h, 2)
            more[2]()
            value(h, 2)
        turn_w(HD - 1, 3)
        value(HD - 1, 3)
        turn_y(HD - 1)

    def scalar(act):
        def keep(h, part):
            act.wait_ge(projected, 3 * h + part + 1)
            src = PS[:, 6 + (3 * h + part) % 2, :]
            if part == 0:
                act.mul(q[h % 2], src, DH ** -0.5).then_inc(kept, 1)
            elif part == 1:
                act.copy(kk[h % 2], src).then_inc(kept, 1)
            else:
                act.copy(v[h % 2], src.rearrange("p (t n) -> p t n", t=NT)).then_inc(kept, 1)

        def rows(h, i):
            n = 4 * h + i
            L = (i + 1) * P
            act.wait_ge(negated, n + 1)
            if n >= 2:
                act.wait_ge(mixed, n - 1)
            for r in range(2):
                mm = act.activation(s[:, n % 2, r, 0:L], s[:, n % 2, r, 0:L], ACT.Exp,
                                    bias=col[:, n % 2, 2 + r:3 + r], accum_out=col[:, n % 2, 4 + r:5 + r])
            mm.then_inc(exped, 1)

        def leave_w(h, i):
            n = 4 * h + i
            act.wait_ge(w_turned, n + 1)
            if n >= 2:
                act.wait_ge(valued, n - 1)
            act.copy(wT[:, n % 2, 0:(i + 1) * P], PS[:, 4, 0:(i + 1) * P]).then_inc(w_out, 1)

        def leave_y(h):
            act.wait_ge(y_turned, h + 1)
            act.copy(YT[:, h, :], PS[:, 4, :]).then_inc(y_out, 1)

        def root(h):
            act.wait_ge(squared, h + 1)
            act.activation(k.stat[:, :, 9], k.stat[:, :, 8], ACT.Sqrt, bias=k.eps_ln).then_inc(rooted, 1)

        for part in range(3):
            keep(0, part)
        for h in range(HD):
            more = [lambda part=part: keep(h + 1, part) for part in range(3)] if h + 1 < HD else \
                [lambda: None] * 3
            if h > 0:
                leave_w(h - 1, 3)
            rows(h, 0)
            rows(h, 1)
            more[0]()
            leave_w(h, 0)
            if h > 0:
                root(h - 1)
            rows(h, 2)
            leave_w(h, 1)
            rows(h, 3)
            more[1]()
            if h > 0:
                leave_y(h - 1)
            leave_w(h, 2)
            more[2]()
        leave_w(HD - 1, 3)
        root(HD - 1)
        leave_y(HD - 1)

    def vector(dve):
        def add_bias(h, i):
            n = 4 * h + i
            L = (i + 1) * P
            b = n % 2
            dve.wait_ge(scored, n + 1)
            for r in range(2):
                dve.tensor_tensor_reduce(s[:, b, r, 0:L], PS[:, 2 * b + r, 0:L], bias[:, h, 512 - L:512],
                                         1.0, -3e38, ALU.add, ALU.max, col[:, b, r:r + 1])
            dve.drain().then_inc(biased, 1)
            dve.tensor_scalar(col[:, b, 2:4], col[:, b, 0:2], -1.0, None, ALU.mult).then_inc(negated, 1)

        def mix(h, i):
            n = 4 * h + i
            L = (i + 1) * P
            b = n % 2
            dve.wait_ge(exped, n + 1)
            dve.reciprocal(col[:, b, 6:8], col[:, b, 4:6])
            dve.drain()
            if n >= 2:
                dve.wait_ge(w_turned, n - 1)
            dve.tensor_scalar(col[:, b, 8:9], col[:, b, 7:8], k.lam[:, 5:6], None, ALU.mult)
            dve.tensor_scalar(w[:, b, 0:L], s[:, b, 0, 0:L], col[:, b, 6:7], None, ALU.mult)
            dve.drain()
            dve.scalar_tensor_tensor(w[:, b, 0:L], s[:, b, 1, 0:L], col[:, b, 8:9], w[:, b, 0:L],
                                     ALU.mult, ALU.add).then_inc(mixed, 1)

        def squares(h):
            dve.wait_ge(valued, 4 * h + 4)
            if h > 0:
                dve.wait_ge(y_turned, h)
            for t in range(NT):
                dve.tensor_copy(on[:, t, :], PS[:, 5, t * P:(t + 1) * P])
            dve.drain()
            for t in range(NT):
                mm = dve.tensor_tensor_reduce(junk, on[:, t, :], on[:, t, :], 1.0 / P, 0.0,
                                              ALU.mult, ALU.add, k.stat[:, t, 8:9])
                dve.drain()
            dve.drain().then_inc(squared, 1)

        def norm(h):
            dve.wait_ge(rooted, h + 1)
            dve.reciprocal(k.stat[:, :, 10], k.stat[:, :, 9])
            dve.drain()
            for t in range(NT):
                mm = dve.scalar_tensor_tensor(on[:, t, :], on[:, t, :], k.stat[:, t, 10:11], gain,
                                              ALU.mult, ALU.mult)
            mm.then_inc(normed, 1)

        dve.wait_ge(bias_in, 16 * HD)
        dve.wait_ge(gain_in, 16)
        dve.tensor_scalar(gain, gain, 1.0 - LAM_INIT, None, ALU.mult)
        for h in range(HD):
            if h > 0:
                mix(h - 1, 3)
            add_bias(h, 0)
            add_bias(h, 1)
            mix(h, 0)
            if h > 0:
                squares(h - 1)
            add_bias(h, 2)
            mix(h, 1)
            if h > 0:
                norm(h - 1)
            add_bias(h, 3)
            mix(h, 2)
        mix(HD - 1, 3)
        squares(HD - 1)
        norm(HD - 1)

    return dict(sync=sync, gpsimd=gpsimd, tensor=tensor, scalar=scalar, vector=vector)


def column_stage(k):
    A, W, PS = k.A, k.W, k.PS
    rows = k.rows[:, 1, 0:256].rearrange("p (a n) -> p a n", a=2)
    rows_in, turned = k.sem("col_rows"), k.sem("cols_turned")
    k.cols_in = k.sem("cols_in")

    def gpsimd(pool):
        for at, half, src in [(0, 0, A["conv_w_2"][0].rearrange("t (n p) -> (t n) p", p=P)),
                              (4 * CW, 0, A["conv_b_2"][0].rearrange("(n p) -> n p", p=P)),
                              (0, 1, A["qk_conv_w_2"][0].rearrange("t (n p) -> (t n) p", p=P)),
                              (32, 1, A["qk_conv_b_2"][0].rearrange("(n p) -> n p", p=P)),
                              (40, 1, A["b_in_2"][0, 0:2048].rearrange("(n p) -> n p", p=P))]:
            pool.dma_start(rows[at:at + src.shape[0], half, :], src).then_inc(rows_in, 16)

    def tensor(pe):
        pe.wait_ge(rows_in, 80)
        pe.transpose(PS[:, 6, 0:128], rows[:, 0, :], k.ident)
        pe.transpose(PS[:, 6, 128:184], rows[0:56, 1, :], k.ident[0:56, 0:56]).then_inc(turned, 1)

    def scalar(act):
        act.wait_ge(turned, 1)
        act.copy(k.chan[:], PS[:, 6, 0:184]).then_inc(k.cols_in, 1)

    return dict(gpsimd=gpsimd, tensor=tensor, scalar=scalar)


def hybrid_stage(k):
    A, W, PS = k.A, k.W, k.PS
    YT = W[:, 0:4096].rearrange("p (c n) -> p c n", c=KC)
    PAD = CW - 1
    u = W[:, 4096:6272].rearrange("p (c n) -> p c n", c=4)
    acc = W[:, 6272:8320].rearrange("p (c n) -> p c n", c=4)
    pre = W[:, 8320:9352].rearrange("p (q n) -> p q n", q=2)
    qk = W[:, 9352:10376].rearrange("p (q n) -> p q n", q=2)
    v = W[:, 10376:11432].rearrange("p (b t n) -> p b t n", b=2, t=NT)
    og = W[:, 11432:12456].rearrange("p (b t n) -> p b t n", b=2, t=NT)
    wt = W[:, 12456:13736]
    on = W[:, 13736:14248].rearrange("p (t n) -> p t n", t=NT)
    fl, t1, t2 = W[0:4, 12456:12968], W[0:4, 12968:13480], W[0:4, 13736:14248]
    negM = W[0:4, 14248:14760]
    sel = W[0:4, 14760:15272]
    arow = W[0:4, 15272:15784]
    acol = W[:, 15784:15800].rearrange("p (t h) -> p t h", t=NT)
    emcol = W[:, 15800:15816].rearrange("p (t h) -> p t h", t=NT)
    gw = W[:, 15816:15880].rearrange("p (k n) -> p k n", k=KC)
    gb = W[0:4, 15880:15882]
    sig = [W[:, 10376:10888], W[:, 11432:11944]]
    unorm = [W[:, 8320:8832], W[:, 8832:9344]]
    wide = k.chan[:, 0:124].rearrange("p (t n) -> p t n", n=4)
    wide_b = k.chan[:, 124:128]
    qk_w = k.chan[:, 128:160].rearrange("p (t n) -> p t n", n=8)
    qk_b, b_in = k.chan[:, 160:168], k.chan[:, 168:184]
    place = [(0, 0), (1, 0), (2, 0), (1, 384)]
    COL = [0, 512, 1024, 896]
    st = k.stat
    names = ("gate_w_in rows_in padded pair_done sig_done u_done g_done g_kept g_kept2 g_exp g_abs g_row "
             "g_em g_turned g_cols projected kept vo_raw og_done seeded convd qk_ready scored bcast "
             "exped cut weighted valued v_read varied rooted normed y_turned y_out acc_done c_turned "
             "c_varied c_rooted c_normed c_silu c_back c_out w_high split_used gw_split").split()
    s = Namespace()
    (s.gate_w_in, s.rows_in, s.padded, s.pair_done, s.sig_done, s.u_done, s.g_done, s.g_kept, s.g_kept2,
     s.g_exp, s.g_abs, s.g_row, s.g_em, s.g_turned, s.g_cols, s.projected, s.kept, s.vo_raw, s.og_done,
     s.seeded, s.convd, s.qk_ready, s.scored, s.bcast, s.exped, s.cut, s.weighted, s.valued, s.v_read,
     s.varied, s.rooted, s.normed, s.y_turned, s.y_out, s.acc_done, s.c_turned, s.c_varied, s.c_rooted,
     s.c_normed, s.c_silu, s.c_back, s.c_out, s.w_high, s.split_used, s.gw_split) = (k.sem("hy_" + n) for n in names)
    k.hy_y_out, k.hy_c_out = s.y_out, s.c_out
    xt_ready, x_ready = k.xt_ready, k.x_ready
    before = k.rows_used
    k.rows_used = (s.c_normed, 4)
    HL = 4
    order = [k.cv_slabs[0], None] + k.cv_slabs[1:] + [slab for pair in k.ml_slabs for slab in pair]
    GATES = 1
    pool_taps = [9, 12, 16, 19, 23]

    def high_w(act, g):
        slab_ready(k, act, order[g])
        if g >= SPLIT:
            act.wait_ge(s.split_used, g - SPLIT + 1)
        split_high(k, act, k.ring[:, order[g][0], :], k.split[:, g % SPLIT, 1, :], s.w_high)

    def low_w(pool, g):
        pool.wait_ge(s.w_high, g + 1 if g < GATES else g)
        split_low(pool, k.ring[:, order[g][0], :], k.split[:, g % SPLIT, 1, :],
                  k.split[:, g % SPLIT, 0, :]).then_inc(k.freed[order[g][0]], 1)

    def halves(pe, g):
        pe.wait_ge(k.freed[order[g][0]], order[g][1] + 1)
        return [k.split[:, g % SPLIT, high, :].rearrange("p (k n) -> p k n", k=KC) for high in (1, 0)]

    def product(pe, to, w, columns, rows=slice(0, S)):
        wh, wl = w
        for c in range(KC):
            for m, (part, high) in enumerate(((wh, 1), (wh, 0), (wl, 1))):
                mm = pe.matmul(to, part[:, c, columns], x_half(k, high)[:, c, rows],
                               start=(c == 0 and m == 0), stop=(c == KC - 1 and m == 2))
        return mm

    def sync(sp):
        w = A["w_in_2"][0]
        sp.dma_start(gw, columns(w, 3072, 8)).then_inc(s.gate_w_in, 16)
        for i in range(2):
            sp.dma_start(gb[:, i:i + 1], A["b_in_2"][0, 3072 + 4 * i:3076 + 4 * i]
                         .rearrange("(p o) -> p o", o=1)).then_inc(s.gate_w_in, 16)
        sp.dma_start(sel, A["c_sel"]).then_inc(s.gate_w_in, 16)
        for h in range(HL):
            for half in range(2):
                load_slab(k, sp, k.ml_slabs[h][half],
                          [columns(w, 1024 + h * P + 512 * part, P) for part in (2 * half, 2 * half + 1)])

    def gpsimd(pool):
        wait_for(pool, before)
        pool.dma_start(k.rows[:, 0, :], row_piece(A["b_in_2"][0, 2048:3072], D)).then_inc(s.rows_in, 16)
        pool.dma_start(k.rows[:, 1, 0:512], row_piece(A["conv_ln_g_2"][0], 512)).then_inc(s.rows_in, 16)
        pool.dma_start(k.rows[:, 1, 512:1024], row_piece(A["conv_ln_b_2"][0], 512)).then_inc(s.rows_in, 16)
        pool.dma_start(k.rows[:, 2, 0:512], row_piece(A["mlstm_norm_g_2"][0], 512)).then_inc(s.rows_in, 16)
        for g in range(3, 9):
            low_w(pool, g)
            if g == 7:
                convolve_on_pool(pool, 0, pool_taps[0])
        for h in range(HL):
            pool.wait_ge(s.exped, h + 1)
            for j in range(NT):
                d = wt[:, COL[j]:COL[j] + P]
                mm = pool.affine_select(out=d, in_=d, pattern=[[1, P]], compare_op=ALU.is_ge,
                                        fill=0.0, base=0, channel_multiplier=-1)
            mm.then_inc(s.cut, 1)
            if h < 2:
                low_w(pool, 9 + 2 * h)
                convolve_on_pool(pool, pool_taps[2 * h], pool_taps[2 * h + 1])
                low_w(pool, 10 + 2 * h)
                convolve_on_pool(pool, pool_taps[2 * h + 1], pool_taps[2 * h + 2])
            if h == 2:
                convolve_on_pool(pool, pool_taps[4], CW)

    def convolve_on_pool(pool, first, end):
        c, term = 2, k.rows[:, 2, 512:1024]
        if first == 0:
            pool.wait_ge(s.u_done, c + 1)
            pool.tensor_scalar(acc[:, c, :], u[:, c, PAD:PAD + S], wide[:, PAD, c:c + 1],
                               wide_b[:, c:c + 1], ALU.mult, ALU.add)
        for i in range(max(first, 1), end):
            pool.drain()
            pool.tensor_scalar(term, u[:, c, i - 1:i - 1 + S], wide[:, i - 1, c:c + 1], None, ALU.mult)
            pool.drain()
            mm = pool.tensor_tensor(acc[:, c, :], acc[:, c, :], term, ALU.add)
        if end == CW:
            mm.then_inc(s.acc_done, 1)

    def convolve(eng, c, first, end):
        if first == 0:
            eng.wait_ge(s.u_done, c + 1)
        eng.drain()
        for i in range(first, end):
            if i == 0:
                mm = eng.tensor_scalar(acc[:, c, :], u[:, c, PAD:PAD + S], wide[:, PAD, c:c + 1],
                                       wide_b[:, c:c + 1], ALU.mult, ALU.add)
            else:
                mm = eng.scalar_tensor_tensor(acc[:, c, :], u[:, c, i - 1:i - 1 + S], wide[:, i - 1, c:c + 1],
                                              acc[:, c, :], ALU.mult, ALU.add)
            if i < CW - 1:
                eng.drain()
        if end == CW:
            mm.then_inc(s.acc_done, 1)

    def tensor(pe):
        wait_for(pe, xt_ready)
        def channels(c):
            w = halves(pe, c if c == 0 else c + 1)
            if c > 1:
                pe.wait_ge(s.u_done, c - 1)
            for q in range(2):
                mm = product(pe, PS[:, 4 + 2 * (c % 2) + q, :], w, slice(q * P, q * P + P))
            mm.then_inc(s.pair_done, 1)
            pe.drain().then_inc(s.split_used, 1)

        channels(0)
        pe.wait_ge(s.gw_split, 1)
        w = [k.split[:, GATES, high, :].rearrange("p (k n) -> p k n", k=KC) for high in (1, 0)]
        for i in range(2):
            mm = product(pe, PS[:, 2 + i, :], w, slice(i * P, i * P + P))
        mm.then_inc(s.g_done, 1)
        pe.drain().then_inc(s.split_used, 1)
        for c in range(1, 4):
            channels(c)

        def project_qk(h):
            w = halves(pe, 5 + 2 * h)
            if h == 0:
                pe.wait_ge(s.u_done, 4)
            for part in range(2):
                if h > 0:
                    pe.wait_ge(s.kept, 2 * (h - 1) + part + 1)
                mm = product(pe, PS[:, 6 + part, :], w, slice(part * P, part * P + P))
                mm.then_inc(s.projected, 1)
            pe.drain().then_inc(s.split_used, 1)

        def project_vo(h):
            wh, wl = halves(pe, 6 + 2 * h)
            for t in range(NT):
                if h > 0:
                    pe.wait_ge(s.vo_raw, 2 * (h - 1) + t // 2 + 1)
                for c in range(KC):
                    for m, (high, w) in enumerate(((1, wh), (1, wl), (0, wh))):
                        mm = pe.matmul(PS[:, 4 + t // 2, 256 * (t % 2):256 * (t % 2) + 256],
                                       x_half(k, high)[:, c, t * P:(t + 1) * P], w[:, c, :],
                                       start=(c == 0 and m == 0), stop=(c == KC - 1 and m == 2))
            mm.then_inc(s.projected, 1)
            pe.drain().then_inc(s.split_used, 1)

        def turn_acc(t):
            if t > 1:
                pe.wait_ge(s.c_normed, t - 1)
            for c in range(4):
                mm = pe.transpose(PS[:, 6 + t % 2, c * P:(c + 1) * P], acc[:, c, t * P:(t + 1) * P], k.ident)
            mm.then_inc(s.c_turned, 1)

        def turn_y(h):
            if h > 0:
                pe.wait_ge(s.y_out, h)
            pe.wait_ge(s.normed, h + 1)
            for t in range(NT):
                mm = pe.transpose(PS[:, 1, t * P:(t + 1) * P], on[:, t, :], k.ident)
            mm.then_inc(s.y_turned, 1)

        project_qk(0)
        project_vo(0)
        pe.wait_ge(s.g_row, 1)
        for i, row in enumerate([arow, t1]):
            for t in range(NT):
                at = 16 * i + 4 * t
                mm = pe.transpose(PS[:, 2, at:at + 4], row[:, t * P:(t + 1) * P], k.ident[0:4, 0:4])
        mm.then_inc(s.g_turned, 1)
        pe.wait_ge(s.g_cols, 1)

        for h in range(HL):
            pe.wait_ge(s.qk_ready, 2 * h + 2)
            if h > 0:
                pe.wait_ge(s.v_read, h)
            if h > 1:
                pe.wait_ge(s.y_out, h - 1)
            pe.matmul(PS[:, 3, :], sel[:, h * P:(h + 1) * P], negM, start=True, stop=True).then_inc(s.bcast, 1)
            for j in range(NT):
                bank, col = place[j]
                n = S - j * P
                mm = pe.matmul(PS[:, bank, col:col + n], qk[:, 1, j * P:(j + 1) * P], qk[:, 0, j * P:S],
                               start=True, stop=True)
            mm.then_inc(s.scored, 1)
            if h + 1 < HL:
                project_qk(h + 1)
            else:
                pe.wait_ge(s.kept, 2 * HL)
                pe.wait_ge(s.acc_done, 4)
                turn_acc(0)
                turn_acc(1)
            pe.wait_ge(s.weighted, h + 1)
            for i in range(NT):
                for j in range(i + 1):
                    at = COL[j] + (i - j) * P
                    mm = pe.matmul(PS[:, 3 - 3 * (i // 2), 256 * (i % 2):256 * (i % 2) + 129], wt[:, at:at + P],
                                   v[:, h % 2, j, 0:129], start=(j == 0), stop=(j == i))
            mm.then_inc(s.valued, 1)
            if h > 0:
                turn_y(h - 1)
            if h + 1 < HL:
                project_vo(h + 1)
        turn_back(pe, 0)
        turn_acc(2)
        turn_back(pe, 1)
        turn_acc(3)
        turn_y(HL - 1)

    def turn_back(pe, t):
        pe.wait_ge(s.c_silu, t + 1)
        if t > 1:
            pe.wait_ge(s.c_out, t - 1)
        if t == 0:
            pe.wait_ge(s.vo_raw, 8)
        for c in range(4):
            mm = pe.transpose(PS[:, 4 + t % 2, c * P:(c + 1) * P], unorm[t % 2][:, c * P:(c + 1) * P], k.ident)
        mm.then_inc(s.c_back, 1)

    def beside(pe, t):
        if t == 1:
            turn_back(pe, 2)
            turn_back(pe, 3)
            pe.wait_ge(s.c_out, NT)
        pe.wait_ge(s.c_out, t + 1)

    k.beside = beside

    def scalar(act):
        def keep(h):
            for part in range(2):
                act.wait_ge(s.projected, 3 * h + part + 1)
                if h > 0:
                    act.wait_ge(s.convd, 2 * (h - 1) + part + 1)
                else:
                    act.wait_ge(s.padded, 1)
                act.activation(pre[:, part, 3:515], PS[:, 6 + part, :], ACT.Identity,
                               bias=b_in[:, 8 + 4 * part + h:9 + 4 * part + h]).then_inc(s.kept, 1)

        def root(t):
            act.wait_ge(s.c_varied, t + 1)
            act.activation(st[:, t, 14:15], st[:, t, 7:8], ACT.Sqrt, bias=k.eps_rms).then_inc(s.c_rooted, 1)

        def silu_c(t):
            act.wait_ge(s.c_normed, t + 1)
            act.activation(unorm[t % 2], unorm[t % 2], ACT.Silu).then_inc(s.c_silu, 1)

        def leave_back(t):
            act.wait_ge(s.c_back, t + 1)
            act.copy(YT[:, 0:4, t * P:(t + 1) * P],
                     PS[:, 4 + t % 2, :].rearrange("p (c n) -> p c n", c=4)).then_inc(s.c_out, 1)

        def leave_y(h):
            act.wait_ge(s.y_turned, h + 1)
            act.copy(YT[:, 4 + h, :], PS[:, 1, :]).then_inc(s.y_out, 1)

        def silu_qk(h):
            for part in range(2):
                act.wait_ge(s.convd, 2 * h + part + 1)
                act.activation(qk[:, part, :], qk[:, part, :], ACT.Silu).then_inc(s.qk_ready, 1)

        def sigmoid(c):
            act.wait_ge(s.pair_done, c + 1)
            if c > 1:
                act.wait_ge(s.u_done, c - 1)
            act.activation(sig[c % 2], PS[:, 5 + 2 * (c % 2), :], ACT.Sigmoid,
                           bias=b_in[:, 4 + c:5 + c]).then_inc(s.sig_done, 1)

        high_w(act, 0)
        high_w(act, 2)
        sigmoid(0)
        high_w(act, 3)
        act.wait_ge(s.g_done, 1)
        act.wait_ge(s.gate_w_in, 64)
        act.activation(arow, PS[0:4, 2, :], ACT.Identity, bias=gb[:, 0:1]).then_inc(s.g_kept, 1)
        act.activation(fl, PS[0:4, 3, :], ACT.Identity, bias=gb[:, 1:2]).then_inc(s.g_kept2, 1)
        act.drain()
        act.activation(t1, fl, ACT.Abs)
        act.drain()
        act.activation(t1, t1, ACT.Exp, scale=-1.0)
        act.drain()
        act.activation(t1, t1, ACT.Ln, bias=1.0).then_inc(s.g_abs, 1)
        high_w(act, 4)
        for c in range(1, 4):
            sigmoid(c)
            high_w(act, 4 + c)
        keep(0)
        high_w(act, 8)
        act.wait_ge(s.g_em, 1)
        act.activation(t1, t2, ACT.Exp, scale=-1.0).then_inc(s.g_row, 1)
        act.wait_ge(s.g_turned, 1)
        act.copy(W[:, 15784:15816], PS[:, 2, 0:32]).then_inc(s.g_cols, 1)
        act.wait_ge(s.vo_raw, 2)
        act.activation(og[:, 0, :, :], og[:, 0, :, :], ACT.Sigmoid).then_inc(s.og_done, 1)
        silu_qk(0)
        for h in range(HL):
            act.wait_ge(s.bcast, h + 1)
            if h > 0:
                act.wait_ge(s.valued, h)
            for j in range(NT):
                n = S - j * P
                mm = act.activation(wt[:, COL[j]:COL[j] + n], PS[:, 3, j * P:S], ACT.Exp,
                                    bias=acol[:, j, h:h + 1])
            mm.then_inc(s.exped, 1)
            if h + 2 < HL:
                high_w(act, 9 + 2 * h)
            if h + 1 < HL:
                keep(h + 1)
                if h + 2 < HL:
                    high_w(act, 10 + 2 * h)
                silu_qk(h + 1)
            else:
                root(0)
                root(1)
                silu_c(0)
                silu_c(1)
            act.wait_ge(s.varied, h + 1)
            act.activation(st[:, :, 14], st[:, :, 7], ACT.Sqrt, bias=k.eps_rms).then_inc(s.rooted, 1)
            if h > 0:
                leave_y(h - 1)
            if h + 1 < HL:
                act.wait_ge(s.vo_raw, 2 * h + 4)
                act.activation(og[:, (h + 1) % 2, :, :], og[:, (h + 1) % 2, :, :], ACT.Sigmoid).then_inc(s.og_done, 1)
        leave_back(0)
        leave_back(1)
        leave_y(HL - 1)
        for t in range(2, NT):
            root(t)
            silu_c(t)
        leave_back(2)
        leave_back(3)

    def vector(dve):
        def make_u(c):
            dve.wait_ge(s.sig_done, c + 1)
            dve.scalar_tensor_tensor(u[:, c, PAD:PAD + S], PS[:, 4 + 2 * (c % 2), :], b_in[:, c:c + 1],
                                     sig[c % 2], ALU.add, ALU.mult).then_inc(s.u_done, 1)

        def bc(ap):
            return bass.AP(tensor=ap.tensor, offset=ap.offset, ap=[list(ap.ap[0]), [0, 2], list(ap.ap[1])])

        def convolve_qk(h):
            for part in range(2):
                dve.wait_ge(s.kept, 2 * h + part + 1)
                if h > 0:
                    dve.wait_ge(s.scored, h)
                ch = 4 * part + h
                dve.tensor_scalar(qk[:, part, :], pre[:, part, 3:515], qk_w[:, 3, ch:ch + 1],
                                  qk_b[:, ch:ch + 1], ALU.mult, ALU.add)
                for tap in range(3):
                    dve.drain()
                    mm = dve.scalar_tensor_tensor(qk[:, part, :], pre[:, part, tap:tap + S],
                                                  qk_w[:, tap, ch:ch + 1], qk[:, part, :], ALU.mult, ALU.add)
                mm.then_inc(s.convd, 1)

        def keep_vo(h):
            dve.wait_ge(s.projected, 3 * h + 3)
            for half in range(2):
                src = PS[:, 4 + half, :].rearrange("p (t n) -> p t n", t=2)
                dve.tensor_tensor(v[:, h % 2, 2 * half:2 * half + 2, 0:P], src[:, :, 0:P],
                                  bc(k.rows[:, 0, h * P:(h + 1) * P]), ALU.add)
                dve.tensor_tensor(og[:, h % 2, 2 * half:2 * half + 2, :], src[:, :, P:2 * P],
                                  bc(k.rows[:, 0, 512 + h * P:512 + (h + 1) * P]), ALU.add)\
                   .then_inc(s.vo_raw, 1)

        def norm_c(t):
            bank = PS[:, 6 + t % 2, :]
            dve.wait_ge(s.c_turned, t + 1)
            dve.bn_stats(st[:, t, 0:6], bank)
            dve.drain()
            dve.bn_aggr(st[:, t, 6:8], st[:, t, 0:6]).then_inc(s.c_varied, 1)
            dve.wait_ge(s.c_rooted, t + 1)
            dve.reciprocal(st[:, t, 15:16], st[:, t, 14:15])
            dve.drain()
            if t > 1:
                dve.wait_ge(s.c_back, t - 1)
            dve.tensor_scalar(unorm[t % 2], bank, st[:, t, 6:7], st[:, t, 15:16], ALU.subtract, ALU.mult)
            dve.drain()
            dve.tensor_tensor(unorm[t % 2], unorm[t % 2], k.rows[:, 1, 0:512], ALU.mult)
            dve.drain()
            dve.tensor_tensor(unorm[t % 2], unorm[t % 2], k.rows[:, 1, 512:1024], ALU.add).then_inc(s.c_normed, 1)

        low_w(dve, 0)
        zero = W[:, 6272:8320]
        dve.memset(zero, 0.0)
        dve.drain()
        for high in range(2):
            dve.tensor_copy(k.split[:, GATES, high, :], zero)
        dve.wait_ge(s.gate_w_in, 64)
        dve.drain()
        gwv = gw.rearrange("p k (i n) -> p k i n", i=2)
        wide_g = [k.split[:, GATES, high, :].rearrange("p (k i n) -> p k i n", k=KC, i=2)[:, :, :, 0:4]
                  for high in (0, 1)]
        for i in range(2):
            dve.tensor_copy(wide_g[1][:, :, i, :], gwv[:, :, i, :])
        dve.drain()
        for i in range(2):
            mm = split_low(dve, gwv[:, :, i, :], wide_g[1][:, :, i, :], wide_g[0][:, :, i, :])
        mm.then_inc(s.gw_split, 1)
        low_w(dve, 2)
        dve.wait_ge(s.rows_in, 64)
        dve.memset(u[:, :, 0:PAD], 0.0)
        dve.memset(pre[:, :, 0:3], 0.0).then_inc(s.padded, 1)
        make_u(0)
        dve.wait_ge(s.g_abs, 1)
        dve.scalar_tensor_tensor(fl, fl, 0.0, t1, ALU.min, ALU.subtract)
        dve.drain()
        dve.tensor_tensor_scan(t2, fl, fl, 0.0, ALU.add, ALU.bypass)
        dve.drain()
        dve.tensor_tensor(arow, arow, t2, ALU.subtract)
        dve.drain()
        dve.tensor_tensor_scan(fl, arow, arow, 0.0, ALU.max, ALU.max)
        dve.drain()
        dve.tensor_scalar(negM, fl, -1.0, None, ALU.mult)
        dve.tensor_tensor(t2, t2, fl, ALU.add)
        dve.drain().then_inc(s.g_em, 1)
        make_u(1)
        convolve(dve, 0, 0, 11)
        make_u(2)
        convolve(dve, 0, 11, 22)
        make_u(3)
        convolve(dve, 0, 22, CW)
        convolve(dve, 1, 0, 8)
        dve.drain()
        dve.memset(v[:, :, :, P:P + 1], 1.0)
        convolve_qk(0)
        convolve(dve, 1, 8, 16)
        keep_vo(0)
        convolve(dve, 1, 16, CW)
        for h in range(HL):
            dve.wait_ge(s.scored, h + 1)
            dve.wait_ge(s.cut, h + 1)
            zz = PS[:, 0:3, :].rearrange("p b n -> p (b n)")[:, 0:CAUSAL]
            dve.scalar_tensor_tensor(wt, zz, P ** -0.5, wt, ALU.mult, ALU.mult).then_inc(s.weighted, 1)
            if h + 1 < HL:
                convolve_qk(h + 1)
                convolve(dve, 3, 11 * h, min(11 * h + 11, CW))
            else:
                norm_c(0)
                norm_c(1)
            dve.wait_ge(s.valued, h + 1)
            if h > 0:
                dve.wait_ge(s.y_turned, h)
            dve.wait_ge(s.og_done, h + 1)
            for t in range(NT):
                o = PS[:, 3 - 3 * (t // 2), 256 * (t % 2):256 * (t % 2) + 129]
                dve.tensor_copy(st[:, t, 8:9], o[:, P:P + 1])
            dve.drain()
            dve.scalar_tensor_tensor(st[:, :, 8], st[:, :, 8], -1.0, st[:, :, 8], ALU.mult, ALU.max)
            dve.drain()
            dve.tensor_tensor(st[:, :, 8], st[:, :, 8], emcol[:, :, h], ALU.max)
            dve.drain()
            dve.reciprocal(st[:, :, 9], st[:, :, 8])
            dve.drain()
            for t in range(NT):
                o = PS[:, 3 - 3 * (t // 2), 256 * (t % 2):256 * (t % 2) + 128]
                mm = dve.scalar_tensor_tensor(on[:, t, :], o, st[:, t, 9:10], og[:, h % 2, t, :],
                                              ALU.mult, ALU.mult)
            mm.then_inc(s.v_read, 1)
            dve.drain()
            for t in range(NT):
                dve.bn_stats(st[:, t, 0:6], on[:, t, :])
            dve.drain()
            for t in range(NT):
                mm = dve.bn_aggr(st[:, t, 6:8], st[:, t, 0:6])
            mm.then_inc(s.varied, 1)
            dve.wait_ge(s.rooted, h + 1)
            dve.reciprocal(st[:, :, 15], st[:, :, 14])
            dve.drain()
            for t in range(NT):
                dve.tensor_scalar(on[:, t, :], on[:, t, :], st[:, t, 6:7], st[:, t, 15:16], ALU.subtract, ALU.mult)
            dve.drain()
            for t in range(NT):
                mm = dve.tensor_tensor(on[:, t, :], on[:, t, :], k.rows[:, 2, h * P:(h + 1) * P], ALU.mult)
            mm.then_inc(s.normed, 1)
            if h + 1 < HL:
                keep_vo(h + 1)
        norm_c(2)
        norm_c(3)

    return dict(sync=sync, gpsimd=gpsimd, tensor=tensor, scalar=scalar, vector=vector)


NB = 42


def along(ap, n):
    return bass.AP(tensor=ap.tensor, offset=ap.offset, ap=[list(x) for x in ap.ap] + [[0, n]])


def across(ap, n):
    return bass.AP(tensor=ap.tensor, offset=ap.offset, ap=[list(ap.ap[0]), [0, n]] + [list(x) for x in ap.ap[1:]])


YB = 40


def clear_stage(k):
    k.y_rows = k.dram("expert_rows", (YB * P, D))
    zeroed, out = k.sem("rows_zeroed"), k.sem("expert_rows_zeroed")
    zero = k.rows[:, 2, :]

    def vector(dve):
        dve.memset(zero, 0.0).then_inc(zeroed, 1)

    def gpsimd(pool):
        pool.wait_ge(zeroed, 1)
        for n in range(8, YB, 8):
            to = k.y_rows[n * P:(n + 8) * P, :].rearrange("(n p) c -> p n c", p=P)
            pool.dma_start(to, across(zero, 8)).then_inc(out, 16)
        pool.wait_ge(out, 16 * (YB // 8 - 1))

    return dict(vector=vector, gpsimd=gpsimd)


def moe_stages(k):
    A, W, PS, X = k.A, k.W, k.PS, k.X
    st = k.stat
    h = W[:, 4096:8192].rearrange("p (t n) -> p t n", t=NT)
    base = [8704]

    def room(n):
        base[0] += n
        return W[:, base[0] - n:base[0]]

    def tiled(n):
        return room(NT * n).rearrange("p (t n) -> p t n", t=NT)

    rw = room(8 * 36).rearrange("p (k n) -> p k n", k=KC)
    rb = room(36)
    iota = room(64)
    e_iota, g_iota, tokf = iota[:, 0:32], iota[:, 32:40], iota[:, 40:44]
    L, work, one1, one2, both, neg, dest = (tiled(n) for n in (36, 32, 32, 32, 32, 32, 32))
    gexp = tiled(4)
    gid = room(32)
    cnt, nblk, ends, first = (room(32) for _ in range(4))
    gmax, gsum, gidx, m1, e1, m2, e2, ex, g1, g2, pg, tmp4 = (room(4) for _ in range(12))
    destf = room(8)
    dest_i, place_i = room(8).bitcast(I32), room(8).bitcast(I32)
    blk, placef = room(8), room(8)
    tok_i = room(4).bitcast(I32)
    bid = room(NB)
    cmpb = room(NB * 32)
    bef = room(NB + 2)
    be_i = room(NB + 2).bitcast(I32)
    idx = room(NB).bitcast(I32)
    idxcol = room(2).bitcast(I32)
    zeros = room(NB).bitcast(I32)
    assert base[0] <= 16128
    xg = [W[:, 1024 * b:1024 * b + 1024] for b in range(2)]
    xT = [W[:, 2048 + 1024 * b:3072 + 1024 * b].rearrange("p (c n) -> p c n", c=KC) for b in range(2)]
    silu = W[:, 4096:4608]
    mid = [W[:, 4608 + 512 * b:5120 + 512 * b] for b in range(2)]
    midT = [W[:, 5632 + 512 * b:6144 + 512 * b].rearrange("p (c n) -> p c n", c=4) for b in range(2)]
    ys = [W[:, 6656 + 1024 * b:7680 + 1024 * b] for b in range(2)]
    h_rows = k.dram("h_rows", (S, D))
    slot_tok = k.dram("slot_tokens", (NB * P, 1), I32)
    y_rows = k.y_rows
    names = ("h_saved table_in logits ranked gexp ex ready placed zeroed zero_out scattered idx_in "
             "x_in0 x_in1 x_turned x_out silued mid mid_turned mid_out y_kept y_saved y_free "
             "found0 found1 found2 found3 combined rooted final out_saved0 out_saved1 out_saved2 out_saved3 "
             "gain_in").split()
    s = Namespace()
    (s.h_saved, s.table_in, s.logits, s.ranked, s.gexp, s.ex, s.ready, s.placed, s.zeroed, s.zero_out,
     s.scattered, s.idx_in, s.x_in0, s.x_in1, s.x_turned, s.x_out, s.silued, s.mid,
     s.mid_turned, s.mid_out, s.y_kept, s.y_saved, s.y_free, s.found0, s.found1, s.found2,
     s.found3, s.combined, s.rooted, s.final, s.out_saved0, s.out_saved1, s.out_saved2, s.out_saved3,
     s.gain_in) = (k.sem("moe_" + n) for n in names)
    x_in = [s.x_in0, s.x_in1]
    found = [s.found0, s.found1, s.found2, s.found3]
    out_saved = [s.out_saved0, s.out_saved1, s.out_saved2, s.out_saved3]
    normed, product_1 = k.tail.normed, k.tail.product
    xt_ready, rows_before = k.xt_ready, k.rows_used
    slabs = k.moe_slabs
    AX = mybir.AxisListType

    def done(eng, slot, turn):
        eng.wait_ge(k.freed[slot], turn + slabs[slot][1] + 1)

    def pairs(eng):
        eng.wait_ge(s.placed, 1)
        return eng.value_load(be_i[0:1, NB:NB + 1], min_val=4, max_val=20)

    def route_sync(sp):
        sp.wait_ge(product_1, 2)
        sp.dma_start(rw[:, :, 0:4], columns(A["router_group_w_2"][0], 0, 4)).then_inc(s.table_in, 16)
        sp.dma_start(rw[:, :, 4:36], columns(A["router_expert_w_2"][0], 0, 32)).then_inc(s.table_in, 16)
        sp.dma_start(rb[:, 0:4], row_piece(A["router_group_b_2"][0], 4)).then_inc(s.table_in, 16)
        sp.dma_start(rb[:, 4:36], row_piece(A["router_expert_b_2"][0], 32)).then_inc(s.table_in, 16)
        sp.dma_start(iota, A["c_iota"]).then_inc(s.table_in, 16)
        for t in range(NT):
            sp.wait_ge(normed, t + 1)
            sp.dma_start(h_rows[t * P:(t + 1) * P, :], h[:, t, :]).then_inc(s.h_saved, 16)
        sp.wait_ge(s.zeroed, 1)
        sp.dma_start(slot_tok.rearrange("(p n) o -> p (n o)", p=P), zeros).then_inc(s.zero_out, 16)

    def route_tensor(pe):
        pe.wait_ge(*xt_ready)
        pe.wait_ge(s.table_in, 80)
        for t in range(NT):
            for c in range(KC):
                mm = pe.matmul(PS[:, 6, 36 * t:36 * t + 36], k.XT[:, c, t * P:(t + 1) * P], rw[:, c, :],
                               start=(c == 0), stop=(c == KC - 1))
        mm.then_inc(s.logits, 1)
        pe.wait_ge(s.ready, 1)
        for t in range(NT):
            mm = pe.matmul(PS[:, 7, 32 * t:32 * t + 32], k.before, both[:, t, :], start=True, stop=(t == 0))
            for t2 in range(t):
                mm = pe.matmul(PS[:, 7, 32 * t:32 * t + 32], k.negone, neg[:, t2, :],
                               start=False, stop=(t2 == t - 1))
        for t in range(NT):
            mm = pe.matmul(PS[:, 7, 128:160], k.negone, neg[:, t, :], start=(t == 0), stop=(t == NT - 1))
        mm.then_inc(s.ranked, 1)

    def route_scalar(act):
        act.wait_ge(s.gexp, 1)
        act.activation(gexp, gexp, ACT.Exp).then_inc(s.gexp, 1)
        act.wait_ge(s.ex, 1)
        act.activation(ex, ex, ACT.Exp).then_inc(s.ex, 1)

    def route_vector(dve):
        dve.drain()
        dve.memset(zeros, 0).then_inc(s.zeroed, 1)
        dve.wait_ge(s.table_in, 80)
        dve.wait_ge(s.logits, 1)
        dve.tensor_tensor(L, PS[:, 6, 0:144].rearrange("p (t n) -> p t n", t=NT), across(rb, NT), ALU.add)
        dve.tensor_copy(tok_i, tokf)
        dve.tensor_scalar(gid, e_iota, 8.0, None, ALU.is_ge)
        dve.drain()
        for edge in (16.0, 24.0):
            dve.scalar_tensor_tensor(gid, e_iota, edge, gid, ALU.is_ge, ALU.add)
            dve.drain()
        G, E = L[:, :, 0:4], L[:, :, 4:36]
        dve.tensor_reduce(gmax, G, AX.X, ALU.max)
        dve.drain()
        dve.tensor_tensor(gexp, G, along(gmax, 4), ALU.subtract).then_inc(s.gexp, 1)
        w4 = work[:, :, 0:4]
        dve.tensor_tensor(w4, G, along(gmax, 4), ALU.is_equal)
        dve.drain()
        dve.scalar_tensor_tensor(w4, w4, -1000.0, across(g_iota[:, 0:4], NT), ALU.mult, ALU.add)
        dve.drain()
        dve.tensor_reduce(gidx, w4, AX.X, ALU.min)
        dve.drain()
        dve.tensor_scalar(gidx, gidx, 1000.0, None, ALU.add)
        dve.drain()
        dve.tensor_tensor(work, across(gid, NT), along(gidx, 32), ALU.not_equal)
        dve.drain()
        dve.scalar_tensor_tensor(E, work, NEG, E, ALU.mult, ALU.add)
        for m, e, one in ((m1, e1, one1), (m2, e2, one2)):
            dve.drain()
            dve.tensor_reduce(m, E, AX.X, ALU.max)
            dve.drain()
            dve.tensor_tensor(work, E, along(m, 32), ALU.is_equal)
            dve.drain()
            dve.scalar_tensor_tensor(work, work, -1000.0, across(e_iota, NT), ALU.mult, ALU.add)
            dve.drain()
            dve.tensor_reduce(e, work, AX.X, ALU.min)
            dve.drain()
            dve.tensor_scalar(e, e, 1000.0, None, ALU.add)
            dve.drain()
            dve.tensor_tensor(one, across(e_iota, NT), along(e, 32), ALU.is_equal)
            dve.drain()
            dve.scalar_tensor_tensor(E, one, 2 * NEG, E, ALU.mult, ALU.add)
        dve.tensor_tensor(both, one1, one2, ALU.add)
        dve.drain()
        dve.tensor_scalar(neg, both, -1.0, None, ALU.mult).then_inc(s.ready, 1)
        dve.tensor_tensor(ex, m2, m1, ALU.subtract).then_inc(s.ex, 1)
        dve.wait_ge(s.gexp, 2)
        dve.tensor_reduce(gsum, gexp, AX.X, ALU.add)
        dve.wait_ge(s.ex, 2)
        dve.tensor_scalar(tmp4, ex, 1.0, None, ALU.add)
        dve.drain()
        dve.tensor_tensor(tmp4, tmp4, gsum, ALU.mult)
        dve.drain()
        dve.reciprocal(g1, tmp4)
        dve.drain()
        dve.tensor_tensor(g2, g1, ex, ALU.mult)
        dve.wait_ge(s.ranked, 1)
        dve.tensor_copy(cnt, PS[:, 7, 128:160])
        dve.drain()
        dve.tensor_scalar(nblk, cnt, 0.5, None, ALU.is_gt)
        for m in range(1, 4):
            dve.drain()
            dve.scalar_tensor_tensor(nblk, cnt, 128.0 * m + 0.5, nblk, ALU.is_gt, ALU.add)
        dve.drain()
        dve.tensor_tensor_scan(ends, nblk, nblk, 0.0, ALU.add, ALU.bypass)
        dve.drain()
        dve.tensor_tensor(first, ends, nblk, ALU.subtract)
        dve.drain()
        dve.tensor_scalar(first, first, 128.0, None, ALU.mult)
        dve.drain()
        dve.tensor_tensor(dest, PS[:, 7, 0:128].rearrange("p (t n) -> p t n", t=NT), across(first, NT), ALU.add)
        for j, one in ((0, one1), (1, one2)):
            dve.drain()
            dve.tensor_tensor(work, dest, one, ALU.mult)
            dve.drain()
            dve.tensor_reduce(destf[:, 4 * j:4 * j + 4], work, AX.X, ALU.add)
        dve.drain()
        dve.tensor_copy(dest_i, destf)
        dve.tensor_scalar(blk, destf, 1.0 / P, -127.0 / 256, ALU.mult, ALU.add)
        dve.drain()
        dve.tensor_scalar(blk, blk, 12582912.0, None, ALU.add)
        dve.drain()
        dve.tensor_scalar(blk, blk, 12582912.0, float(1 - P * NB), ALU.subtract, ALU.mult)
        dve.drain()
        dve.scalar_tensor_tensor(placef, destf, float(NB), blk, ALU.mult, ALU.add)
        dve.drain()
        dve.tensor_copy(place_i, placef).then_inc(s.ready, 1)
        for b in range(NB):
            dve.tensor_scalar(cmpb[:, 32 * b:32 * b + 32], ends, float(b), None, ALU.is_le)
        dve.tensor_scalar(bid[:, 0:20], e_iota[:, 0:20], 2.0, None, ALU.mult)
        dve.drain()
        dve.tensor_reduce(bef[:, 0:NB], cmpb.rearrange("p (b e) -> p b e", e=32), AX.X, ALU.add)
        dve.tensor_scalar(bid[:, 0:20], bid[:, 0:20], ends[:, 31:32], None, ALU.is_lt)
        dve.drain()
        dve.tensor_scalar(bef[:, 0:NB], bef[:, 0:NB], float(NE - 1), None, ALU.min)
        dve.tensor_reduce(bef[:, NB:NB + 1], bid[:, 0:20], AX.X, ALU.add)
        dve.drain()
        dve.tensor_copy(be_i[:, 0:NB + 1], bef[:, 0:NB + 1]).then_inc(s.placed, 1)

    def route_gpsimd(pool):
        pool.dma_start(k.rows[:, 1, :], row_piece(A["final_norm_g_2"], D)).then_inc(s.gain_in, 16)
        pool.wait_ge(s.ready, 2)
        pool.wait_ge(s.zero_out, 16)
        for j in range(2):
            for t in range(NT):
                pool.indirect_dma_start(slot_tok, bass.IndirectOffsetOnAxis(
                    ap=place_i[:, 4 * j + t:4 * j + t + 1].bitcast(U32), axis=0),
                    tok_i[:, t:t + 1], None).then_inc(s.scattered, 16)
        pool.wait_ge(s.scattered, 128)
        pool.dma_start(idx, slot_tok.rearrange("(p n) o -> p (n o)", p=P)).then_inc(s.idx_in, 16)
        pool.wait_ge(s.idx_in, 16)
        pool.wait_ge(s.h_saved, 64)

    def experts_sync(sp):
        n = pairs(sp)
        sp.wait_ge(s.idx_in, 16)
        wg = A["expert_w_gate_2"][0].rearrange("e (k p) n -> e p k n", p=P)
        wu = A["expert_w_up_2"][0].rearrange("e (k p) n -> e p k n", p=P)
        wd = A["expert_w_down_2"][0].rearrange("e (k p) n -> e p k n", p=P)
        with sp.Fori(0, n) as i:
            for b in range(2):
                e = sp.value_load(be_i[0:1, bass.ds(2 * i + b, 1)], min_val=0, max_val=NE - 1)
                for m, (w, nk) in enumerate(((wg, 4), (wg, 4), (wu, 4), (wu, 4), (wd, 2), (wd, 2))):
                    half = m % 2
                    src = w[bass.ds(e, 1), :, nk * half:nk * half + nk, :].rearrange("e p k n -> (e p) k n")
                    load_slab(k, sp, slabs[6 * b + m], [src], i)

    def experts_gpsimd(pool):
        pool.sem_inc(s.y_free, 1)

        def gather(b, n):
            pool.tensor_copy(idxcol[:, b:b + 1], idx[:, bass.ds(n, 1)])
            pool.drain()
            pool.indirect_dma_start(xg[b], None, h_rows, bass.IndirectOffsetOnAxis(
                ap=idxcol[:, b:b + 1].bitcast(U32), axis=0)).then_inc(x_in[b], 16)

        for b in range(2):
            pool.indirect_dma_start(xg[b], None, h_rows, bass.IndirectOffsetOnAxis(
                ap=idx[:, b:b + 1].bitcast(U32), axis=0)).then_inc(x_in[b], 16)
        n = pairs(pool)
        with pool.Fori(0, n) as i:
            for b in range(2):
                pool.wait_ge(s.x_turned, 4 * i + 2 * b + 2)
                pool.wait_ge(x_in[b], 16 * i + 16)
                gather(b, 2 * i + 2 + b)
            for b in range(2):
                pool.wait_ge(s.y_kept, 2 * i + b + 2)
                pool.dma_start(y_rows[bass.ds((2 * i + b) * P, P), :], ys[b]).then_inc(s.y_saved, 16)
            for b in range(2):
                pool.wait_ge(x_in[b], 16 * i + 32)
            pool.wait_ge(s.y_saved, 32 * i + 32)
            pool.sem_inc(s.y_free, 1)

    def experts_tensor(pe):
        n = pairs(pe)
        with pe.Fori(0, n) as i:
            def turn_x(b):
                pe.wait_ge(x_in[b], 16 * i + 16)
                for half in range(2):
                    pe.wait_ge(s.x_out, 4 * i + (2 * b + half if b else 1))
                    if b == 0:
                        pe.wait_ge(s.mid_out, 2 * i + 1)
                    for c in range(4):
                        at = (4 * half + c) * P
                        mm = pe.transpose(PS[:, 6 + half, c * P:(c + 1) * P], xg[b][:, at:at + P], k.ident)
                    mm.then_inc(s.x_turned, 1)

            def product(b, m):
                for half in range(2):
                    slab = slabs[6 * b + 2 * m + half]
                    slab_ready(k, pe, slab, i)
                    pe.wait_ge(s.x_out, 4 * i + 2 * b + half + 2)
                    w = k.ring[:, slab[0], :].rearrange("p (k n) -> p k n", k=4)
                    for c in range(4):
                        mm = pe.matmul(PS[:, 2 * b + m, :], xT[b][:, 4 * half + c, :], w[:, c, :],
                                       start=(half == 0 and c == 0), stop=(half == 1 and c == 3))
                    mm.then_inc(k.freed[slab[0]], 1)

            def turn_mid(b):
                pe.wait_ge(s.mid, 2 * i + b + 2)
                for c in range(4):
                    mm = pe.transpose(PS[:, 6 + b, c * P:(c + 1) * P], mid[b][:, c * P:(c + 1) * P], k.ident)
                mm.then_inc(s.mid_turned, 1)

            def down(b):
                pe.wait_ge(s.mid_out, 2 * i + b + 2)
                if b == 0:
                    pe.wait_ge(s.y_kept, 2 * i + 1)
                for half in range(2):
                    slab = slabs[6 * b + 4 + half]
                    slab_ready(k, pe, slab, i)
                    w = k.ring[:, slab[0], :].rearrange("p (k n) -> p k n", k=2)
                    for c in range(2):
                        for side in range(2):
                            bank = (4 if b == 0 else 2) + side
                            mm = pe.matmul(PS[:, bank, :], midT[b][:, 2 * half + c, :],
                                           w[:, c, 512 * side:512 * side + 512],
                                           start=(half == 0 and c == 0), stop=(half == 1 and c == 1))
                    mm.then_inc(k.freed[slab[0]], 1)

            turn_x(0)
            product(0, 0)
            product(0, 1)
            turn_x(1)
            pe.wait_ge(s.y_kept, 2 * i + 1)
            product(1, 0)
            turn_mid(0)
            product(1, 1)
            down(0)
            turn_mid(1)
            down(1)

    def experts_scalar(act):
        act.sem_inc(s.x_out, 1)
        act.sem_inc(s.mid_out, 1)
        n = pairs(act)
        with act.Fori(0, n) as i:
            def leave_x(b):
                for half in range(2):
                    act.wait_ge(s.x_turned, 4 * i + 2 * b + half + 1)
                    act.copy(xT[b][:, 4 * half:4 * half + 4, :],
                             PS[:, 6 + half, :].rearrange("p (c n) -> p c n", c=4)).then_inc(s.x_out, 1)

            def gate(b):
                done(act, 6 * b + 1, i)
                act.wait_ge(s.mid, 2 * i + b + 1)
                act.activation(silu, PS[:, 2 * b, :], ACT.Silu).then_inc(s.silued, 1)

            def leave_mid(b):
                act.wait_ge(s.mid_turned, 2 * i + b + 1)
                act.copy(midT[b], PS[:, 6 + b, :].rearrange("p (c n) -> p c n", c=4)).then_inc(s.mid_out, 1)

            leave_x(0)
            gate(0)
            leave_x(1)
            gate(1)
            leave_mid(0)
            leave_mid(1)

    def experts_vector(dve):
        dve.sem_inc(s.mid, 1)
        dve.sem_inc(s.y_kept, 1)
        n = pairs(dve)
        with dve.Fori(0, n) as i:
            def multiply(b):
                dve.wait_ge(s.silued, 2 * i + b + 1)
                done(dve, 6 * b + 3, i)
                dve.tensor_tensor(mid[b], PS[:, 2 * b + 1, :], silu, ALU.mult).then_inc(s.mid, 1)

            def keep(b):
                done(dve, 6 * b + 5, i)
                dve.wait_ge(s.y_free, i + 1)
                for side in range(2):
                    mm = dve.tensor_copy(ys[b][:, 512 * side:512 * side + 512],
                                         PS[:, (4 if b == 0 else 2) + side, :])
                mm.then_inc(s.y_kept, 1)

            multiply(0)
            multiply(1)
            keep(0)
            keep(1)

    y1 = [W[:, 2048 * t:2048 * t + 1024] for t in range(NT)]
    y2 = [W[:, 2048 * t + 1024:2048 * t + 2048] for t in range(NT)]

    def end_gpsimd(pool):
        for t in range(NT):
            for j, y in ((0, y1), (1, y2)):
                pool.indirect_dma_start(y[t], None, y_rows, bass.IndirectOffsetOnAxis(
                    ap=dest_i[:, 4 * j + t:4 * j + t + 1].bitcast(U32), axis=0)).then_inc(found[t], 16)

    def end_vector(dve):
        dve.wait_ge(s.gain_in, 16)
        for t in range(NT):
            dve.wait_ge(found[t], 32)
            dve.scalar_tensor_tensor(X[:, t, :], y1[t], g1[:, t:t + 1], X[:, t, :], ALU.mult, ALU.add)
            dve.drain()
            dve.scalar_tensor_tensor(X[:, t, :], y2[t], g2[:, t:t + 1], X[:, t, :], ALU.mult, ALU.add)\
               .then_inc(s.combined, 1)
            if t > 0:
                last_norm(dve, t - 1)
        last_norm(dve, NT - 1)

    def last_norm(dve, t):
        dve.wait_ge(s.rooted, t + 1)
        dve.reciprocal(st[:, t, 15:16], st[:, t, 14:15])
        dve.drain()
        dve.scalar_tensor_tensor(y1[t], X[:, t, :], st[:, t, 15:16], k.rows[:, 1, :],
                                 ALU.mult, ALU.mult).then_inc(s.final, 1)

    def end_scalar(act):
        for t in range(NT):
            act.wait_ge(s.combined, t + 1)
            act.activation(y2[t], X[:, t, :], ACT.Square, accum_out=st[:, t, 13:14])
            act.drain()
            act.activation(st[:, t, 14:15], st[:, t, 13:14], ACT.Sqrt, bias=k.eps_rms, scale=1.0 / D)\
               .then_inc(s.rooted, 1)

    def end_sync(sp):
        for t in range(NT):
            sp.wait_ge(s.final, t + 1)
            sp.dma_start(k.out[0, t * P:(t + 1) * P, :], y1[t]).then_inc(out_saved[t], 16)
        for t in range(NT):
            sp.wait_ge(out_saved[t], 16)

    yield dict(sync=route_sync, gpsimd=route_gpsimd, tensor=route_tensor, scalar=route_scalar, vector=route_vector)
    yield dict(sync=experts_sync, gpsimd=experts_gpsimd, tensor=experts_tensor, scalar=experts_scalar,
               vector=experts_vector)
    yield dict(sync=end_sync, gpsimd=end_gpsimd, scalar=end_scalar, vector=end_vector)


def taps_stage(k):
    A, W, PS = k.A, k.W, k.PS
    n = 2 * FT
    rows = k.rows[0:n, 0, :].rearrange("p (l t n) -> p l t n", l=2, t=4)
    rows_in, turned = k.sem("tap_rows"), k.sem("taps_turned")
    k.taps_in = k.sem("taps_in")

    def gpsimd(pool):
        for layer in range(2):
            for tap in range(4):
                src = A["conv_b"][layer] if tap == 3 else A["conv_w"][layer, tap]
                pool.dma_start(rows[:, layer, tap, :], src.rearrange("(n p) -> n p", p=P))\
                    .then_inc(rows_in, 16)
        pool.wait_ge(rows_in, 128)

    def tensor(pe):
        pe.wait_ge(rows_in, 128)
        pe.wait_ge(k.ret_kept, 16)
        pe.wait_ge(k.ret_rotated, 16)
        for layer in range(2):
            for tap in range(4):
                at = (4 * layer + tap) * n
                mm = pe.transpose(PS[:, 7, at:at + n], rows[:, layer, tap, :], k.ident[0:n, 0:n])
        mm.then_inc(turned, 1)

    def scalar(act):
        act.wait_ge(turned, 1)
        act.copy(k.taps[:].rearrange("p l t n -> p (l t n)"), PS[:, 7, 0:8 * n]).then_inc(k.taps_in, 1)

    return dict(gpsimd=gpsimd, tensor=tensor, scalar=scalar)


def program(nc, A, out, stop=99):
    plan = Plan()
    k = Namespace()
    k.nc, k.A, k.out = nc, A, out
    k.ret_slabs = [plan.take(2, 4) for _ in range(4)]
    k.sb_slabs = [plan.take(2, 3) for _ in range(4)]
    plan.at = 6
    k.even_out_slabs = plan.take(4)
    k.ffn0_slabs = plan.turns(UD, 2, 3)
    plan.at = 0
    k.odd_slabs = [plan.take(2, 3) for _ in range(8)]
    plan.at = 6
    k.odd_out_slabs = plan.take(4)
    k.ffn1_slabs = plan.turns(UD, 2, 3)
    plan.at = 0
    k.cv_slabs = plan.take_raw(4, 2)
    k.ml_slabs = [plan.take_raw(2, 2) for _ in range(4)]
    k.out2_slabs = plan.take_raw(4)
    k.moe_slabs = [plan.place(s, 1, 0) for s in range(RING)]
    with ExitStack() as ctx:
        def sb(name, shape, dt=F32):
            return ctx.enter_context(nc.sbuf_tensor(name, shape, dt))

        k.sem = lambda name: ctx.enter_context(nc.semaphore(name))
        k.X = sb("X", [P, NT, D])
        k.rows = sb("rows", [P, 3, D])
        k.small = sb("small", [P, 4 * P])
        k.taps = sb("taps", [P, 2, 4, 2 * FT])
        k.stat = sb("stat", [P, NT, 16])
        k.PS = ctx.enter_context(nc.psum_tensor("PS", [P, 8, 512], F32))
        k.eps_col = sb("eps_col", [P, 2])
        k.eps_ln, k.eps_rms = k.eps_col[:, 0:1], k.eps_col[:, 1:2]
        k.ident, k.negtri, k.negone, k.before = (
            k.small[:, i * P:(i + 1) * P] for i in range(4))
        k.chan = sb("chan", [P, 184])
        k.lam = sb("lam", [P, 8])
        k.cols = sb("cols", [P, 2, 9])
        with nc.sbuf_tensor("ring", [P, RING, SLOT], F32) as ring, \
                nc.sbuf_tensor("XT", [P, KC, S], F32) as XT, \
                nc.sbuf_tensor("W", [P, 16128], F32) as Wt:
            k.ring = ring
            k.XT = XT
            k.W = Wt
        with nc.sbuf_tensor("raw_slots", [P, RAW, SLOT], F32), \
                nc.sbuf_tensor("split", [P, SPLIT, 2, SLOT], F32R) as split, \
                nc.sbuf_tensor("XS", [P, 2, KC * S], F32R) as XS, \
                nc.sbuf_tensor("W_head", [P, 14080], F32), \
                nc.sbuf_tensor("H0", [P, 2, 1024], F32R) as H0:
            k.split, k.XS, k.H0 = split, XS, H0
        k.lam_vec = k.rows[:, 2, 648:904]
        k.bias_line = k.rows[0:8, 1, 384:1024]
        k.landed = [k.sem(f"slab_landed{s}") for s in range(RING)]
        k.freed = [k.sem(f"slab_freed{s}") for s in range(RING)]
        k.rows_used = None
        k.dram = lambda name, shape, dt=F32: nc.dram_tensor(name, shape, dt).ap()

        def start_vector(dve):
            dve.memset(k.eps_col[:, 0:1], LN_EPS).then_inc(k.s_eps, 1)
            dve.memset(k.eps_col[:, 1:2], EPS).then_inc(k.s_eps, 1)

        def start_scalar(act):
            act.wait_ge(k.s_eps, 2)

        def even_block():
            k.s_eps = k.sem("eps_set")
            yield dict(vector=start_vector, scalar=start_scalar)
            yield entry(k)
            yield retention_stage(k)
            yield taps_stage(k)
            yield column_stage(k)
            bias = bias_stage(k)
            yield bias
            clear = clear_stage(k)
            yield dict(vector=clear["vector"])
            yield stick_stage(k)
            yield dict(sync=bias["late_sync"])
            yield mix_out_stage(k, "even", A["w_out_even"][0], k.even_out_slabs,
                                [(k.ret_y_out, 4), (k.sb_y_out, 8)], [A["ln1_g"][0], A["ln1_b"][0]], "ln")
            yield ffn_stage(k, 0, k.ffn0_slabs, [A["ln2_g"][0], A["ln2_b"][0]], "ln")
            yield dict(gpsimd=clear["gpsimd"])
            yield odd_ahead(k)

        def odd_block():
            yield diff_stage(k)
            yield mix_out_stage(k, "odd", A["w_out_odd"][0], k.odd_out_slabs, [(k.df_y_out, 8)],
                                [A["ln1_g"][1], A["ln1_b"][1]], "ln")
            if stop != "1":
                yield ffn_stage(k, 1, k.ffn1_slabs,
                                [A["ln2_g"][1], A["ln2_b"][1], A["norm_mix_g_2"][0]], "ln+rms")
                yield hybrid_ahead(k)

        def second_block():
            if stop == "1":
                return
            yield hybrid_stage(k)
            yield mix_out_stage(k, "out2", A["w_out_2"][0], k.out2_slabs, [(k.hy_y_out, 4)],
                                [A["norm_ffn_g_2"][0]], "rms", k.beside)
            if stop != "2":
                yield from moe_stages(k)

        for phase in (even_block, odd_block, second_block):
            held = []
            k.xt_ready = k.x_ready = k.rows_used = None

            def phase_sem(name):
                held.append(nc.alloc_semaphore(name=name))
                return held[-1]

            k.sem = phase_sem
            stages = list(phase())
            with nc.Block() as block:
                @block.sync
                def _(sp):
                    for stage in stages:
                        if "sync" in stage:
                            stage["sync"](sp)

                @block.gpsimd
                def _(pool):
                    for stage in stages:
                        if "gpsimd" in stage:
                            stage["gpsimd"](pool)

                @block.scalar
                def _(act):
                    for stage in stages:
                        if "scalar" in stage:
                            stage["scalar"](act)

                @block.tensor
                def _(pe):
                    for stage in stages:
                        if "tensor" in stage:
                            stage["tensor"](pe)

                @block.vector
                def _(dve):
                    for stage in stages:
                        if "vector" in stage:
                            stage["vector"](dve)
            nc.clear_and_free_semaphores(held)
            nc.all_engine_barrier()



def kernel(**inputs):
    import concourse.bacc as bacc
    from concourse.bass_utils import run_bass_kernel_spmd

    nc = bacc.Bacc("TRN2", target_bir_lowering=False, num_devices=1)
    arrays, aps = {}, {}
    for name, a in {**{n: np.ascontiguousarray(v) for n, v in inputs.items()}, **shape_constants()}.items():
        arrays[f"in_{name}"] = a
        aps[name] = nc.dram_tensor(f"in_{name}", a.shape, mybir.dt.from_np(a.dtype), kind="ExternalInput").ap()
    out = nc.dram_tensor("out", (1, S, D), F32, kind="ExternalOutput").ap()
    program(nc, aps, out)
    return run_bass_kernel_spmd(nc, [arrays], core_ids=[0]).results[0]["out"]
```
